# Optimizing a Trainium2 kernel written in Bass

```python
import math
import jax, jax.numpy as jnp
from jax import lax
import numpy as np

D_MODEL = 1024
BATCH = 1
SEQ = 512
DEPTH = 2

D_MIX = D_MODEL
D_CONV = D_MIX // 4
D_LRU = D_MIX // 4
D_ATTN = D_MIX // 2
CONV_KERNEL = 31
LRU_HEADS = 4
LRU_HEAD_DIM = D_LRU // LRU_HEADS
LRU_CONV = 4
LRU_C = 8.0
HEAD_DIM = 64
N_Q_HEADS = D_ATTN // HEAD_DIM
N_KV_HEADS = 2
GQA_REP = N_Q_HEADS // N_KV_HEADS
KV_DIM = N_KV_HEADS * HEAD_DIM
WINDOW = 128
BLOCK = 128
REL_BUCKETS = 32
REL_MAX_DIST = 128
D_FF = 2816
ALPHA = (2.0 * DEPTH) ** 0.25
BETA = (8.0 * DEPTH) ** -0.25
LN_EPS = 1e-5
D_IN = 2 * D_CONV + 2 * D_LRU + D_ATTN + 2 * KV_DIM


def _layernorm(x, g, b):
    xf = x.astype(jnp.float32)
    mu = jnp.mean(xf, axis=-1, keepdims=True)
    var = jnp.mean(jnp.square(xf - mu), axis=-1, keepdims=True)
    return ((xf - mu) * lax.rsqrt(var + LN_EPS)).astype(x.dtype) * g + b

def _swiglu(x, wg, wu, wd):
    return (jax.nn.silu(x @ wg) * (x @ wu)) @ wd

def _causal_dw_conv(x, w):
    k = w.shape[0]
    return lax.conv_general_dilated(
        x, w[:, None, :].astype(x.dtype), window_strides=(1,), padding=[(k - 1, 0)],
        dimension_numbers=('NWC', 'WIO', 'NWC'), feature_group_count=x.shape[-1])

def _conv_module(u, dw_w, dw_b, g, b):
    a, gate = jnp.split(u, 2, axis=-1)
    y = a * jax.nn.sigmoid(gate)
    y = _causal_dw_conv(y, dw_w) + dw_b
    y = _layernorm(y, g, b)
    return jax.nn.silu(y)

def _lin_combine(left, right):
    a1, b1 = left
    a2, b2 = right
    return a1 * a2, a2 * b1 + b2

def _recurrent(u, conv_w, conv_b, wa, ba, wx, bx, lam):
    B, S, _ = u.shape
    xb, gb = jnp.split(u, 2, axis=-1)
    xb = _causal_dw_conv(xb, conv_w) + conv_b
    xh = xb.reshape(B, S, LRU_HEADS, LRU_HEAD_DIM)
    r = jax.nn.sigmoid(jnp.einsum('bshi,hij->bshj', xh, wa).reshape(B, S, D_LRU) + ba)
    i = jax.nn.sigmoid(jnp.einsum('bshi,hij->bshj', xh, wx).reshape(B, S, D_LRU) + bx)
    log_a = LRU_C * r.astype(jnp.float32) * jax.nn.log_sigmoid(lam.astype(jnp.float32))
    a = jnp.exp(log_a)
    mult = jnp.sqrt(-jnp.expm1(2.0 * log_a))
    bterm = mult * (i * xb).astype(jnp.float32)
    _, h = lax.associative_scan(_lin_combine, (a, bterm), axis=1)
    return h.astype(u.dtype) * jax.nn.gelu(gb)

def _rel_bucket(dist):
    max_exact = REL_BUCKETS // 2
    is_small = dist < max_exact
    large = max_exact + (jnp.log(jnp.maximum(dist, 1).astype(jnp.float32) / max_exact)
                         / math.log(REL_MAX_DIST / max_exact)
                         * (REL_BUCKETS - max_exact)).astype(jnp.int32)
    large = jnp.minimum(large, REL_BUCKETS - 1)
    return jnp.where(is_small, dist, large)

def _band_bias_and_mask(rel_bias, seq):
    nb = seq // BLOCK
    qi = jnp.arange(BLOCK)[:, None]
    kj = jnp.arange(2 * BLOCK)[None, :]
    dist = qi - kj + BLOCK
    bucket = _rel_bucket(jnp.maximum(dist, 0))
    bias = rel_bias[bucket].astype(jnp.float32)
    bias = jnp.transpose(bias, (2, 0, 1)).reshape(N_KV_HEADS, GQA_REP, BLOCK, 2 * BLOCK)
    blk = jnp.arange(nb)[:, None, None]
    valid = (dist >= 0) & (dist < WINDOW) & (blk * BLOCK + kj - BLOCK >= 0)
    return bias, valid

def _band(t, nb):
    B = t.shape[0]
    tp = jnp.pad(t, ((0, 0), (BLOCK, 0), (0, 0), (0, 0)))
    tp = tp.reshape(B, nb + 1, BLOCK, t.shape[2], t.shape[3])
    return jnp.concatenate([tp[:, :-1], tp[:, 1:]], axis=2)

def _swa(q, k, v, band_bias, valid, sinks):
    B, S, _ = q.shape
    nb = S // BLOCK
    qb = q.reshape(B, nb, BLOCK, N_KV_HEADS, GQA_REP, HEAD_DIM)
    kb = _band(k.reshape(B, S, N_KV_HEADS, HEAD_DIM), nb)
    vb = _band(v.reshape(B, S, N_KV_HEADS, HEAD_DIM), nb)
    s = jnp.einsum('bnqgrd,bnkgd->bngrqk', qb, kb).astype(jnp.float32) * (HEAD_DIM ** -0.5)
    s = s + band_bias[None, None]
    s = jnp.where(valid[None, :, None, None], s, -1e30)
    sink = jnp.broadcast_to(sinks.astype(jnp.float32).reshape(1, 1, N_KV_HEADS, GQA_REP, 1, 1),
                            s.shape[:-1] + (1,))
    p = jax.nn.softmax(jnp.concatenate([s, sink], axis=-1), axis=-1)[..., :-1]
    o = jnp.einsum('bngrqk,bnkgd->bnqgrd', p.astype(vb.dtype), vb)
    return o.reshape(B, S, D_ATTN)

def _mixer(x, w_in, conv_dw_w, conv_dw_b, conv_ln_g, conv_ln_b, lru_conv_w, lru_conv_b,
           lru_wa, lru_ba, lru_wx, lru_bx, lru_lambda, sinks, w_out, band_bias, valid):
    u = x @ w_in
    o1 = 2 * D_CONV
    o2 = o1 + 2 * D_LRU
    o3 = o2 + D_ATTN
    o4 = o3 + KV_DIM
    u_conv, u_lru, q, k, v = jnp.split(u, [o1, o2, o3, o4], axis=-1)
    y_conv = _conv_module(u_conv, conv_dw_w, conv_dw_b, conv_ln_g, conv_ln_b)
    y_lru = _recurrent(u_lru, lru_conv_w, lru_conv_b, lru_wa, lru_ba, lru_wx, lru_bx, lru_lambda)
    y_attn = _swa(q, k, v, band_bias, valid, sinks)
    return jnp.concatenate([y_conv, y_lru, y_attn], axis=-1) @ w_out

def first_inputs(seed: int = 0) -> dict:
    key = jax.random.key(seed)
    ks = jax.random.split(key, 24)
    f32 = jnp.float32
    nrm = lambda k, shape, scale: jax.random.normal(k, shape, f32) * scale
    x = nrm(ks[0], (BATCH, SEQ, D_MODEL), 1.0)
    rel_bias = nrm(ks[1], (REL_BUCKETS, N_Q_HEADS), 0.5)
    ln_g = 1.0 + nrm(ks[2], (DEPTH, 3, D_MODEL), 0.1)
    ln_b = nrm(ks[3], (DEPTH, 3, D_MODEL), 0.02)
    ffn_w_gate = nrm(ks[4], (DEPTH, 2, D_MODEL, D_FF), D_MODEL ** -0.5)
    ffn_w_up = nrm(ks[5], (DEPTH, 2, D_MODEL, D_FF), D_MODEL ** -0.5)
    ffn_w_down = nrm(ks[6], (DEPTH, 2, D_FF, D_MODEL), BETA * D_FF ** -0.5)
    w_in = nrm(ks[7], (DEPTH, D_MODEL, D_IN), D_MODEL ** -0.5)
    conv_dw_w = nrm(ks[8], (DEPTH, CONV_KERNEL, D_CONV), CONV_KERNEL ** -0.5)
    conv_dw_b = nrm(ks[9], (DEPTH, D_CONV), 0.02)
    conv_ln_g = 1.0 + nrm(ks[10], (DEPTH, D_CONV), 0.1)
    conv_ln_b = nrm(ks[11], (DEPTH, D_CONV), 0.02)
    lru_conv_w = nrm(ks[12], (DEPTH, LRU_CONV, D_LRU), LRU_CONV ** -0.5)
    lru_conv_b = nrm(ks[13], (DEPTH, D_LRU), 0.02)
    lru_wa = nrm(ks[14], (DEPTH, LRU_HEADS, LRU_HEAD_DIM, LRU_HEAD_DIM), LRU_HEAD_DIM ** -0.5)
    lru_ba = nrm(ks[15], (DEPTH, D_LRU), 0.02)
    lru_wx = nrm(ks[16], (DEPTH, LRU_HEADS, LRU_HEAD_DIM, LRU_HEAD_DIM), LRU_HEAD_DIM ** -0.5)
    lru_bx = nrm(ks[17], (DEPTH, D_LRU), 0.02)
    a_init = jax.random.uniform(ks[18], (DEPTH, D_LRU), f32, 0.9, 0.999)
    sig = a_init ** (1.0 / LRU_C)
    lru_lambda = jnp.log(sig) - jnp.log1p(-sig)
    attn_sinks = nrm(ks[19], (DEPTH, N_Q_HEADS), 0.5)
    w_out = nrm(ks[20], (DEPTH, D_MIX, D_MODEL), BETA * D_MIX ** -0.5)
    return {'x': x, 'rel_bias': rel_bias, 'ln_g': ln_g, 'ln_b': ln_b,
            'ffn_w_gate': ffn_w_gate, 'ffn_w_up': ffn_w_up, 'ffn_w_down': ffn_w_down,
            'w_in': w_in, 'conv_dw_w': conv_dw_w, 'conv_dw_b': conv_dw_b,
            'conv_ln_g': conv_ln_g, 'conv_ln_b': conv_ln_b,
            'lru_conv_w': lru_conv_w, 'lru_conv_b': lru_conv_b,
            'lru_wa': lru_wa, 'lru_ba': lru_ba, 'lru_wx': lru_wx, 'lru_bx': lru_bx,
            'lru_lambda': lru_lambda, 'attn_sinks': attn_sinks, 'w_out': w_out}

def first_block(x, rel_bias, ln_g, ln_b, ffn_w_gate, ffn_w_up, ffn_w_down, w_in,
              conv_dw_w, conv_dw_b, conv_ln_g, conv_ln_b, lru_conv_w, lru_conv_b,
              lru_wa, lru_ba, lru_wx, lru_bx, lru_lambda, attn_sinks, w_out):
    band_bias, valid = _band_bias_and_mask(rel_bias, x.shape[1])
    for l in range(DEPTH):
        h = 0.5 * _swiglu(x, ffn_w_gate[l, 0], ffn_w_up[l, 0], ffn_w_down[l, 0])
        x = _layernorm(ALPHA * x + h, ln_g[l, 0], ln_b[l, 0])
        h = _mixer(x, w_in[l], conv_dw_w[l], conv_dw_b[l], conv_ln_g[l], conv_ln_b[l],
                   lru_conv_w[l], lru_conv_b[l], lru_wa[l], lru_ba[l], lru_wx[l], lru_bx[l],
                   lru_lambda[l], attn_sinks[l], w_out[l], band_bias, valid)
        x = _layernorm(ALPHA * x + h, ln_g[l, 1], ln_b[l, 1])
        h = 0.5 * _swiglu(x, ffn_w_gate[l, 1], ffn_w_up[l, 1], ffn_w_down[l, 1])
        x = _layernorm(ALPHA * x + h, ln_g[l, 2], ln_b[l, 2])
    return x


DEPTH_2 = 1

CTX_LEN = 256
GRID_W = 64
CHUNK = 128
ROWS_PER_CHUNK = CHUNK // GRID_W
EPS = 1e-6

SSD_HEAD_DIM = 64
SSD_HEADS = D_MODEL // SSD_HEAD_DIM
SSD_WIDTH = SSD_HEADS * SSD_HEAD_DIM
SSD_GROUPS = 4
SSD_STATE = 128
SSD_CONV = 3
DT_MIN = 0.001
DT_MAX = 0.1
GN = SSD_GROUPS * SSD_STATE
N_XBC = SSD_WIDTH + 2 * GN
N_SCAN = N_XBC + 2 * SSD_HEADS

MLP_WIDTH = D_MODEL
MLP_GROUP_DIM = 128
MLP_GROUPS = MLP_WIDTH // MLP_GROUP_DIM

N_IN = N_SCAN + SSD_WIDTH + 2 * MLP_WIDTH + 2 * D_MODEL

N_EXPERTS = 16
EXPERT_FF = D_MODEL
CAPACITY_FACTOR = 2


def split_cols(p, sizes):
    idx = np.cumsum(sizes)[:-1].tolist()
    return jnp.split(p, idx, axis=-1)

def rmsnorm(x, w):
    xf = x.astype(jnp.float32)
    y = xf * lax.rsqrt(jnp.mean(xf * xf, axis=-1, keepdims=True) + EPS)
    return (y * w.astype(jnp.float32)).astype(x.dtype)

def layernorm(x, w, b):
    xf = x.astype(jnp.float32)
    mu = jnp.mean(xf, axis=-1, keepdims=True)
    var = jnp.mean(jnp.square(xf - mu), axis=-1, keepdims=True)
    y = (xf - mu) * lax.rsqrt(var + EPS)
    return (y * w.astype(jnp.float32) + b.astype(jnp.float32)).astype(x.dtype)

def dwconv_centred(x, w, b):
    ch = x.shape[-1]
    k = w.shape[0]
    y = lax.conv_general_dilated(x, w[:, None, :].astype(x.dtype), window_strides=(1,),
                                 padding=[(k // 2, k // 2)],
                                 dimension_numbers=('NWC', 'WIO', 'NWC'),
                                 feature_group_count=ch)
    return y + b.astype(x.dtype)

def ssd_chunked(xh, dt, A, bm, cm, h0):
    b, l, H, P = xh.shape
    G, N = bm.shape[2], bm.shape[3]
    R = H // G
    nc = l // CHUNK
    x = xh.reshape(b, nc, CHUNK, G, R, P)
    dt_c = dt.reshape(b, nc, CHUNK, G, R)
    a_cum = jnp.cumsum(dt_c * A.reshape(G, R), axis=2)
    Bc = bm.reshape(b, nc, CHUNK, G, N)
    Cc = cm.reshape(b, nc, CHUNK, G, N)
    xdt = x * dt_c[..., None].astype(x.dtype)
    lower = jnp.tril(jnp.ones((CHUNK, CHUNK), dtype=bool))[None, None, :, :, None, None]
    seg = a_cum[:, :, :, None] - a_cum[:, :, None, :]
    decay = jnp.exp(jnp.where(lower, seg, -jnp.inf))
    cb = jnp.einsum('bcign,bcjgn->bcijg', Cc, Bc)
    y_diag = jnp.einsum('bcijg,bcijgr,bcjgrp->bcigrp', cb, decay, xdt)
    decay_to_end = jnp.exp(a_cum[:, :, -1:] - a_cum)
    states = jnp.einsum('bcjgn,bcjgr,bcjgrp->bcgrpn', Bc, decay_to_end, xdt)
    chunk_decay = jnp.exp(a_cum[:, :, -1])

    def step(h, inp):
        st, dcy = inp
        return h * dcy[..., None, None] + st, h

    h_final, h_in = lax.scan(step, h0, (jnp.moveaxis(states, 1, 0).astype(jnp.float32),
                                        jnp.moveaxis(chunk_decay, 1, 0)))
    y_off = jnp.einsum('bcign,bcigr,cbgrpn->bcigrp', Cc, jnp.exp(a_cum), h_in)
    y = (y_diag + y_off).reshape(b, l, H, P).astype(xh.dtype)
    return y, h_final

def ssd_scan_bidir(p_scan, conv_w, conv_b, dt_bias, a_log, h0_f, h0_b):
    xbc, dt_raw = p_scan[..., :N_XBC], p_scan[..., N_XBC:]
    xbc = jax.nn.silu(dwconv_centred(xbc, conv_w, conv_b))
    xs, bm, cm = split_cols(xbc, [SSD_WIDTH, GN, GN])
    b, l, _ = xs.shape
    xh = xs.reshape(b, l, SSD_HEADS, SSD_HEAD_DIM)
    bm = bm.reshape(b, l, SSD_GROUPS, SSD_STATE)
    cm = cm.reshape(b, l, SSD_GROUPS, SSD_STATE)
    dt = jax.nn.softplus(dt_raw.astype(jnp.float32).reshape(b, l, 2, SSD_HEADS)
                         + dt_bias.astype(jnp.float32))
    A = -jnp.exp(a_log.astype(jnp.float32))
    y_f, st_f = ssd_chunked(xh, dt[:, :, 0], A[0], bm, cm, h0_f)
    rev = lambda t: jnp.flip(t, axis=1)
    y_b, st_b = ssd_chunked(rev(xh), rev(dt[:, :, 1]), A[1], rev(bm), rev(cm), h0_b)
    return y_f + rev(y_b), xh, st_f, st_b

def ssd_output(y, xh, z, d_skip, norm_w):
    b, l, H, P = xh.shape
    y = y + d_skip.astype(xh.dtype)[:, None] * xh
    g = y.reshape(b, l, SSD_WIDTH) * jax.nn.silu(z)
    g = rmsnorm(g.reshape(b, l, SSD_GROUPS, SSD_WIDTH // SSD_GROUPS),
                norm_w.reshape(SSD_GROUPS, SSD_WIDTH // SSD_GROUPS))
    return g.reshape(b, l, SSD_WIDTH)

def spatial_gating(u, v, n_chunks, ln_w, ln_b, w_s, b_s):
    b, l, _ = v.shape
    v = layernorm(v, ln_w, ln_b)
    vc = v.reshape(b, n_chunks, CHUNK, MLP_GROUPS, MLP_GROUP_DIM)
    mixed = jnp.einsum('gij,bcjgd->bcigd', w_s, vc) + b_s.T[None, None, :, :, None]
    return u * mixed.reshape(b, l, MLP_WIDTH)

def mixer_out(y, xh, p_rest, n_chunks, d_skip, ssd_norm_w, ln_w, ln_b, w_s, b_s, w_pa, w_pb, w_o):
    z, uv, gate_a, gate_b = split_cols(p_rest, [SSD_WIDTH, 2 * MLP_WIDTH, D_MODEL, D_MODEL])
    ssd = ssd_output(y, xh, z, d_skip, ssd_norm_w)
    u, v = jnp.split(jax.nn.gelu(uv), 2, axis=-1)
    sgu = spatial_gating(u, v, n_chunks, ln_w, ln_b, w_s, b_s)
    merged = jax.nn.sigmoid(gate_a) * (ssd @ w_pa) + jax.nn.sigmoid(gate_b) * (sgu @ w_pb)
    return merged @ w_o

def expert_choice_ffn(xn, router_w, w_gate, w_up, w_down):
    b, n, d = xn.shape
    cap = CAPACITY_FACTOR * n // N_EXPERTS
    logits = jnp.einsum('bnd,de->ben', xn, router_w).astype(jnp.float32)
    aff = jax.nn.softmax(logits, axis=1)
    gate, idx = lax.top_k(aff, cap)
    xg = jax.vmap(lambda xs, ix: xs[ix])(xn, idx)
    hid = jax.nn.silu(jnp.einsum('becd,edf->becf', xg, w_gate)) * jnp.einsum('becd,edf->becf', xg, w_up)
    y = jnp.einsum('becf,efd->becd', hid, w_down) * gate[..., None].astype(xn.dtype)
    scatter = lambda ix, ys: jnp.zeros((n, d), ys.dtype).at[ix.reshape(-1)].add(ys.reshape(-1, d))
    return jax.vmap(scatter)(idx, y)

def second_inputs(seed: int = 0) -> dict:
    key = jax.random.key(seed)
    ks = jax.random.split(key, 32)
    f32 = jnp.float32
    L = DEPTH_2
    nrm = lambda k, shape, s: jax.random.normal(k, shape, f32) * s
    gain = lambda k, shape: 1.0 + 0.01 * jax.random.normal(k, shape, f32)
    dt0 = jnp.exp(jax.random.uniform(ks[12], (L, 2, SSD_HEADS), f32, math.log(DT_MIN), math.log(DT_MAX)))
    return {
        'x': nrm(ks[0], (BATCH, SEQ, D_MODEL), 1.0),
        'c': nrm(ks[1], (BATCH, D_MODEL), 1.0),
        'ctx': nrm(ks[2], (BATCH, CTX_LEN, D_MODEL), 1.0),
        'c_ctx': nrm(ks[3], (D_MODEL,), 1.0),
        'ada_w': nrm(ks[4], (L, D_MODEL, 6 * D_MODEL), 0.5 * D_MODEL ** -0.5),
        'ada_b': nrm(ks[5], (L, 6 * D_MODEL), 0.01),
        'norm1_w': gain(ks[6], (L, D_MODEL)),
        'norm2_w': gain(ks[7], (L, D_MODEL)),
        'w_in': nrm(ks[8], (L, D_MODEL, N_IN), D_MODEL ** -0.5),
        'conv_w': nrm(ks[9], (L, SSD_CONV, N_XBC), SSD_CONV ** -0.5),
        'conv_b': nrm(ks[10], (L, N_XBC), 0.01),
        'dt_bias': dt0 + jnp.log(-jnp.expm1(-dt0)),
        'a_log': jnp.log(jax.random.uniform(ks[13], (L, 2, SSD_HEADS), f32, 1.0, 16.0)),
        'd_skip': gain(ks[14], (L, SSD_HEADS)),
        'ssd_norm_w': gain(ks[15], (L, SSD_WIDTH)),
        'sgu_ln_w': gain(ks[16], (L, MLP_WIDTH)),
        'sgu_ln_b': nrm(ks[17], (L, MLP_WIDTH), 0.01),
        'w_s': nrm(ks[18], (L, MLP_GROUPS, CHUNK, CHUNK), CHUNK ** -0.5),
        'b_s': gain(ks[19], (L, MLP_GROUPS, CHUNK)),
        'w_pa': nrm(ks[20], (L, SSD_WIDTH, D_MODEL), SSD_WIDTH ** -0.5),
        'w_pb': nrm(ks[21], (L, MLP_WIDTH, D_MODEL), MLP_WIDTH ** -0.5),
        'w_o': nrm(ks[22], (L, D_MODEL, D_MODEL), D_MODEL ** -0.5),
        'router_w': nrm(ks[23], (L, D_MODEL, N_EXPERTS), D_MODEL ** -0.5),
        'w_gate': nrm(ks[24], (L, N_EXPERTS, D_MODEL, EXPERT_FF), D_MODEL ** -0.5),
        'w_up': nrm(ks[25], (L, N_EXPERTS, D_MODEL, EXPERT_FF), D_MODEL ** -0.5),
        'w_down': nrm(ks[26], (L, N_EXPERTS, EXPERT_FF, D_MODEL), EXPERT_FF ** -0.5),
        'final_norm_w': gain(ks[27], (D_MODEL,)),
    }

def second_block(x, c, ctx, c_ctx, ada_w, ada_b, norm1_w, norm2_w, w_in, conv_w, conv_b, dt_bias, a_log,
              d_skip, ssd_norm_w, sgu_ln_w, sgu_ln_b, w_s, b_s, w_pa, w_pb, w_o, router_w,
              w_gate, w_up, w_down, final_norm_w):
    bsz, n_lat, _ = x.shape
    rows = n_lat // GRID_W
    lat_chunks = rows // ROWS_PER_CHUNK
    ctx_chunks = ctx.shape[1] // CHUNK
    h0 = jnp.zeros((bsz, SSD_GROUPS, SSD_HEADS // SSD_GROUPS, SSD_HEAD_DIM, SSD_STATE), jnp.float32)
    h, hc = x, ctx
    for layer in range(DEPTH_2):
        last = layer == DEPTH_2 - 1
        mod_l = (jax.nn.silu(c) @ ada_w[layer] + ada_b[layer])[:, None, :]
        mod_c = (jax.nn.silu(c_ctx) @ ada_w[layer] + ada_b[layer])[None, None, :]
        sh1_l, sc1_l, g1_l, sh2_l, sc2_l, g2_l = jnp.split(mod_l, 6, axis=-1)
        sh1_c, sc1_c, g1_c, sh2_c, sc2_c, g2_c = jnp.split(mod_c, 6, axis=-1)
        w_in_l = w_in[layer]
        mix_args = (d_skip[layer], ssd_norm_w[layer], sgu_ln_w[layer], sgu_ln_b[layer],
                    w_s[layer], b_s[layer], w_pa[layer], w_pb[layer], w_o[layer])
        xm_c = rmsnorm(hc, norm1_w[layer]) * (1 + sc1_c) + sh1_c
        xm_l = rmsnorm(h, norm1_w[layer]) * (1 + sc1_l) + sh1_l
        y_c, xh_c, st_f, st_b = ssd_scan_bidir(xm_c @ w_in_l[:, :N_SCAN], conv_w[layer], conv_b[layer],
                                               dt_bias[layer], a_log[layer], h0, h0)
        p_l = xm_l @ w_in_l
        y_l, xh_l, _, _ = ssd_scan_bidir(p_l[..., :N_SCAN], conv_w[layer], conv_b[layer],
                                         dt_bias[layer], a_log[layer], st_f, st_b)
        h = h + g1_l * mixer_out(y_l, xh_l, p_l[..., N_SCAN:], lat_chunks, *mix_args)
        if not last:
            hc = hc + g1_c * mixer_out(y_c, xh_c, xm_c @ w_in_l[:, N_SCAN:], ctx_chunks, *mix_args)
        moe_args = (router_w[layer], w_gate[layer], w_up[layer], w_down[layer])
        xf_l = rmsnorm(h, norm2_w[layer]) * (1 + sc2_l) + sh2_l
        h = h + g2_l * expert_choice_ffn(xf_l, *moe_args)
        if not last:
            xf_c = rmsnorm(hc, norm2_w[layer]) * (1 + sc2_c) + sh2_c
            hc = hc + g2_c * expert_choice_ffn(xf_c, *moe_args)
    return rmsnorm(h, final_norm_w)


_first_inputs = second_inputs


def second_inputs(seed=0):
    import zlib

    import numpy as np

    out = dict(_first_inputs(seed))
    spreads = {}
    factors = {'ctx': 6.61,
     'c_ctx': 6.049,
     'ada_b': 5.101,
     'norm1_w': 8.0,
     'norm2_w': 8.0,
     'conv_b': 8.0,
     'd_skip': 8.0,
     'ssd_norm_w': 8.0,
     'sgu_ln_w': 8.0,
     'sgu_ln_b': 8.0,
     'b_s': 8.0,
     'final_norm_w': 6.227}
    for name, (base, spread) in spreads.items():
        noise = np.random.default_rng([zlib.crc32(name.encode()), seed]).standard_normal(out[name].shape)
        drawn = base * np.exp(spread * noise) if base else spread * noise
        out[name] = __import__('jax').numpy.asarray(drawn.astype(out[name].dtype))
    for name, factor in factors.items():
        out[name] = (out[name] * factor).astype(out[name].dtype)
    return out


_narrow_inputs = second_inputs


def second_inputs(seed=0):

    out = dict(_narrow_inputs(seed))
    wider = {'conv_b': 12.0,
     'd_skip': 12.0,
     'ssd_norm_w': 12.0,
     'sgu_ln_w': 3.15,
     'b_s': 3.06,
     'final_norm_w': 7.1}
    for name, times in wider.items():
        mean = out[name].mean()
        out[name] = (mean + times * (out[name] - mean)).astype(out[name].dtype)
    return out


def setup_inputs(seed=0):
    out = dict(first_inputs(seed))
    for name, value in second_inputs(seed + 1).items():
        if name != "x":
            out[name + "_2"] = value
    return out


def reference(
    x, rel_bias, ln_g, ln_b, ffn_w_gate, ffn_w_up, ffn_w_down, w_in, conv_dw_w, conv_dw_b,
    conv_ln_g, conv_ln_b, lru_conv_w, lru_conv_b, lru_wa, lru_ba, lru_wx, lru_bx, lru_lambda,
    attn_sinks, w_out, c_2, ctx_2, c_ctx_2, ada_w_2, ada_b_2, norm1_w_2, norm2_w_2, w_in_2,
    conv_w_2, conv_b_2, dt_bias_2, a_log_2, d_skip_2, ssd_norm_w_2, sgu_ln_w_2, sgu_ln_b_2,
    w_s_2, b_s_2, w_pa_2, w_pb_2, w_o_2, router_w_2, w_gate_2, w_up_2, w_down_2, final_norm_w_2,
):
    x = first_block(
        x, rel_bias, ln_g, ln_b, ffn_w_gate, ffn_w_up, ffn_w_down, w_in, conv_dw_w, conv_dw_b,
        conv_ln_g, conv_ln_b, lru_conv_w, lru_conv_b, lru_wa, lru_ba, lru_wx, lru_bx,
        lru_lambda, attn_sinks, w_out,
    )
    return second_block(
        x, c_2, ctx_2, c_ctx_2, ada_w_2, ada_b_2, norm1_w_2, norm2_w_2, w_in_2, conv_w_2,
        conv_b_2, dt_bias_2, a_log_2, d_skip_2, ssd_norm_w_2, sgu_ln_w_2, sgu_ln_b_2, w_s_2,
        b_s_2, w_pa_2, w_pb_2, w_o_2, router_w_2, w_gate_2, w_up_2, w_down_2, final_norm_w_2,
    )


_drawn_inputs = setup_inputs


def setup_inputs(seed=0):
    import zlib

    import numpy as np

    out = dict(_drawn_inputs(seed))
    spreads = {}
    factors = {'lru_bx': 8.0, 'attn_sinks': 6.59, 'c_ctx_2': 2.76, 'd_skip_2': 8.0}
    for name, (base, spread) in spreads.items():
        noise = np.random.default_rng([zlib.crc32(name.encode()), seed]).standard_normal(out[name].shape)
        drawn = base * np.exp(spread * noise) if base else spread * noise
        out[name] = __import__('jax').numpy.asarray(drawn.astype(out[name].dtype))
    for name, factor in factors.items():
        out[name] = (out[name] * factor).astype(out[name].dtype)
    return out
```

```python
import concourse.bass as bass
from concourse import mybir
from contextlib import ExitStack
import numpy as np


def first_block_program(nc, d, mem):
    f32 = mybir.dt.float32
    ALU, ACT, AX = mybir.AluOpType, mybir.ActivationFunctionType, mybir.AxisListType
    ALPHA = (2.0 * 2) ** 0.25
    L, KT, FT, T = 2, 8, 22, 512
    HEADS, WIN = 8, 128

    ctx = ExitStack()
    with ctx:
        arena, psum, scratch = mem["arena"], mem["psum"], mem["scratch"]
        cursor = [0]

        def place(*shape):
            size = int(np.prod(shape))
            v = arena[:, cursor[0]:cursor[0] + size]
            cursor[0] += size
            assert cursor[0] <= mem["size"], cursor[0]
            if len(shape) == 2:
                return v.rearrange("p (a b) -> p a b", b=shape[1])
            if len(shape) == 3:
                return v.rearrange("p (a b c) -> p a b c", b=shape[1], c=shape[2])
            return v

        def sem(name):
            return mem["sem"](name)

        xT = place(KT, T)
        ident = place(128)
        mod = place(49, 2)
        params2 = place(160)
        rT = place(KT, T)
        ring = [place(FT * 128) for _ in range(2)]
        onesD = place(128)
        ones256 = place(128)
        CL = 136
        params = place(L * CL)
        cur = place(CL)
        lam_y, lam_z, lam_q, lam_s = place(L, 2), place(L, 2), place(L, 2), place(L, 2)
        sinks = place(L * HEADS)
        gate_w = place(4, 128)
        band = place(HEADS, 2 * WIN)
        acc = place(T)
        std = place(T)
        sg = place(2, T)
        eps_ln, eps_conv = place(1), place(1)
        silu_c = place(2, KT)
        ada_slot = place(KT, 128)
        ada_prod = place(2, KT, 128)
        ada_acc = place(2, 128)
        ones_col = place(1)
        mx, nmx, esink, esum, rsum = (place(2, HEADS) for _ in range(5))
        hid_at = cursor[0]
        hid = place(FT, T)
        end = cursor[0]
        cursor[0] = hid_at
        cpad = place(2, 30 + T)
        lpad = place(2, 3 + T)
        gelu_b = place(2, T)
        qT = place(4, T)
        kT = place(T)
        v_tok = place(4, 128)
        xc = place(2, T)
        r_gate, i_gate, decay, mult = (place(2, T) for _ in range(4))
        conv = place(2, T)
        conv_sq = place(2, T)
        conv_rstd = place(T)
        yT = place(KT, T)
        prob = [place(HEADS, 2 * WIN) for _ in range(2)]
        probT = place(HEADS, 2, WIN)
        cursor[0] = max(cursor[0], end)
        x_tok = yT.rearrange("p a b -> p (a b)").rearrange("p (t n) -> p t n", n=KT * 128)
        rows = prob[0].rearrange("p a b -> p (a b)")[:, 0:768].rearrange("p (a b) -> p a b", b=128)
        onehot = prob[1].rearrange("p a b -> p (a b)")[:, 0:WIN]
        relb = prob[1].rearrange("p a b -> p (a b)")[:, WIN:WIN + HEADS]
        erow = prob[1].rearrange("p a b -> p (a b)")[:, 256:256 + 3 * WIN]

        def bank(b):
            return psum[:, b, :]

        LNG, LNB, CB, CG, CBB, LW, LB, BA, BX, LAM, CW, C8, NC8 = (
            0, 24, 48, 50, 52, 54, 62, 64, 66, 68, 70, 132, 134)

        def col(c):
            return cur[:, c:c + 1]

        x_in, rows_in, oh_in, sink_in, e_out, band_in = map(sem, (
            "x_in", "rows_in", "oh_in", "sink_in", "e_out", "band_in"))
        consts, x_tr, par_tr, par_ok, e_mm, e_ok, y_exp, y_in, lam_ok = map(sem, (
            "consts", "x_tr", "par_tr", "par_ok", "e_mm", "e_ok", "y_exp", "y_in", "lam_ok"))
        ada_in, ada_prods, ada_ready, ada_sum, silu_ok, par2_ok = map(sem, (
            "ada_in", "ada_prods", "ada_ready", "ada_sum", "silu_ok", "par2_ok"))
        w_ready = [sem("w_ready0"), sem("w_ready1")]
        bank_free = [sem("bank_free0"), sem("bank_free1")]
        unit_done, x_ready, silu_done = sem("unit_done"), sem("x_ready"), sem("silu_done")
        cur_ready, acc_taken = sem("cur_ready"), sem("acc_taken")
        acc_ready, mean_done, diff_ready, sq_ready, var_done, std_ready, norm_ready = map(sem, (
            "acc_ready", "mean_done", "diff_ready", "sq_ready", "var_done", "std_ready",
            "norm_ready"))
        gw_ready, gw_used, xc_ready, gate_mm, gates_ready, decay_ready, m2_ready, mult_ready = map(
            sem, ("gw_ready", "gw_used", "xc_ready", "gate_mm", "gates_ready", "decay_ready",
                  "m2_ready", "mult_ready"))
        conv_ready, cmean_done, cdiff, csq, cvar_done, cstd, cnorm, y_act, y_dve = map(sem, (
            "conv_ready", "cmean_done", "cdiff", "csq", "cvar_done", "cstd", "cnorm", "y_act",
            "y_dve"))
        s_done, s_used, max_ready, exp_ready, prob_ready, tr_done, pt_ready, o_done, o_used = map(
            sem, ("s_done", "s_used", "max_ready", "exp_ready", "prob_ready", "tr_done",
                  "pt_ready", "o_done", "o_used"))

        UP, DOWN, WIN_P, WOUT = FT // 2, KT // 2, 7, KT // 2
        AT_MIX = UP + DOWN
        AT_OUT = AT_MIX + WIN_P
        AT_FF2 = AT_OUT + WOUT
        PL = AT_FF2 + UP + DOWN
        MIX = [("a", 0), ("g", 0), ("a", 1), ("g", 1), ("xb", 0), ("xb", 1), ("gb", 0), ("gb", 1),
               ("k", 0), ("v", 0), ("q", 0), ("q", 1), ("q", 2), ("q", 3)]
        COLS = {"a": 0, "g": 256, "xb": 512, "gb": 768, "k": 1536, "v": 1664}

        block = ctx.enter_context(nc.Block())

        @block.sync
        def _(sp):
            sp.dma_start(x_tok, d["x"][0].rearrange("(t p) n -> p t n", p=128)).then_inc(x_in, 16)
            for l in range(L):
                at = 0
                for name in ("ln_g", "ln_b"):
                    sp.dma_start(rows[at:at + 24, 2 * l, :],
                                 d[name][l].rearrange("s (k p) -> (s k) p", p=128)).then_inc(rows_in, 16)
                    at += 24
                for name in ("conv_dw_b", "conv_ln_g", "conv_ln_b", "lru_conv_w", "lru_conv_b",
                             "lru_ba", "lru_bx", "lru_lambda"):
                    n = 8 if name == "lru_conv_w" else 2
                    src = (d[name][l].rearrange("s (k p) -> (s k) p", p=128) if n == 8
                           else d[name][l].rearrange("(k p) -> k p", p=128))
                    sp.dma_start(rows[at:at + n, 2 * l, :], src).then_inc(rows_in, 16)
                    at += n
                sp.dma_start(rows[0:62, 2 * l + 1, :],
                             d["conv_dw_w"][l].rearrange("s (k p) -> (s k) p", p=128)).then_inc(rows_in, 16)
            at = 0
            for name, n in (("c_2", 8), ("c_ctx_2", 8), ("ada_b_2", 48), ("norm1_w_2", 8), ("norm2_w_2", 8),
                            ("conv_b_2", 16), ("ssd_norm_w_2", 8), ("final_norm_w_2", 8)):
                v = d[name] if len(d[name].shape) == 1 else d[name][0]
                sp.dma_start(rows[at:at + n, 4, :], v.rearrange("(k p) -> k p", p=128)).then_inc(rows_in, 16)
                at += n
            sp.dma_start(rows[0:48, 5, :], d["conv_w_2"][0].rearrange("s (k p) -> (s k) p", p=128))\
              .then_inc(rows_in, 16)
            sp.dma_start(onehot[0:32, :], d["bucket_onehot"]).then_inc(oh_in, 16)
            sp.dma_start(relb[0:32, :], d["rel_bias"]).then_inc(oh_in, 16)
            sp.dma_start(sinks, d["attn_sinks"].rearrange("l h -> (l h)").partition_broadcast(128))\
              .then_inc(sink_in, 16)
            sp.wait_ge(e_ok, 1)
            sp.dma_start(scratch, erow[0:HEADS, :].unsqueeze(1).to_broadcast([HEADS, 128, 3 * WIN]))\
              .then_inc(e_out, 16)
            sp.wait_ge(e_out, 16)
            sp.dma_start(band, bass.AP(scratch.tensor, scratch.offset + WIN - 1,
                                       [[3 * WIN - 1, 128], [128 * 3 * WIN, HEADS], [1, 2 * WIN]]))\
              .then_inc(band_in, 16)

            def slot_free(pair, side):
                sp.wait_ge(unit_done, 2 * pair + side + 1)

            def tiles(w):
                return w.rearrange("(k p) c -> p k c", p=128)

            def ada_load(a):
                sp.wait_ge(ada_prods, a + 1)
                sp.dma_start(ada_slot, tiles(d["ada_w_2"][0, :, bass.ds(a * 128, 128)])).then_inc(ada_in, 16)

            def ffn_loads(l, s, at):
                with sp.Fori(0, UP) as i:
                    ada_load(l * 24 + s * 12 + i)
                    for side in range(2):
                        slot_free(at + i, side)
                        to = ring[side][:, 0:2 * KT * 128].rearrange("p (k c) -> p k c", c=128)
                        cols = bass.ds((i * 2 + side) * 128, 128)
                        sp.dma_start(to[:, 0:KT, :], tiles(d["ffn_w_gate"][l, s, :, cols]))\
                          .then_inc(w_ready[side], 16)
                        sp.dma_start(to[:, KT:, :], tiles(d["ffn_w_up"][l, s, :, cols]))\
                          .then_inc(w_ready[side], 16)
                ada_load(l * 24 + s * 12 + UP)
                with sp.Fori(0, DOWN) as i:
                    for side in range(2):
                        slot_free(at + UP + i, side)
                        to = ring[side].rearrange("p (k c) -> p k c", c=128)
                        cols = bass.ds((i * 2 + side) * 128, 128)
                        half = FT // 2
                        sp.dma_start(to[:, 0:half, :], tiles(d["ffn_w_down"][l, s, 0:half * 128, cols]))\
                          .then_inc(w_ready[side], 16)
                        sp.dma_start(to[:, half:, :], tiles(d["ffn_w_down"][l, s, half * 128:, cols]))\
                          .then_inc(w_ready[side], 16)

            sp.wait_ge(consts, 1)
            with sp.Fori(0, L) as l:
                sp.wait_ge(gw_used, l + 1)
                for a, name in enumerate(("lru_wa", "lru_wx")):
                    for half in range(2):
                        part = slice(64 * half, 64 * half + 64)
                        src = d[name][l].rearrange("(t f) i j -> f i t j", f=2)[half]
                        sp.dma_start(gate_w[part, 2 * a:2 * a + 2, part], src).then_inc(gw_ready, 16)
                ffn_loads(l, 0, l * PL)
                for n, (kind, t) in enumerate(MIX):
                    pair, side = l * PL + AT_MIX + n // 2, n % 2
                    slot_free(pair, side)
                    to = ring[side][:, 0:KT * 128].rearrange("p (k c) -> p k c", c=128)
                    if kind == "q":
                        for g in range(2):
                            c = 1024 + 64 * (t + 4 * g)
                            sp.dma_start(to[:, :, 64 * g:64 * g + 64], tiles(d["w_in"][l, :, c:c + 64]))\
                              .then_inc(w_ready[side], 16)
                    else:
                        c = COLS[kind] + 128 * t
                        for h in range(2):
                            sp.dma_start(to[:, 4 * h:4 * h + 4, :],
                                         tiles(d["w_in"][l, 512 * h:512 * h + 512, c:c + 128]))\
                              .then_inc(w_ready[side], 16)
                with sp.Fori(0, WOUT) as i:
                    for side in range(2):
                        slot_free(l * PL + AT_OUT + i, side)
                        to = ring[side][:, 0:KT * 128].rearrange("p (k c) -> p k c", c=128)
                        cols = bass.ds((i * 2 + side) * 128, 128)
                        sp.dma_start(to[:, 0:4, :], tiles(d["w_out"][l, 0:512, cols]))\
                          .then_inc(w_ready[side], 16)
                        for g in range(2):
                            src = d["w_out"][l, 512 + 256 * g:768 + 256 * g, cols]
                            sp.dma_start(to[64 * g:64 * g + 64, 4:8, :],
                                         src.rearrange("(j p) c -> p j c", p=64)).then_inc(w_ready[side], 16)
                ffn_loads(l, 1, l * PL + AT_FF2)

        @block.gpsimd
        def _(pool):
            pool.memset(gate_w, 0.0)
            pool.memset(onesD, 1.0 / 1024)
            pool.memset(ones256, 1.0 / 256)
            pool.memset(eps_ln, 1e-5 / ALPHA ** 2)
            pool.memset(eps_conv, 1e-5)
            pool.memset(ones_col, 1.0)
            pool.memset(ada_acc, 0.0)
            pool.memset(ident, 0.0)
            pool.drain()
            pool.affine_select(out=ident, in_=ident, compare_op=ALU.not_equal, fill=1.0, base=0,
                               pattern=[[-1, 128]], channel_multiplier=1)
            pool.drain()
            pool.memset(acc, 0.0).then_inc(consts, 1)
            pool.sem_inc(ada_prods, 1)
            pool.wait_ge(silu_ok, 1)

            def ada_products(a):
                pool.wait_ge(ada_in, a * 16 + 16)
                pool.wait_ge(ada_ready, a + 1)
                for w in range(2):
                    last = pool.tensor_tensor(ada_prod[:, w, :, :], ada_slot,
                                              silu_c[:, w, :].unsqueeze(2).to_broadcast([128, KT, 128]),
                                              ALU.mult)
                last.then_inc(ada_prods, 1)

            def ada_all(a0):
                with pool.Fori(0, UP) as i:
                    ada_products(a0 + i)
                ada_products(a0 + UP)

            def sum_tiles(pair0):
                with pool.Fori(0, KT // 2) as i:
                    for side in range(2):
                        pool.wait_ge(bank_free[side], pair0 + i + 2)
                        tile = rT[:, bass.ds(i * 2 + side, 1), :].rearrange("p a b -> p (a b)")
                        pool.tensor_tensor(acc, acc, tile, ALU.add)
                        pool.drain()

            with pool.Fori(0, L) as l:
                for n, at in enumerate((UP, AT_OUT, AT_FF2 + UP)):
                    if n != 1:
                        ada_all(l * 24 + 6 * n)
                    pool.wait_ge(bank_free[0], l * PL + at + 1)
                    pool.sem_inc(acc_taken, 1)
                    pool.memset(acc, 0.0)
                    pool.drain()
                    sum_tiles(l * PL + at)
                    pool.sem_inc(acc_ready, 1)

        @block.tensor
        def _(pe):
            pe.sem_inc(unit_done, 2)
            pe.sem_inc(bank_free[0], 1)
            pe.sem_inc(bank_free[1], 1)
            pe.sem_inc(gw_used, 1)
            pe.wait_ge(consts, 1)
            pe.wait_ge(x_in, 16)
            for k in range(KT):
                if k >= 2:
                    pe.wait_ge(x_ready, k - 1)
                for t in range(4):
                    mm = pe.transpose(bank(6 + k % 2)[:, t * 128:(t + 1) * 128],
                                      x_tok[:, t, k * 128:(k + 1) * 128], ident)
                mm.then_inc(x_tr, 1)
            pe.wait_ge(rows_in, 16 * (11 * L + 9))
            for l in range(L):
                pe.transpose(psum[:, 4, l * 132:l * 132 + 70], rows[0:70, 2 * l, :], ident[0:70, 0:70])
                mm = pe.transpose(psum[:, 4, l * 132 + 70:l * 132 + 132], rows[0:62, 2 * l + 1, :],
                                  ident[0:62, 0:62])
            pe.transpose(psum[:, 4, 264:376], rows[0:112, 4, :], ident[0:112, 0:112])
            mm = pe.transpose(psum[:, 4, 376:424], rows[0:48, 5, :], ident[0:48, 0:48])
            mm.then_inc(par_tr, 1)
            pe.wait_ge(oh_in, 32)
            pe.matmul(psum[0:HEADS, 5, 0:WIN], relb[0:32, :], onehot[0:32, :], start=True, stop=True)\
              .then_inc(e_mm, 1)

            def wait_unit(pair, side, extra):
                pe.wait_ge(w_ready[side], pair * 32 + extra + 32)
                pe.wait_ge(bank_free[side], pair + 1)

            def norm_stats(n):
                pe.wait_ge(acc_ready, n + 1)
                pe.matmul(bank(4), onesD, acc, start=True, stop=True).then_inc(mean_done, 1)
                for k in range(KT):
                    pe.wait_ge(sq_ready, n * KT + k + 1)
                    mm = pe.matmul(bank(5), onesD, xT[:, k, :], start=(k == 0), stop=(k == KT - 1))
                mm.then_inc(var_done, 1)

            def ada_column(a):
                pe.wait_ge(ada_ready, a + 1)
                pe.matmul(psum[:, 6, 0:1], ada_acc[:, 0, :], ones_col, start=True, stop=True)
                pe.matmul(psum[:, 6, 1:2], ada_acc[:, 1, :], ones_col, start=True, stop=True)\
                  .then_inc(ada_sum, 1)

            def ffn(l, s, at, extra):
                with pe.Fori(0, UP) as i:
                    ada_column(l * 24 + s * 12 + i)
                    for side in range(2):
                        wait_unit(at + i, side, extra)
                        for half in range(2):
                            for k in range(KT):
                                if side == 0 and half == 0:
                                    pe.wait_ge(x_ready, l * 24 + s * 16 + k + 1)
                                c = (half * KT + k) * 128
                                mm = pe.matmul(bank(side + 2 * half), ring[side][:, c:c + 128],
                                               xT[:, k, :], start=(k == 0), stop=(k == KT - 1))
                        mm.then_inc(unit_done, 1)
                ada_column(l * 24 + s * 12 + UP)
                with pe.Fori(0, DOWN) as i:
                    for side in range(2):
                        wait_unit(at + UP + i, side, extra)
                        if side == 0:
                            pe.wait_ge(bank_free[1], at + UP + 1)
                        for k in range(FT):
                            mm = pe.matmul(bank(side), ring[side][:, k * 128:(k + 1) * 128],
                                           hid[:, k, :], start=(k == 0), stop=(k == FT - 1))
                        mm.then_inc(unit_done, 1)
                norm_stats(l * 3 + 2 * s)

            def scores(l, n):
                if n == 0:
                    pe.wait_ge(gates_ready, l + 1)
                else:
                    pe.wait_ge(s_used, l * 4 + n)
                first = 0 if n else WIN
                for j in range(4):
                    for g in range(2):
                        part = slice(64 * g, 64 * g + 64)
                        c = 256 * (j % 2)
                        mm = pe.matmul(psum[:, 4 + 2 * g + j // 2, c + first:c + 256],
                                       qT[part, j, n * 128:(n + 1) * 128],
                                       kT[part, (n - 1) * 128 + first:(n + 1) * 128],
                                       start=True, stop=True)
                mm.then_inc(s_done, 1)

            def attend(l, n):
                pe.wait_ge(prob_ready, l * 4 + n + 1)
                halves = (0, 1) if n else (1,)
                for r in range(4):
                    if r >= 2:
                        pe.wait_ge(pt_ready, l * 16 + n * 4 + r - 1)
                    for h in (2 * r, 2 * r + 1):
                        for half in halves:
                            c = ((h % 2) * 2 + half) * 128
                            mm = pe.transpose(psum[:, 2 + r % 2, c:c + 128],
                                              prob[n % 2][:, h, half * 128:half * 128 + 128], ident)
                    mm.then_inc(tr_done, 1)
                pe.wait_ge(pt_ready, l * 16 + n * 4 + 4)
                if n >= 2:
                    pe.wait_ge(o_used, l * 4 + n - 1)
                for j in range(4):
                    for g in range(2):
                        for half in halves:
                            mm = pe.matmul(psum[64 * g:64 * g + 64, n % 2, j * 128:(j + 1) * 128],
                                           v_tok[:, n - 1 + half, 64 * g:64 * g + 64],
                                           probT[:, 4 * g + j, half, :],
                                           start=(half == halves[0]), stop=(half == 1))
                mm.then_inc(o_done, 1)

            def mixer(l, extra):
                for n, (kind, _) in enumerate(MIX):
                    side = n % 2
                    wait_unit(l * PL + AT_MIX + n // 2, side, extra)
                    w = ring[side][:, 0:KT * 128].rearrange("p (k c) -> p k c", c=128)
                    for t in range(4 if kind == "v" else 1):
                        for k in range(KT):
                            if n == 0:
                                pe.wait_ge(x_ready, l * 24 + 8 + k + 1)
                            if kind == "v":
                                mm = pe.matmul(bank(side)[:, t * 128:(t + 1) * 128],
                                               xT[:, k, t * 128:(t + 1) * 128], w[:, k, :],
                                               start=(k == 0), stop=(k == KT - 1))
                            else:
                                mm = pe.matmul(bank(side), w[:, k, :], xT[:, k, :],
                                               start=(k == 0), stop=(k == KT - 1))
                    mm.then_inc(unit_done, 1)
                pe.wait_ge(xc_ready, l + 1)
                pe.wait_ge(gw_ready, l * 64 + 64)
                for a in range(2):
                    for t in range(2):
                        mm = pe.matmul(bank(4 + 2 * a + t), gate_w[:, 2 * a + t, :], xc[:, t, :],
                                       start=True, stop=True)
                mm.then_inc(gate_mm, 1)
                pe.wait_ge(conv_ready, l + 1)
                for t in range(2):
                    mm = pe.matmul(bank(2), ones256, conv[:, t, :], start=(t == 0), stop=(t == 1))
                mm.then_inc(cmean_done, 1)
                for t in range(2):
                    pe.wait_ge(csq, l * 2 + t + 1)
                    mm = pe.matmul(bank(3), ones256, conv_sq[:, t, :], start=(t == 0), stop=(t == 1))
                mm.then_inc(cvar_done, 1)
                pe.wait_ge(bank_free[0], l * PL + AT_OUT + 1)
                pe.wait_ge(bank_free[1], l * PL + AT_OUT + 1)
                pe.wait_ge(cstd, l + 1)
                scores(l, 0)
                for n in range(4):
                    if n < 3:
                        scores(l, n + 1)
                    attend(l, n)
                pe.sem_inc(gw_used, 1)
                with pe.Fori(0, WOUT) as i:
                    for side in range(2):
                        wait_unit(l * PL + AT_OUT + i, side, extra + (i * 16 + 16))
                        if side == 0:
                            pe.wait_ge(o_used, l * 4 + 4)
                            pe.wait_ge(y_act, l * 2 + 2)
                            pe.wait_ge(y_dve, l * 2 + 2)
                        for k in range(KT):
                            mm = pe.matmul(bank(side), ring[side][:, k * 128:(k + 1) * 128],
                                           yT[:, k, :], start=(k == 0), stop=(k == KT - 1))
                        mm.then_inc(unit_done, 1)
                norm_stats(l * 3 + 1)

            pe.wait_ge(par_ok, 1)
            with pe.Fori(0, L) as l:
                ffn(l, 0, l * PL, l * 64)
                mixer(l, l * 64)
                ffn(l, 1, l * PL + AT_FF2, l * 64 + 64)
            ada_column(2 * 24)

        @block.scalar
        def _(act):
            for k in range(KT):
                act.wait_ge(x_tr, k + 1)
                act.copy(xT[:, k, :], bank(6 + k % 2)).then_inc(x_ready, 1)
            act.wait_ge(par2_ok, 1)
            act.activation(silu_c.rearrange("p w k -> p (w k)"), params2[:, 0:16], ACT.Silu)\
               .then_inc(silu_ok, 1)
            act.wait_ge(y_in, 1)
            act.activation(lam_y, lam_y, ACT.Exp).then_inc(y_exp, 1)
            act.wait_ge(consts, 1)

            def norm(n, g):
                for k in range(KT):
                    act.wait_ge(diff_ready, n * KT + k + 1)
                    act.activation(xT[:, k, :], rT[:, k, :], ACT.Square).then_inc(sq_ready, 1)
                act.wait_ge(var_done, n + 1)
                act.activation(std, bank(5), ACT.Sqrt, bias=eps_ln).then_inc(std_ready, 1)
                for k in range(KT):
                    act.wait_ge(norm_ready, n * KT + k + 1)
                    act.activation(xT[:, k, :], rT[:, k, :], ACT.Identity,
                                   bias=col(LNB + g + k)).then_inc(x_ready, 1)

            def ffn(l, s, at):
                with act.Fori(0, UP) as i:
                    for side in range(2):
                        act.wait_ge(unit_done, at * 2 + i * 2 + side + 3)
                        act.activation(sg[:, side, :], bank(side), ACT.Silu).then_inc(silu_done, 1)
                norm(l * 3 + 2 * s, 16 * s)

            def exps(l, n):
                act.wait_ge(max_ready, l * 4 + n + 1)
                first = 0 if n else WIN
                for h in range(HEADS):
                    p = prob[n % 2][:, h, first:]
                    act.activation(p, p, ACT.Exp, bias=nmx[:, n % 2, h:h + 1],
                                   accum_out=esum[:, n % 2, h:h + 1])
                act.activation(esink[:, n % 2, :], esink[:, n % 2, :], ACT.Exp).then_inc(exp_ready, 1)

            def copies(l, n):
                for r in range(4):
                    act.wait_ge(tr_done, l * 16 + n * 4 + r + 1)
                    first = 0 if n else 1
                    src = psum[:, 2 + r % 2, :].rearrange("p (h f q) -> p h f q", f=2, q=128)
                    act.copy(probT[:, 2 * r:2 * r + 2, first:, :], src[:, :, first:, :])\
                       .then_inc(pt_ready, 1)
                act.wait_ge(o_done, l * 4 + n + 1)
                act.copy(yT[:, 4:8, n * 128:(n + 1) * 128],
                         psum[:, n % 2, :].rearrange("p (j q) -> p j q", q=128)).then_inc(o_used, 1)

            def mixer(l):
                for n, (kind, t) in enumerate(MIX):
                    side = n % 2
                    if kind in ("a", "xb"):
                        continue
                    act.wait_ge(unit_done, (l * PL + AT_MIX) * 2 + n + 3)
                    if kind == "g":
                        out, func, scale = sg[:, t, :], ACT.Sigmoid, 1.0
                    elif kind == "gb":
                        out, func, scale = gelu_b[:, t, :], ACT.Gelu_apprx_tanh, 1.0
                    elif kind == "k":
                        out, func, scale = kT, ACT.Copy, 1.0
                    elif kind == "v":
                        out, func, scale = v_tok.rearrange("p a b -> p (a b)"), ACT.Copy, 1.0
                    else:
                        out, func, scale = qT[:, t, :], ACT.Copy, 64 ** -0.5
                    act.activation(out, bank(side), func, scale=scale).then_inc(bank_free[side], 1)
                act.wait_ge(gate_mm, l + 1)
                for t in range(2):
                    act.activation(r_gate[:, t, :], bank(4 + t), ACT.Sigmoid, bias=col(BA + t))
                for t in range(2):
                    last = act.activation(i_gate[:, t, :], bank(6 + t), ACT.Sigmoid, bias=col(BX + t))
                last.then_inc(gates_ready, 1)
                act.drain()
                for t in range(2):
                    act.activation(decay[:, t, :], r_gate[:, t, :], ACT.Exp, scale=col(C8 + t))
                    last = act.activation(mult[:, t, :], r_gate[:, t, :], ACT.Tanh, scale=col(NC8 + t))
                last.then_inc(decay_ready, 1)
                for t in range(2):
                    act.wait_ge(cdiff, l * 2 + t + 1)
                    act.activation(conv_sq[:, t, :], conv[:, t, :], ACT.Square).then_inc(csq, 1)
                act.wait_ge(m2_ready, l + 1)
                act.activation(mult, mult, ACT.Sqrt).then_inc(mult_ready, 1)
                act.wait_ge(cvar_done, l + 1)
                act.activation(conv_rstd, bank(3), ACT.Sqrt, bias=eps_conv).then_inc(cstd, 1)
                for t in range(2):
                    act.wait_ge(cnorm, l * 2 + t + 1)
                    act.activation(yT[:, t, :], conv[:, t, :], ACT.Silu, bias=col(CBB + t))\
                       .then_inc(y_act, 1)
                exps(l, 0)
                for n in range(4):
                    if n < 3:
                        exps(l, n + 1)
                    copies(l, n)
                norm(l * 3 + 1, 8)

            with act.Fori(0, L) as l:
                act.wait_ge(cur_ready, l + 1)
                ffn(l, 0, l * PL)
                mixer(l)
                ffn(l, 1, l * PL + AT_FF2)

        @block.vector
        def _(dve):
            dve.memset(erow[0:HEADS, :], -1e30)
            dve.wait_ge(par_tr, 1)
            dve.tensor_copy(params2, psum[:, 4, 264:424]).then_inc(par2_ok, 1)
            pv = params.rearrange("p (l c) -> p l c", c=CL)
            dve.tensor_copy(pv[:, :, 0:132], psum[:, 4, 0:2 * 132].rearrange("p (l c) -> p l c", c=132))\
               .then_inc(par_ok, 1)
            dve.wait_ge(e_mm, 1)
            dve.drain()
            dve.tensor_copy(erow[0:HEADS, WIN:2 * WIN], psum[0:HEADS, 5, 0:WIN]).then_inc(e_ok, 1)
            lam = pv[:, :, LAM:LAM + 2]
            dve.drain()
            dve.scalar_tensor_tensor(out=lam_y, in0=lam, scalar=-1.0, in1=lam, op0=ALU.mult,
                                     op1=ALU.min).then_inc(y_in, 1)
            dve.wait_ge(y_exp, 1)
            dve.tensor_scalar(lam_z, lam_y, 2.0, None, ALU.add)
            dve.drain()
            dve.reciprocal(lam_z, lam_z)
            dve.drain()
            dve.tensor_tensor(lam_z, lam_z, lam_y, ALU.mult)
            dve.drain()
            dve.tensor_tensor(lam_q, lam_z, lam_z, ALU.mult)
            dve.memset(lam_s, 1.0 / 19)
            for c in range(17, 0, -2):
                dve.drain()
                dve.tensor_tensor(lam_s, lam_s, lam_q, ALU.mult)
                dve.drain()
                dve.tensor_scalar(lam_s, lam_s, 1.0 / c, None, ALU.add)
            dve.drain()
            dve.scalar_tensor_tensor(out=lam_s, in0=lam_s, scalar=2.0, in1=lam_z, op0=ALU.mult, op1=ALU.mult)
            dve.drain()
            dve.scalar_tensor_tensor(out=lam_s, in0=lam, scalar=0.0, in1=lam_s, op0=ALU.min,
                                     op1=ALU.subtract)
            dve.drain()
            dve.tensor_scalar(pv[:, :, C8:C8 + 2], lam_s, 8.0, None, ALU.mult)
            dve.tensor_scalar(pv[:, :, NC8:NC8 + 2], lam_s, -8.0, None, ALU.mult)
            dve.wait_ge(sink_in, 16)
            dve.wait_ge(band_in, 16)
            dve.wait_ge(consts, 1)
            dve.drain()
            dve.sem_inc(ada_ready, 1)

            def norm(n, g):
                dve.wait_ge(mean_done, n + 1)
                for k in range(KT):
                    dve.tensor_tensor(rT[:, k, :], rT[:, k, :], bank(4), ALU.subtract)\
                       .then_inc(diff_ready, 1)
                dve.wait_ge(std_ready, n + 1)
                dve.reciprocal(std, std)
                dve.drain()
                for k in range(KT):
                    dve.scalar_tensor_tensor(out=rT[:, k, :], in0=rT[:, k, :], scalar=col(LNG + g + k),
                                             in1=std, op0=ALU.mult, op1=ALU.mult)\
                       .then_inc(norm_ready, 1)

            def residuals(pair0, scale):
                with dve.Fori(0, KT // 2) as i:
                    for side in range(2):
                        dve.wait_ge(unit_done, (pair0 + i) * 2 + side + 3)
                        tile = bass.ds(i * 2 + side, 1)
                        dve.scalar_tensor_tensor(
                            out=rT[:, tile, :].rearrange("p a b -> p (a b)"), in0=bank(side),
                            scalar=scale, in1=xT[:, tile, :].rearrange("p a b -> p (a b)"),
                            op0=ALU.mult, op1=ALU.add).then_inc(bank_free[side], 1)

            def put_modulation(a):
                dve.wait_ge(ada_sum, a + 1)
                dve.tensor_tensor(mod[:, bass.ds(a, 1), :].rearrange("p a b -> p (a b)"), psum[:, 6, 0:2],
                                  params2[:, bass.ds(a + 15, 1)].to_broadcast([128, 2]), ALU.add)

            def ada_sums(a):
                put_modulation(a)
                dve.wait_ge(ada_prods, a + 2)
                dve.tensor_reduce(ada_acc, ada_prod.rearrange("p w k c -> p w c k"), AX.X, ALU.add)\
                   .then_inc(ada_ready, 1)

            def ffn(l, s, at):
                with dve.Fori(0, UP) as i:
                    ada_sums(l * 24 + s * 12 + i)
                    for side in range(2):
                        dve.wait_ge(silu_done, l * 2 * FT + s * FT + i * 2 + side + 1)
                        tile = hid[:, bass.ds(i * 2 + side, 1), :].rearrange("p a b -> p (a b)")
                        dve.tensor_tensor(tile, sg[:, side, :], bank(2 + side), ALU.mult)\
                           .then_inc(bank_free[side], 1)
                ada_sums(l * 24 + s * 12 + UP)
                residuals(at + UP, 0.5 / ALPHA)
                norm(l * 3 + 2 * s, 16 * s)

            def scores(l, n):
                b, first = n % 2, 0 if n else WIN
                p = prob[b][:, :, first:]
                dve.wait_ge(s_done, l * 4 + n + 1)
                ps = psum[:, 4:8, :].rearrange("p b (h k) -> p (b h) k", k=256)
                dve.tensor_tensor(p, ps[:, :, first:], band[:, :, first:], ALU.add).then_inc(s_used, 1)
                dve.drain()
                dve.tensor_reduce(mx[:, b, :], p, AX.X, ALU.max)
                dve.drain()
                dve.tensor_tensor(mx[:, b, :], mx[:, b, :], sink_of[0], ALU.max)
                dve.drain()
                dve.tensor_tensor(esink[:, b, :], sink_of[0], mx[:, b, :], ALU.subtract)
                dve.tensor_scalar(nmx[:, b, :], mx[:, b, :], -1.0, None, ALU.mult).then_inc(max_ready, 1)

            def normalise(l, n):
                b, first = n % 2, 0 if n else WIN
                p = prob[b][:, :, first:]
                dve.wait_ge(exp_ready, l * 4 + n + 1)
                dve.tensor_tensor(rsum[:, b, :], esum[:, b, :], esink[:, b, :], ALU.add)
                dve.drain()
                dve.reciprocal(rsum[:, b, :], rsum[:, b, :])
                dve.drain()
                dve.tensor_tensor(p, p, rsum[:, b, :].unsqueeze(2).to_broadcast([128, HEADS, 256 - first]),
                                  ALU.mult).then_inc(prob_ready, 1)

            def taps(out, pad, n, w, bias):
                for c in range(n):
                    for t in range(2):
                        src = pad[:, t, c:c + T]
                        if c == 0:
                            last = dve.tensor_scalar(out[:, t, :], src, col(w + t), col(bias + t),
                                                     ALU.mult, ALU.add)
                        else:
                            last = dve.scalar_tensor_tensor(out=out[:, t, :], in0=src,
                                                            scalar=col(w + 2 * c + t), in1=out[:, t, :],
                                                            op0=ALU.mult, op1=ALU.add)
                    if c < n - 1:
                        dve.drain()
                return last

            sink_of = [None]

            def mixer(l):
                sink_of[0] = sinks[:, bass.ds(l * HEADS, HEADS)]
                dve.memset(cpad[:, :, 0:30], 0.0)
                dve.memset(lpad[:, :, 0:3], 0.0)
                for n, (kind, t) in enumerate(MIX[:6]):
                    pair, side = l * PL + AT_MIX + n // 2, n % 2
                    if kind == "a":
                        dve.wait_ge(bank_free[1], pair + 2)
                        dve.tensor_tensor(cpad[:, t, 30:], sg[:, t, :], bank(0), ALU.mult)\
                           .then_inc(bank_free[0], 1)
                    elif kind == "xb":
                        dve.wait_ge(unit_done, pair * 2 + side + 3)
                        dve.tensor_copy(lpad[:, t, 3:], bank(side)).then_inc(bank_free[side], 1)
                dve.drain()
                taps(xc, lpad, 4, LW, LB).then_inc(xc_ready, 1)
                taps(conv, cpad, 31, CW, CB).then_inc(conv_ready, 1)
                dve.wait_ge(decay_ready, l + 1)
                dve.tensor_tensor(i_gate, i_gate, xc, ALU.mult)
                dve.tensor_tensor(r_gate, decay, decay, ALU.mult)
                dve.drain()
                dve.scalar_tensor_tensor(out=mult, in0=r_gate, scalar=1.0, in1=mult, op0=ALU.add,
                                         op1=ALU.mult).then_inc(m2_ready, 1)
                dve.wait_ge(cmean_done, l + 1)
                for t in range(2):
                    dve.tensor_tensor(conv[:, t, :], conv[:, t, :], bank(2), ALU.subtract)\
                       .then_inc(cdiff, 1)
                dve.wait_ge(mult_ready, l + 1)
                dve.tensor_tensor(i_gate, i_gate, mult, ALU.mult)
                dve.drain()
                for t in range(2):
                    dve.tensor_tensor_scan(r_gate[:, t, :], decay[:, t, :], i_gate[:, t, :], 0.0,
                                           ALU.mult, ALU.add)
                dve.wait_ge(cstd, l + 1)
                dve.reciprocal(conv_rstd, conv_rstd)
                dve.drain()
                for t in range(2):
                    dve.scalar_tensor_tensor(out=conv[:, t, :], in0=conv[:, t, :], scalar=col(CG + t),
                                             in1=conv_rstd, op0=ALU.mult, op1=ALU.mult)\
                       .then_inc(cnorm, 1)
                for t in range(2):
                    dve.wait_ge(bank_free[t], l * PL + AT_MIX + 5)
                    dve.tensor_tensor(yT[:, 2 + t, :], r_gate[:, t, :], gelu_b[:, t, :], ALU.mult)\
                       .then_inc(y_dve, 1)
                scores(l, 0)
                for n in range(4):
                    if n < 3:
                        scores(l, n + 1)
                    normalise(l, n)
                residuals(l * PL + AT_OUT, 1.0 / ALPHA)
                norm(l * 3 + 1, 8)

            with dve.Fori(0, L) as l:
                dve.wait_ge(x_ready, l * 24 + 8)
                dve.tensor_copy(cur, params[:, bass.ds(l * CL, CL)]).then_inc(cur_ready, 1)
                ffn(l, 0, l * PL)
                mixer(l)
                ffn(l, 1, l * PL + AT_FF2)
            put_modulation(2 * 24)


def second_mixer_program(nc, d, mem):
    f32 = mybir.dt.float32
    ALU, ACT, AX = mybir.AluOpType, mybir.ActivationFunctionType, mybir.AxisListType
    KT, T, C = 8, 512, 256
    NT, NC, CH = 4, 2, 128
    H, G = 16, 4
    XS, BM, CM = 0, 8, 12
    ZC, UC, VC, GA, GB = 2080, 3104, 4128, 5152, 6176

    ctx = ExitStack()
    with ctx:
        arena, psum = mem["arena"], mem["psum"]
        cursor = [0]

        def place(*shape):
            size = int(np.prod(shape))
            v = arena[:, cursor[0]:cursor[0] + size]
            cursor[0] += size
            assert cursor[0] <= mem["size"], cursor[0]
            if len(shape) == 2:
                return v.rearrange("p (a b) -> p a b", b=shape[1])
            if len(shape) == 3:
                return v.rearrange("p (a b c) -> p a b c", b=shape[1], c=shape[2])
            return v

        def sem(name):
            return mem["sem"]("m_" + name)

        res = place(KT, T)
        ident = place(128)
        mod = place(49, 2)[:, 1:, :]
        params = place(160)
        ring = [place(2048) for _ in range(2)]
        onesD, ones1, ones256 = place(128), place(128), place(128)
        tri_f, tri_b, mask_f, mask_b = place(128), place(128), place(128), place(128)
        eps6 = place(1)
        nscale = place(KT, 2)
        d_all, d_skip = place(H), place(KT)
        dt_bias, a_neg = place(32), place(32)
        w_dt = place(KT, 32)
        dt, dta, dt_y, dt_z, dt_q, dt_s = (place(6, 32) for _ in range(6))
        nacum, w_end, c_dec = place(6, 32), place(6, 32), place(6, 32)
        rstd = place(T)
        pad_l = place(2, T + 2)
        pad_c = place(2, C + 2)
        cv = place(2, T)
        xm = place(KT, T)
        y = place(KT, T)
        c_in = y[:, 0:4, :].rearrange("p a b -> p (a b)").rearrange("p (a b) -> p a b", b=C)
        xm_c = y[:, 4:8, :].rearrange("p a b -> p (a b)").rearrange("p (a b) -> p a b", b=C)
        xbc = place(16, T)
        xbc_flat = xbc.rearrange("p a b -> p (a b)")
        xbc_c = xbc_flat[:, 0:12 * C].rearrange("p (a b) -> p a b", b=C)
        sq_c = xbc_flat[:, 4096:4096 + KT * C].rearrange("p (a b) -> p a b", b=C)
        c_tok = xbc_flat[:, 0:2048].rearrange("p (a b) -> p a b", b=1024)
        x_tok = place(NT, 1024)
        b_tok = place(NT, 512)
        xw = place(2, 1024)
        state = [place(NT, 1024) for _ in range(2)]
        df, db, cf, cb = (place(2, 4, CH) for _ in range(4))
        v_tok = x_tok
        uT = state[0].rearrange("p a b -> p (a b)").rearrange("p (a b) -> p a b", b=T)
        sgu = state[1].rearrange("p a b -> p (a b)").rearrange("p (a b) -> p a b", b=T)
        sq_y = xbc[:, 0:8, :]
        merged = v_tok.rearrange("p a b -> p (a b)").rearrange("p (a b) -> p a b", b=T)
        tail = xbc[:, 8:16, :].rearrange("p a b -> p (a b)")
        ln_w, ln_b, bs_bc = tail[:, 0:1024], tail[:, 1024:2048], tail[:, 2048:3072]
        ws_T = tail[:, 3072:4096].rearrange("p (g i) -> p g i", g=8)
        ws_in = b_tok.rearrange("p a b -> p (a b)")[:, 0:1024].rearrange("p (g j) -> p g j", g=8)
        sq_v = xw.rearrange("p a b -> p (a b)")[:, 0:1024]
        mixed = xw.rearrange("p a b -> p (a b)")[:, 1024:2048].rearrange("p (s t) -> p s t", s=2)
        z_s = df.rearrange("p s h i -> p s (h i)")
        ga_s, gb_s = (cf.rearrange("p s h i -> p s (h i)")[:, 0, :], cf.rearrange("p s h i -> p s (h i)")[:, 1, :])
        rs_y = db.rearrange("p s h i -> p s (h i)")
        rs_y2 = cb.rearrange("p s h i -> p s (h i)")
        v_sum, v_var = place(NT), place(NT)

        PN1, PCB, PSN, PCW = 64, 80, 96, 112

        def bank(b):
            return psum[:, b, :]

        def par(c):
            return params[:, c:c + 1]

        names = ("ctx_in small_in wdt_in consts ctx_tr ctx_t a_exp "
                 "unit_done sqc_ready varc_done stdc_ready nc_ready xmc_ready sql_ready varl_done "
                 "stdl_ready nl_ready xml_ready dt_mm dt_abs dt_exp dt_ok cum_done ac_ready w_ready2 tr_done "
                 "tr_used xw_ready st_done st_used  conv_done xbc_ready bc_done tm_ready "
                 "ea_ready fb_ready ff_ready cc_ready pb_ready m_ready y_done y_used ln_in ws_in_s "
                 "v_gelu v_mean v_sq v_std v_ok ws_tr ws_ok u_ok mix_done mix_used y_sq gvar_done gstd y_ok "
                 "z_ok ga_ready mg_ready sgu_ok").split()
        s = {n: sem(n) for n in names}
        w_ready = [sem("w_ready0"), sem("w_ready1")]
        bank_free = [sem("bank_free0"), sem("bank_free1")]
        unit_done = s["unit_done"]

        CTX, SCAN, VP, UP, ZP, MERGE, WO = 0, 6, 14, 16, 20, 24, 32

        block = ctx.enter_context(nc.Block())

        @block.sync
        def _(sp):
            sp.dma_start(c_tok, d["ctx_2"][0].rearrange("(t p) n -> p t n", p=128)).then_inc(s["ctx_in"], 16)

            def slot_free(pair, side):
                sp.wait_ge(unit_done, 2 * pair + side + 1)

            def tiles(w):
                return w.rearrange("(k p) c -> p k c", p=128)

            def load(side, cols, sources):
                if len(sources) == 1:
                    to = ring[side][:, 0:KT * cols].rearrange("p (k c) -> p k c", c=cols)
                    for h in range(2):
                        sp.dma_start(to[:, 4 * h:4 * h + 4, :], tiles(sources[0](512 * h, 512)))\
                          .then_inc(w_ready[side], 16)
                else:
                    to = ring[side].rearrange("p (k c) -> p k c", c=cols)
                    for h in range(2):
                        sp.dma_start(to[:, KT * h:KT * h + KT, :], tiles(sources[h](0, 1024)))\
                          .then_inc(w_ready[side], 16)

            def of(name, c0, i, step, width):
                return lambda r, n: d[name][0, r:r + n, bass.ds(i * step + c0, width)]

            sp.dma_start(d_all, d["d_skip_2"][0].partition_broadcast(128)).then_inc(s["small_in"], 16)
            sp.dma_start(dt_bias, d["dt_bias_2"][0].rearrange("a h -> (a h)").partition_broadcast(128))\
              .then_inc(s["small_in"], 16)
            sp.dma_start(a_neg, d["a_log_2"][0].rearrange("a h -> (a h)").partition_broadcast(128))\
              .then_inc(s["small_in"], 16)
            sp.dma_start(w_dt, tiles(d["w_in_2"][0, :, 2048:2080])).then_inc(s["wdt_in"], 16)

            def single(pair0, n, c0, name="w_in_2"):
                with sp.Fori(0, n) as i:
                    for side in range(2):
                        slot_free(i + pair0, side)
                        load(side, 128, [of(name, c0 + side * 128, i, 256, 128)])

            single(CTX, 6, 0)
            single(SCAN, 8, 0)
            for n in range(4):
                slot_free(VP + n // 2, n % 2)
                load(n % 2, 256, [of("w_in_2", VC + 256 * n, 0, 0, 256)])
            sp.wait_ge(s["y_used"], 16)
            for to, name in ((ln_w, "sgu_ln_w_2"), (ln_b, "sgu_ln_b_2")):
                sp.dma_start(to, d[name][0].partition_broadcast(128)).then_inc(s["ln_in"], 16)
            sp.dma_start(bs_bc, d["b_s_2"][0].rearrange("g i -> (g i)").partition_broadcast(128))\
              .then_inc(s["ln_in"], 16)
            sp.dma_start(ws_in, d["w_s_2"][0].rearrange("g i j -> i g j")).then_inc(s["ws_in_s"], 16)
            single(UP, 4, UC)
            single(ZP, 4, ZC)
            with sp.Fori(0, 8) as i:
                slot_free(i + MERGE, 0)
                load(0, 128, [of("w_pa_2", 0, i, 128, 128), of("w_pb_2", 0, i, 128, 128)])
                slot_free(i + MERGE, 1)
                load(1, 128, [of("w_in_2", GA, i, 128, 128), of("w_in_2", GB, i, 128, 128)])
            single(WO, 4, 0, "w_o_2")

        @block.gpsimd
        def _(pool):
            pool.memset(onesD, 1.0 / 1024)
            pool.memset(ones1, 1.0)
            pool.memset(ones256, 1.0 / 256)
            pool.memset(eps6, 1e-6)
            pool.memset(tri_f, 1.0)
            pool.memset(tri_b, 1.0)
            pool.memset(mask_f, 0.0)
            pool.memset(mask_b, 0.0)
            pool.memset(pad_l, 0.0)
            pool.memset(pad_c, 0.0)
            pool.memset(state[0], 0.0)
            pool.memset(state[1], 0.0)
            pool.drain()
            for m, fill, sign in ((tri_f, 0.0, 1), (tri_b, 0.0, -1), (mask_f, -1e30, 1), (mask_b, -1e30, -1)):
                pool.affine_select(out=m, in_=m, compare_op=ALU.is_ge, fill=fill, base=0,
                                   pattern=[[sign, 128]], channel_multiplier=-sign)
            pool.drain()
            pool.sem_inc(s["consts"], 1)
            for n in range(NT * G):
                c, g, b = n // G, n % G, n % 2
                ct = xbc[:, CM + g, c * CH:(c + 1) * CH].unsqueeze(1).to_broadcast([128, 4, CH])
                pool.wait_ge(s["ea_ready"], n + 1)
                pool.tensor_tensor(cf[:, b, :, :], cf[:, b, :, :], ct, ALU.mult)
                pool.tensor_tensor(cb[:, b, :, :], cb[:, b, :, :], ct, ALU.mult).then_inc(s["cc_ready"], 1)
                pool.wait_ge(s["fb_ready"], n + 1)
                dtb = dt[:, c, H + 4 * g:H + 4 * g + 4].unsqueeze(2).to_broadcast([128, 4, CH])
                pool.tensor_tensor(db[:, b, :, :], db[:, b, :, :], dtb, ALU.mult).then_inc(s["pb_ready"], 1)

        steps = ([(0, NT + c, 0, 0) for c in range(NC)] + [(1, NT + c, 3, 3) for c in reversed(range(NC))])
        steps_l = [(0, c, c, c + 1) for c in range(3)] + [(1, c, c, c - 1) for c in (3, 2, 1)]

        def st_banks(k):
            return (2, 3) if k % 2 == 0 else (6, 7)

        @block.tensor
        def _(pe):
            pe.sem_inc(unit_done, 2)
            pe.sem_inc(bank_free[0], 1)
            pe.sem_inc(bank_free[1], 1)
            pe.wait_ge(s["ctx_in"], 16)
            for k in range(KT):
                if k >= 2:
                    pe.wait_ge(s["ctx_t"], k - 1)
                for t in range(NC):
                    mm = pe.transpose(psum[:, 6 + k % 2, t * 128:(t + 1) * 128],
                                      c_tok[:, t, k * 128:(k + 1) * 128], ident)
                mm.then_inc(s["ctx_tr"], 1)

            def wait_unit(pair, side):
                pe.wait_ge(w_ready[side], pair * 32 + 32)
                pe.wait_ge(bank_free[side], pair + 1)

            pe.wait_ge(s["consts"], 1)
            def rms(sq, ready, done, width):
                for k in range(KT):
                    pe.wait_ge(ready, k + 1)
                    mm = pe.matmul(psum[:, 5, 0:width], onesD, sq[:, k, :], start=(k == 0), stop=(k == KT - 1))
                mm.then_inc(done, 1)

            def raw_dt(x, ready, t0, n, base):
                pe.wait_ge(ready, KT)
                pe.wait_ge(s["wdt_in"], 16)
                for t in range(n):
                    for k in range(KT):
                        mm = pe.matmul(psum[:, 4, (t0 + t) * 32:(t0 + t + 1) * 32], x[:, k, t * 128:(t + 1) * 128],
                                       w_dt[:, k, :], start=(k == 0), stop=(k == KT - 1))
                mm.then_inc(s["dt_mm"], 1)

            def units(pair0, n, x, width):
                with pe.Fori(0, n) as i:
                    for side in range(2):
                        wait_unit(i + pair0, side)
                        for k in range(KT):
                            mm = pe.matmul(psum[:, side, 0:width], ring[side][:, k * 128:(k + 1) * 128],
                                           x[:, k, :], start=(k == 0), stop=(k == KT - 1))
                        mm.then_inc(unit_done, 1)

            def cumulate(t0, n, call):
                pe.wait_ge(s["dt_ok"], call)
                for t in range(t0, t0 + n):
                    pe.matmul(psum[:, 5, t * 64:t * 64 + 16], tri_f, dta[:, t, 0:16], start=True, stop=True)
                    pe.matmul(psum[:, 5, t * 64 + 16:t * 64 + 32], tri_b, dta[:, t, 16:32], start=True, stop=True)
                    mm = pe.matmul(psum[:, 5, t * 64 + 32:t * 64 + 64], ones1, dta[:, t, :], start=True, stop=True)
                mm.then_inc(s["cum_done"], 1)

            def to_tokens(x, n, round0, x_count):
                pe.wait_ge(s["xbc_ready"], x_count)
                for r in range(3 * n):
                    if round0 + r >= 2:
                        pe.wait_ge(s["tr_used"], round0 + r - 1)
                    c, part = r // 3, r % 3
                    for q in range(4):
                        mm = pe.transpose(psum[:, 6 + r % 2, q * 128:(q + 1) * 128],
                                          x[:, 4 * part + q, c * CH:(c + 1) * CH], ident)
                    mm.then_inc(s["tr_done"], 1)
                pe.wait_ge(s["tr_used"], round0 + 3 * n)

            def states(k0, some):
                for k, (way, t, _, _) in enumerate(some, k0):
                    pe.wait_ge(s["xw_ready"], k + 1)
                    if k >= 2:
                        pe.wait_ge(s["st_used"], k - 1)
                    for g in range(G):
                        mm = pe.matmul(psum[:, st_banks(k)[g // 2], (g % 2) * 256:(g % 2) * 256 + 256],
                                       b_tok[:, t % NT, g * 128:(g + 1) * 128],
                                       xw[:, k % 2, g * 256:(g + 1) * 256], start=True, stop=True)
                    mm.then_inc(s["st_done"], 1)

            rms(sq_c, s["sqc_ready"], s["varc_done"], C)
            raw_dt(xm_c, s["xmc_ready"], NT, NC, 0)
            units(CTX, 6, xm_c, C)
            cumulate(NT, NC, 1)
            to_tokens(xbc_c, NC, 0, 12)
            states(0, steps)
            rms(y, s["sql_ready"], s["varl_done"], T)
            raw_dt(xm, s["xml_ready"], 0, NT, 0)
            units(SCAN, 8, xm, T)
            cumulate(0, NT, 2)
            to_tokens(xbc, NT, 3 * NC, 12 + 16)
            states(4, steps_l)
            pe.wait_ge(s["st_used"], 10)
            pe.wait_ge(bank_free[0], VP + 1)
            pe.wait_ge(bank_free[1], VP + 1)

            def bcasts(n):
                c, g, b = n // G, n % G, n % 2
                if n >= 2:
                    pe.wait_ge(s["ff_ready"], n - 1)
                    pe.wait_ge(s["m_ready"], n - 1)
                chunk = slice(c * CH, (c + 1) * CH)
                pe.matmul(psum[:, 4 + 3 * b, 0:CH], xbc[:, BM + g, chunk], xbc[:, CM + g, chunk],
                          start=True, stop=True)
                for way, tri in ((0, tri_f), (1, tri_b)):
                    for h in range(4):
                        col = dta[:, c, H * way + 4 * g + h:H * way + 4 * g + h + 1]
                        mm = pe.matmul(psum[:, 2 + 3 * b + way, h * CH:(h + 1) * CH],
                                       col.to_broadcast([128, 128]), tri, start=True, stop=True)
                mm.then_inc(s["bc_done"], 1)

            def outputs(n):
                c, g, b = n // G, n % G, n % 2
                pe.wait_ge(s["cc_ready"], n + 1)
                pe.wait_ge(s["m_ready"], n + 1)
                if n >= 2:
                    pe.wait_ge(s["y_used"], n - 1)
                for h in range(4):
                    cols = slice((4 * g + h) * 64, (4 * g + h + 1) * 64)
                    out = psum[64 * (h % 2):64 * (h % 2) + 64, b, (h // 2) * CH:(h // 2 + 1) * CH]
                    pe.matmul(out, x_tok[:, c, cols], df[:, b, h, :], start=True, stop=False)
                    pe.matmul(out, state[0][:, c, cols], cf[:, b, h, :], start=False, stop=False)
                    mm = pe.matmul(out, state[1][:, c, cols], cb[:, b, h, :], start=False, stop=True)
                mm.then_inc(s["y_done"], 1)

            bcasts(0)
            for n in range(NT * G):
                if n + 1 < NT * G:
                    bcasts(n + 1)
                outputs(n)
            pe.wait_ge(s["y_used"], 16)
            for n in range(4):
                side = n % 2
                wait_unit(VP + n // 2, side)
                w = ring[side].rearrange("p (k c) -> p k c", c=256)
                for t in range(NT):
                    for k in range(KT):
                        mm = pe.matmul(psum[:, side + 2 * (t // 2), (t % 2) * 256:(t % 2) * 256 + 256],
                                       xm[:, k, t * 128:(t + 1) * 128], w[:, k, :],
                                       start=(k == 0), stop=(k == KT - 1))
                mm.then_inc(unit_done, 1)
            units(UP, 4, xm, T)
            pe.wait_ge(s["ws_in_s"], 16)
            for r in range(2):
                for q in range(4):
                    mm = pe.transpose(psum[:, 6 + r, q * 128:(q + 1) * 128], ws_in[:, 4 * r + q, :], ident)
            mm.then_inc(s["ws_tr"], 1)
            units(ZP, 4, xm, T)
            pe.wait_ge(s["v_ok"], 1)
            pe.wait_ge(s["ws_ok"], 1)
            for g in range(8):
                if g >= 2:
                    pe.wait_ge(s["mix_used"], g - 1)
                for c in range(NT):
                    mm = pe.matmul(psum[:, 4 + g % 2, c * CH:(c + 1) * CH], v_tok[:, c, g * 128:(g + 1) * 128],
                                   ws_T[:, g, :], start=True, stop=True)
                mm.then_inc(s["mix_done"], 1)
            for q in range(4):
                if q >= 2:
                    pe.wait_ge(s["gstd"], q - 1)
                for t in range(2):
                    pe.wait_ge(s["y_sq"], 2 * q + t + 1)
                    mm = pe.matmul(bank(6 + q % 2), ones256, sq_y[:, 2 * q + t, :], start=(t == 0), stop=(t == 1))
                mm.then_inc(s["gvar_done"], 1)
            with pe.Fori(0, 8) as i:
                for side in range(2):
                    wait_unit(i + MERGE, side)
                    if side == 0:
                        pe.wait_ge(s["y_ok"], 8)
                        pe.wait_ge(s["mix_used"], 8)
                    for half in range(2):
                        x = xm if side else (y, sgu)[half]
                        for k in range(KT):
                            c = (half * KT + k) * 128
                            mm = pe.matmul(bank(side + 2 * half), ring[side][:, c:c + 128], x[:, k, :],
                                           start=(k == 0), stop=(k == KT - 1))
                    mm.then_inc(unit_done, 1)
            pe.wait_ge(bank_free[0], WO + 1)
            pe.sem_inc(s["mg_ready"], 1)
            units(WO, 4, merged, T)

        @block.scalar
        def _(act):
            for k in range(KT):
                act.wait_ge(s["ctx_tr"], k + 1)
                act.copy(c_in[:, k, :], psum[:, 6 + k % 2, 0:C]).then_inc(s["ctx_t"], 1)
            act.drain()
            for k in range(KT):
                act.activation(sq_c[:, k, :], c_in[:, k, :], ACT.Square).then_inc(s["sqc_ready"], 1)
            act.wait_ge(s["small_in"], 48)
            act.activation(a_neg, a_neg, ACT.Exp).then_inc(s["a_exp"], 1)

            def rms(width, dst, which, done, std_ready, n_ready, out_ready):
                act.wait_ge(done, 1)
                act.activation(rstd[:, 0:width], psum[:, 5, 0:width], ACT.Sqrt, bias=eps6).then_inc(std_ready, 1)
                for k in range(KT):
                    act.wait_ge(n_ready, k + 1)
                    act.activation(dst[:, k, :], dst[:, k, :], ACT.Identity, bias=mod[:, k, which:which + 1])\
                       .then_inc(out_ready, 1)

            def scan_units(pair0, n, pad, width, dst):
                with act.Fori(0, n) as i:
                    for side in range(2):
                        act.wait_ge(unit_done, (i + pair0) * 2 + side + 3)
                        act.copy(pad[:, side, 1:1 + width], psum[:, side, 0:width]).then_inc(bank_free[side], 1)
                        act.wait_ge(s["conv_done"], (i + (pair0 - CTX)) * 2 + side + 1)
                        act.activation(dst[:, bass.ds(i * 2 + side, 1), :].rearrange("p a b -> p (a b)"),
                                       cv[:, side, 0:width], ACT.Silu,
                                       bias=params[:, bass.ds(i * 2 + (PCB + side), 1)])\
                           .then_inc(s["xbc_ready"], 1)

            def softplus_exp(call, t0, n):
                act.wait_ge(s["dt_abs"], call)
                act.activation(dt_y[:, t0:t0 + n, :], dt_y[:, t0:t0 + n, :], ACT.Exp).then_inc(s["dt_exp"], 1)

            def decays(call, t0, n):
                act.wait_ge(s["ac_ready"], call)
                act.activation(w_end[:, t0:t0 + n, :], w_end[:, t0:t0 + n, :], ACT.Exp)
                act.activation(c_dec[:, t0:t0 + n, :], c_dec[:, t0:t0 + n, :], ACT.Exp).then_inc(s["w_ready2"], 1)

            def token_copies(n, round0):
                for r in range(3 * n):
                    act.wait_ge(s["tr_done"], round0 + r + 1)
                    c, part = r // 3, r % 3
                    to = x_tok[:, c, part * 512:(part + 1) * 512] if part < 2 else b_tok[:, c, :]
                    act.copy(to, bank(6 + r % 2)).then_inc(s["tr_used"], 1)

            rms(C, xm_c, 1, s["varc_done"], s["stdc_ready"], s["nc_ready"], s["xmc_ready"])
            softplus_exp(1, NT, NC)
            scan_units(CTX, 6, pad_c, C, xbc_c)
            decays(1, NT, NC)
            token_copies(NC, 0)
            act.wait_ge(unit_done, SCAN * 2 + 2)
            for k in range(KT):
                act.activation(y[:, k, :], res[:, k, :], ACT.Square).then_inc(s["sql_ready"], 1)
            rms(T, xm, 0, s["varl_done"], s["stdl_ready"], s["nl_ready"], s["xml_ready"])
            softplus_exp(2, 0, NT)
            scan_units(SCAN, 8, pad_l, T, xbc)
            decays(2, 0, NT)
            token_copies(NT, 3 * NC)
            for n in range(NT * G):
                c, g, b = n // G, n % G, n % 2
                act.wait_ge(s["tm_ready"], n + 1)
                if n >= 2:
                    act.wait_ge(s["y_done"], n - 1)
                act.activation(cf[:, b, :, :].rearrange("p h i -> p (h i)"), bank(2 + 3 * b), ACT.Exp)
                act.activation(cb[:, b, :, :].rearrange("p h i -> p (h i)"), bank(3 + 3 * b), ACT.Exp)\
                   .then_inc(s["ea_ready"], 1)
                for way, m, ready in ((1, db, "fb_ready"), (0, df, "ff_ready")):
                    for h in range(4):
                        at = H * way + 4 * g + h
                        last = act.activation(m[:, b, h, :], m[:, b, h, :], ACT.Exp,
                                              bias=nacum[:, c, at:at + 1])
                    last.then_inc(s[ready], 1)
            for n in range(4):
                side = n % 2
                act.wait_ge(unit_done, (VP + n // 2) * 2 + side + 3)
                for half in range(2):
                    last = act.activation(v_tok[:, 2 * half:2 * half + 2, n * 256:(n + 1) * 256],
                                          psum[:, side + 2 * half, :].rearrange("p (t c) -> p t c", c=256),
                                          ACT.Gelu_apprx_tanh)
                last.then_inc(bank_free[side], 1)
            act.drain()
            act.sem_inc(s["v_gelu"], 1)
            with act.Fori(0, 4) as i:
                for side in range(2):
                    act.wait_ge(unit_done, (i + UP) * 2 + side + 3)
                    act.activation(uT[:, bass.ds(i * 2 + side, 1), :].rearrange("p a b -> p (a b)"),
                                   bank(side), ACT.Gelu_apprx_tanh).then_inc(bank_free[side], 1)
            act.wait_ge(s["ws_tr"], 1)
            for r in range(2):
                last = act.copy(ws_T[:, 4 * r:4 * r + 4, :].rearrange("p a b -> p (a b)"), bank(6 + r))
            last.then_inc(s["ws_ok"], 1)
            act.wait_ge(s["v_mean"], 1)
            for t in range(NT):
                if t:
                    act.drain()
                last = act.activation(sq_v, v_tok[:, t, :], ACT.Square, accum_out=v_var[:, t:t + 1])
            act.drain()
            act.activation(v_var, v_var, ACT.Sqrt, scale=1.0 / 1024, bias=eps6).then_inc(s["v_std"], 1)
            with act.Fori(0, 4) as i:
                for side in range(2):
                    act.wait_ge(unit_done, (i + ZP) * 2 + side + 3)
                    act.activation(z_s[:, side, :], bank(side), ACT.Silu).then_inc(bank_free[side], 1)
                    tile = bass.ds(i * 2 + side, 1)
                    act.wait_ge(s["z_ok"], i * 2 + side + 1)
                    act.activation(sq_y[:, tile, :].rearrange("p a b -> p (a b)"),
                                   y[:, tile, :].rearrange("p a b -> p (a b)"), ACT.Square)\
                       .then_inc(s["y_sq"], 1)
            for q in range(4):
                act.wait_ge(s["gvar_done"], q + 1)
                act.activation((rs_y if q < 2 else rs_y2)[:, q % 2, :], bank(6 + q % 2), ACT.Sqrt, bias=eps6)\
                   .then_inc(s["gstd"], 1)
            with act.Fori(0, 8) as i:
                act.wait_ge(unit_done, (i + MERGE) * 2 + 4)
                act.activation(ga_s, bank(1), ACT.Sigmoid)
                act.activation(gb_s, bank(3), ACT.Sigmoid).then_inc(bank_free[1], 1)

        @block.vector
        def _(dve):
            n1 = params[:, PN1:PN1 + KT].unsqueeze(2).to_broadcast([128, KT, 2])
            dve.tensor_tensor(nscale, mod[:, 8:16, :], n1, ALU.mult)
            dve.drain()
            dve.tensor_tensor(nscale, nscale, n1, ALU.add)
            dve.wait_ge(s["a_exp"], 1)
            dve.tensor_scalar(a_neg, a_neg, -1.0, None, ALU.mult)
            for half in range(2):
                part = slice(64 * half, 64 * half + 64)
                dve.tensor_copy(d_skip[part, :], d_all[part, :].rearrange("p (k f) -> p k f", f=2)[:, :, half])
            dve.drain()

            def rms(src, dst, width, which, std_ready, n_ready):
                dve.wait_ge(std_ready, 1)
                dve.reciprocal(rstd[:, 0:width], rstd[:, 0:width])
                dve.drain()
                for k in range(KT):
                    dve.scalar_tensor_tensor(out=dst[:, k, :], in0=src[:, k, :],
                                             scalar=nscale[:, k, which:which + 1], in1=rstd[:, 0:width],
                                             op0=ALU.mult, op1=ALU.mult).then_inc(n_ready, 1)

            def time_steps(call, t0, n):
                x, e, z, q, p = (v[:, t0:t0 + n, :] for v in (dt, dt_y, dt_z, dt_q, dt_s))
                bias = dt_bias.unsqueeze(1).to_broadcast([128, n, 32])
                dve.wait_ge(s["dt_mm"], call)
                dve.tensor_tensor(x, psum[:, 4, t0 * 32:(t0 + n) * 32].rearrange("p (t h) -> p t h", h=32),
                                  bias, ALU.add)
                dve.drain()
                dve.scalar_tensor_tensor(out=e, in0=x, scalar=-1.0, in1=x, op0=ALU.mult, op1=ALU.min)\
                   .then_inc(s["dt_abs"], 1)
                dve.wait_ge(s["dt_exp"], call)
                dve.tensor_scalar(z, e, 2.0, None, ALU.add)
                dve.drain()
                dve.reciprocal(z, z)
                dve.drain()
                dve.tensor_tensor(z, z, e, ALU.mult)
                dve.drain()
                dve.tensor_tensor(q, z, z, ALU.mult)
                dve.memset(p, 1.0 / 19)
                for c in range(17, 0, -2):
                    dve.drain()
                    dve.tensor_tensor(p, p, q, ALU.mult)
                    dve.drain()
                    dve.tensor_scalar(p, p, 1.0 / c, None, ALU.add)
                dve.drain()
                dve.scalar_tensor_tensor(out=p, in0=p, scalar=2.0, in1=z, op0=ALU.mult, op1=ALU.mult)
                dve.drain()
                dve.scalar_tensor_tensor(out=x, in0=x, scalar=0.0, in1=p, op0=ALU.max, op1=ALU.add)
                dve.drain()
                dve.tensor_tensor(dta[:, t0:t0 + n, :], x, a_neg.unsqueeze(1).to_broadcast([128, n, 32]),
                                  ALU.mult).then_inc(s["dt_ok"], 1)

            def scan_units(pair0, n, pad, width):
                with dve.Fori(0, n) as i:
                    for side in range(2):
                        dve.wait_ge(bank_free[side], i + pair0 + 2)
                        o = cv[:, side, 0:width]
                        w = [params[:, bass.ds(i * 2 + (PCW + 16 * c + side), 1)] for c in range(3)]
                        dve.tensor_scalar(o, pad[:, side, 0:width], w[0], None, ALU.mult)
                        for c in (1, 2):
                            dve.drain()
                            last = dve.scalar_tensor_tensor(out=o, in0=pad[:, side, c:c + width], scalar=w[c],
                                                            in1=o, op0=ALU.mult, op1=ALU.add)
                        last.then_inc(s["conv_done"], 1)

            def decays(call, t0, n):
                cum = psum[:, 5, t0 * 64:(t0 + n) * 64].rearrange("p (t h) -> p t h", h=64)
                dve.wait_ge(s["cum_done"], call)
                dve.tensor_scalar(nacum[:, t0:t0 + n, :], cum[:, :, 0:32], -1.0, None, ALU.mult)
                dve.tensor_copy(c_dec[:, t0:t0 + n, :], cum[:, :, 32:64])
                dve.drain()
                dve.tensor_tensor(w_end[:, t0:t0 + n, :], nacum[:, t0:t0 + n, :], c_dec[:, t0:t0 + n, :],
                                  ALU.add).then_inc(s["ac_ready"], 1)
                dve.wait_ge(s["w_ready2"], call)
                dve.tensor_tensor(w_end[:, t0:t0 + n, :], w_end[:, t0:t0 + n, :], dt[:, t0:t0 + n, :], ALU.mult)
                dve.drain()

            def heads(v):
                return v.rearrange("p (h d) -> p h d", d=64)

            def states(k0, some, tr):
                dve.wait_ge(s["tr_used"], tr)
                def weigh(k):
                    way, t, _, _ = some[k - k0]
                    if k >= 2:
                        dve.wait_ge(s["st_done"], k - 1)
                    w = w_end[:, t, H * way:H * way + H].unsqueeze(2).to_broadcast([128, H, 64])
                    dve.tensor_tensor(heads(xw[:, k % 2, :]), heads(x_tok[:, t % NT, :]), w, ALU.mult)\
                       .then_inc(s["xw_ready"], 1)

                weigh(k0)
                for k, (way, t, a, b) in enumerate(some, k0):
                    if k + 1 < k0 + len(some):
                        weigh(k + 1)
                    old, new = state[way][:, a, :], state[way][:, b, :]
                    dec = c_dec[:, t, H * way:H * way + H].unsqueeze(2).to_broadcast([128, H, 64])
                    dve.tensor_tensor(heads(new), heads(old), dec, ALU.mult)
                    dve.wait_ge(s["st_done"], k + 1)
                    dve.drain()
                    b0 = st_banks(k)[0]
                    dve.tensor_tensor(new, new, psum[:, b0:b0 + 2, :].rearrange("p a b -> p (a b)"), ALU.add)\
                       .then_inc(s["st_used"], 1)
                    dve.drain()

            rms(c_in, xm_c, C, 1, s["stdc_ready"], s["nc_ready"])
            time_steps(1, NT, NC)
            scan_units(CTX, 6, pad_c, C)
            decays(1, NT, NC)
            dve.wait_ge(s["consts"], 1)
            states(0, steps, 3 * NC)
            rms(res, xm, T, 0, s["stdl_ready"], s["nl_ready"])
            time_steps(2, 0, NT)
            scan_units(SCAN, 8, pad_l, T)
            decays(2, 0, NT)
            states(4, steps_l, 3 * NC + 3 * NT)

            def masked(n):
                b = n % 2
                dve.wait_ge(s["bc_done"], n + 1)
                if n >= 2:
                    dve.wait_ge(s["y_done"], n - 1)
                for m, at, mask in ((df, 2 + 3 * b, mask_f), (db, 3 + 3 * b, mask_b)):
                    last = dve.tensor_tensor(m[:, b, :, :], psum[:, at, :].rearrange("p (h i) -> p h i", i=CH),
                                             mask.unsqueeze(1).to_broadcast([128, 4, CH]), ALU.add)
                last.then_inc(s["tm_ready"], 1)

            def combine(n):
                c, g, b = n // G, n % G, n % 2
                m = df[:, b, :, :]
                dve.wait_ge(s["ff_ready"], n + 1)
                dve.tensor_tensor(m, m, dt[:, c, 4 * g:4 * g + 4].unsqueeze(2).to_broadcast([128, 4, CH]),
                                  ALU.mult)
                dve.wait_ge(s["pb_ready"], n + 1)
                dve.drain()
                dve.tensor_tensor(m, m, db[:, b, :, :], ALU.add)
                dve.drain()
                dve.tensor_tensor(m, m, psum[:, 4 + 3 * b, 0:CH].unsqueeze(1).to_broadcast([128, 4, CH]),
                                  ALU.mult).then_inc(s["m_ready"], 1)

            def skip(n):
                c, g, b = n // G, n % G, n % 2
                chunk = slice(c * CH, (c + 1) * CH)
                dve.wait_ge(s["y_done"], n + 1)
                for t in range(2):
                    k = 2 * g + t
                    last = dve.scalar_tensor_tensor(out=y[:, k, chunk], in0=xbc[:, k, chunk],
                                                    scalar=d_skip[:, k:k + 1],
                                                    in1=psum[:, b, t * CH:(t + 1) * CH],
                                                    op0=ALU.mult, op1=ALU.add)
                last.then_inc(s["y_used"], 1)

            masked(0)
            for n in range(NT * G):
                if n + 1 < NT * G:
                    masked(n + 1)
                combine(n)
                if n:
                    skip(n - 1)
            skip(NT * G - 1)
            dve.wait_ge(s["v_gelu"], 1)
            dve.tensor_reduce(v_sum, v_tok, AX.X, ALU.add)
            dve.drain()
            dve.tensor_scalar(v_sum, v_sum, 1.0 / 1024, None, ALU.mult)
            dve.drain()
            for t in range(NT):
                last = dve.tensor_scalar(v_tok[:, t, :], v_tok[:, t, :], v_sum[:, t:t + 1], None, ALU.subtract)
            last.then_inc(s["v_mean"], 1)
            dve.wait_ge(s["v_std"], 1)
            dve.reciprocal(v_var, v_var)
            dve.wait_ge(s["ln_in"], 48)
            dve.drain()
            for t in range(NT):
                dve.scalar_tensor_tensor(out=v_tok[:, t, :], in0=v_tok[:, t, :], scalar=v_var[:, t:t + 1],
                                         in1=ln_w, op0=ALU.mult, op1=ALU.mult)
            dve.drain()
            dve.tensor_tensor(v_tok, v_tok, ln_b.unsqueeze(1).to_broadcast([128, NT, 1024]), ALU.add)\
               .then_inc(s["v_ok"], 1)
            with dve.Fori(0, 4) as i:
                for side in range(2):
                    dve.wait_ge(bank_free[side], i + ZP + 2)
                    tile = y[:, bass.ds(i * 2 + side, 1), :].rearrange("p a b -> p (a b)")
                    dve.tensor_tensor(tile, tile, z_s[:, side, :], ALU.mult).then_inc(s["z_ok"], 1)
            for g in range(8):
                dve.wait_ge(s["mix_done"], g + 1)
                bias = bs_bc[:, g * CH:(g + 1) * CH].unsqueeze(1).to_broadcast([128, NT, CH])
                dve.tensor_tensor(mixed[:, g % 2, :].rearrange("p (c i) -> p c i", i=CH),
                                  psum[:, 4 + g % 2, :].rearrange("p (c i) -> p c i", i=CH), bias, ALU.add)
                dve.drain()
                dve.tensor_tensor(sgu[:, g, :], mixed[:, g % 2, :], uT[:, g, :], ALU.mult).then_inc(s["mix_used"], 1)
            for q in range(4):
                dve.wait_ge(s["gstd"], q + 1)
                r = (rs_y if q < 2 else rs_y2)[:, q % 2, :]
                dve.reciprocal(r, r)
                dve.drain()
                for t in range(2):
                    k = 2 * q + t
                    dve.scalar_tensor_tensor(out=y[:, k, :], in0=y[:, k, :], scalar=par(PSN + k), in1=r,
                                             op0=ALU.mult, op1=ALU.mult).then_inc(s["y_ok"], 1)
            dve.drain()
            with dve.Fori(0, 8) as i:
                dve.wait_ge(bank_free[1], i + MERGE + 2)
                dve.tensor_tensor(ga_s, ga_s, bank(0), ALU.mult)
                dve.tensor_tensor(gb_s, gb_s, bank(2), ALU.mult)
                dve.drain()
                dve.tensor_tensor(merged[:, bass.ds(i, 1), :].rearrange("p a b -> p (a b)"), ga_s, gb_s,
                                  ALU.add).then_inc(bank_free[0], 1)
            with dve.Fori(0, 4) as i:
                for side in range(2):
                    dve.wait_ge(unit_done, (i + WO) * 2 + side + 3)
                    tile = res[:, bass.ds(i * 2 + side, 1), :].rearrange("p a b -> p (a b)")
                    dve.scalar_tensor_tensor(out=tile, in0=bank(side),
                                             scalar=mod[:, bass.ds(i * 2 + (16 + side), 1), 0:1]
                                             .rearrange("p a b -> p (a b)"), in1=tile,
                                             op0=ALU.mult, op1=ALU.add).then_inc(bank_free[side], 1)


def experts_program(nc, d, mem):
    f32 = mybir.dt.float32
    ALU, ACT, AX = mybir.AluOpType, mybir.ActivationFunctionType, mybir.AxisListType
    KT, T, NT, E, CAP, D = 8, 512, 4, 16, 64, 1024
    PAIRS, SLOTS = E // 2, 8

    ctx = ExitStack()
    with ctx:
        arena, psum = mem["arena"], mem["psum"]
        cursor = [0]

        def place(*shape):
            size = int(np.prod(shape))
            v = arena[:, cursor[0]:cursor[0] + size]
            cursor[0] += size
            assert cursor[0] <= mem["size"], cursor[0]
            if len(shape) == 2:
                return v.rearrange("p (a b) -> p a b", b=shape[1])
            if len(shape) == 3:
                return v.rearrange("p (a b c) -> p a b c", b=shape[1], c=shape[2])
            return v

        res = place(KT, T)
        ident = place(128)
        mod = place(49, 2)[:, 1:, :]
        params = place(160)
        onesD, eps6 = place(128), place(1)
        nscale = place(KT)
        rstd = place(T)
        xf = place(KT, T)
        xf_tok = place(NT, D)
        one_hot = place(NT, E * CAP)
        scatter = place(PAIRS, T)
        squares = scatter
        y = place(PAIRS, D)
        ring = [place(2, D) for _ in range(SLOTS)]
        xg = place(KT, 128)
        hid = place(D)
        hidT = place(KT, 128)
        w_router = place(KT, E)
        aff = place(NT, E)
        amax, asum = place(NT), place(NT)
        slot_tok = place(NT, E)
        slot_iota = place(CAP)
        slot_of_part = place(1)
        gate = place(PAIRS)
        junk = hid[:, 0:T]
        wide = y.rearrange("p a b -> p (a b)")[0:E, :]
        aff_row, left, taken, pos, ones_row = (wide[:, i * T:(i + 1) * T] for i in range(5))
        top8 = wide[:, 5 * T:5 * T + 8]
        rows_at = place(2, T)
        aff_rows, slot_rows = rows_at[0:E, 0, :], rows_at[0:E, 1, :]
        pair_rows = place(PAIRS, 128)[0:E]
        out_tok = one_hot

        s = {n: mem["sem"]("e_" + n) for n in (
            "consts const_in sq_ready var_done std_ready n_ready xf_ready logit_done aff_sub aff_exp "
            "aff_ok affT_done slot_ok slotT_done hot_ok tok_tr tok_ok "
            "unit_used gather_done xg_act xg_dve silu_ok hid_ok hT_done hT_act hT_dve rows_done scat_ok "
            "y_free sc_done res_ok fsq_ready fvar_done fstd fn_ok out_tr out_ok out_done").split()}
        w_ready = [mem["sem"](f"e_w_ready{i}") for i in range(SLOTS)]

        block = ctx.enter_context(nc.Block())

        @block.sync
        def _(sp):
            sp.dma_start(w_router, d["router_w_2"][0].rearrange("(k p) e -> p k e", p=128))\
              .then_inc(s["const_in"], 16)
            sp.dma_start(slot_iota, d["slot_iota"].partition_broadcast(128)).then_inc(s["const_in"], 16)
            sp.dma_start(slot_of_part, d["slot_of_partition"]).then_inc(s["const_in"], 16)
            sp.dma_start(pair_rows, d["pair_selector"]).then_inc(s["const_in"], 16)
            with sp.Fori(0, PAIRS) as q:
                for u in range(3 * KT):
                    name, k = ("w_gate_2", "w_up_2", "w_down_2")[u // KT], u % KT
                    sp.wait_ge(s["unit_used"], q * (3 * KT) + (u + 1))
                    src = d[name][0, bass.ds(q * 2, 2), k * 128:(k + 1) * 128, :]
                    sp.dma_start(ring[u % SLOTS], src.rearrange("e p c -> p e c"))\
                      .then_inc(w_ready[u % SLOTS], 16)
            for t in range(NT):
                sp.wait_ge(s["out_ok"], 2 * t + 2)
                sp.dma_start(d["out"][0, t * 128:(t + 1) * 128, :], out_tok[:, t, :]).then_inc(s["out_done"], 16)
            sp.wait_ge(s["out_done"], 16 * NT)

        @block.gpsimd
        def _(pool):
            pool.memset(onesD, 1.0 / 1024)
            pool.memset(ones_row, 1.0)
            pool.memset(eps6, 1e-6)
            pool.drain()
            pool.sem_inc(s["consts"], 1)

        @block.tensor
        def _(pe):
            pe.sem_inc(s["unit_used"], SLOTS)
            pe.sem_inc(s["y_free"], 1)
            pe.wait_ge(s["consts"], 1)
            for k in range(KT):
                pe.wait_ge(s["sq_ready"], k + 1)
                mm = pe.matmul(psum[:, 5, :], onesD, squares[:, k, :], start=(k == 0), stop=(k == KT - 1))
            mm.then_inc(s["var_done"], 1)
            pe.wait_ge(s["xf_ready"], KT)
            pe.wait_ge(s["const_in"], 64)
            for t in range(NT):
                for k in range(KT):
                    mm = pe.matmul(psum[:, 4, t * E:(t + 1) * E], xf[:, k, t * 128:(t + 1) * 128],
                                   w_router[:, k, :], start=(k == 0), stop=(k == KT - 1))
            mm.then_inc(s["logit_done"], 1)
            for r in range(2 * NT):
                if r >= 2:
                    pe.wait_ge(s["tok_ok"], r - 1)
                for k in range(4):
                    mm = pe.transpose(psum[:, 6 + r % 2, k * 128:(k + 1) * 128],
                                      xf[:, 4 * (r % 2) + k, (r // 2) * 128:(r // 2 + 1) * 128], ident)
                mm.then_inc(s["tok_tr"], 1)
            pe.wait_ge(s["aff_ok"], 1)
            for t in range(NT):
                mm = pe.transpose(psum[0:E, 0, t * 128:(t + 1) * 128], aff[:, t, :], ident)
            mm.then_inc(s["affT_done"], 1)
            pe.wait_ge(s["slot_ok"], 1)
            for t in range(NT):
                mm = pe.transpose(psum[:, 1, t * E:(t + 1) * E], slot_rows[:, t * 128:(t + 1) * 128],
                                  ident[0:E, 0:E])
            mm.then_inc(s["slotT_done"], 1)

            for q in range(PAIRS):
                if q >= 2:
                    pe.wait_ge(s["scat_ok"], q - 1)
                elif q:
                    pe.wait_ge(s["tok_ok"], 2 * NT)
                b = 4 if q % 2 == 0 else 2
                pe.matmul(psum[:, b, :], pair_rows[:, q, :], slot_rows, start=True, stop=True)
                pe.matmul(psum[:, b + 1, :], pair_rows[:, q, :], aff_rows, start=True, stop=True)\
                  .then_inc(s["rows_done"], 1)

            def gather(q):
                for k in range(KT):
                    for t in range(NT):
                        mm = pe.matmul(psum[:, 4 + k // 4, (k % 4) * 128:(k % 4 + 1) * 128],
                                       xf_tok[:, t, k * 128:(k + 1) * 128],
                                       one_hot[:, t, bass.ds(q * 128, 128)],
                                       start=(t == 0), stop=(t == NT - 1))
                mm.then_inc(s["gather_done"], 1)

            def both_experts(bank0, x, u, k, start, stop):
                for half in range(2):
                    for e in range(2):
                        mm = pe.matmul(psum[64 * e:64 * e + 64, bank0 + half, :], x[:, k, 64 * e:64 * e + 64],
                                       ring[u % SLOTS][:, e, half * 512:(half + 1) * 512],
                                       start=start, stop=stop)
                mm.then_inc(s["unit_used"], 1)

            def pair(q, more):
                pe.wait_ge(s["xg_act"], q + 1)
                pe.wait_ge(s["xg_dve"], q + 1)
                for u in range(2 * KT):
                    pe.wait_ge(w_ready[u % SLOTS], q * 48 + (u // SLOTS) * 16 + 16)
                    k = u % KT
                    both_experts(2 * (u // KT), xg, u, k, k == 0, k == KT - 1)
                if more:
                    gather(q + 1)
                pe.wait_ge(s["hid_ok"], q + 1)
                for k in range(KT):
                    mm = pe.transpose(psum[:, k // 4, (k % 4) * 128:(k % 4 + 1) * 128],
                                      hid[:, k * 128:(k + 1) * 128], ident)
                mm.then_inc(s["hT_done"], 1)
                pe.wait_ge(s["hT_act"], q + 1)
                pe.wait_ge(s["hT_dve"], q + 1)
                pe.wait_ge(s["y_free"], q + 1)
                for u in range(2 * KT, 3 * KT):
                    pe.wait_ge(w_ready[u % SLOTS], q * 48 + 48)
                    k = u % KT
                    both_experts(6, hidT, u, k, k == 0, k == KT - 1)

            pe.wait_ge(s["hot_ok"], 1)
            pe.wait_ge(s["scat_ok"], PAIRS)
            gather(0)
            with pe.Fori(0, PAIRS - 1) as q:
                pair(q, 1)
            pair(PAIRS - 1, 0)
            pe.wait_ge(s["y_free"], PAIRS + 1)
            for m in range(KT):
                if m >= 2:
                    pe.wait_ge(s["res_ok"], m - 1)
                for q in range(PAIRS):
                    mm = pe.matmul(psum[:, m % 2, :], y[:, q, m * 128:(m + 1) * 128], scatter[:, q, :],
                                   start=(q == 0), stop=(q == PAIRS - 1))
                mm.then_inc(s["sc_done"], 1)
            for k in range(KT):
                pe.wait_ge(s["fsq_ready"], k + 1)
                mm = pe.matmul(psum[:, 5, :], onesD, xf[:, k, :], start=(k == 0), stop=(k == KT - 1))
            mm.then_inc(s["fvar_done"], 1)
            pe.wait_ge(s["fn_ok"], KT)
            for r in range(2 * NT):
                if r >= 2:
                    pe.wait_ge(s["out_ok"], r - 1)
                for k in range(4):
                    mm = pe.transpose(psum[:, 6 + r % 2, k * 128:(k + 1) * 128],
                                      res[:, 4 * (r % 2) + k, (r // 2) * 128:(r // 2 + 1) * 128], ident)
                mm.then_inc(s["out_tr"], 1)

        @block.scalar
        def _(act):
            for k in range(KT):
                act.activation(squares[:, k, :], res[:, k, :], ACT.Square).then_inc(s["sq_ready"], 1)
            act.wait_ge(s["consts"], 1)
            act.wait_ge(s["var_done"], 1)
            act.activation(rstd, psum[:, 5, :], ACT.Sqrt, bias=eps6).then_inc(s["std_ready"], 1)
            for k in range(KT):
                act.wait_ge(s["n_ready"], k + 1)
                act.activation(xf[:, k, :], xf[:, k, :], ACT.Identity, bias=mod[:, 24 + k, 0:1])\
                   .then_inc(s["xf_ready"], 1)
            act.wait_ge(s["aff_sub"], 1)
            act.activation(aff, aff, ACT.Exp).then_inc(s["aff_exp"], 1)
            for r in range(2 * NT):
                act.wait_ge(s["tok_tr"], r + 1)
                act.copy(xf_tok[:, r // 2, (r % 2) * 512:(r % 2 + 1) * 512], psum[:, 6 + r % 2, :])\
                   .then_inc(s["tok_ok"], 1)

            def halves(v):
                return v.rearrange("p k c -> p (k c)")

            act.wait_ge(s["gather_done"], 1)
            act.copy(halves(xg[:, 0:4, :]), psum[:, 4, :]).then_inc(s["xg_act"], 1)

            def pair(q, more):
                act.wait_ge(s["unit_used"], q * 24 + 24)
                act.activation(hid, psum[:, 0:2, :].rearrange("p b c -> p (b c)"), ACT.Silu)\
                   .then_inc(s["silu_ok"], 1)
                if more:
                    act.wait_ge(s["gather_done"], q + 2)
                    act.copy(halves(xg[:, 0:4, :]), psum[:, 4, :]).then_inc(s["xg_act"], 1)
                act.wait_ge(s["hT_done"], q + 1)
                act.copy(halves(hidT[:, 0:4, :]), psum[:, 0, :]).then_inc(s["hT_act"], 1)
                act.wait_ge(s["unit_used"], q * 24 + 32)
                act.activation(y[:, bass.ds(q, 1), :].rearrange("p a b -> p (a b)"),
                               psum[:, 6:8, :].rearrange("p b c -> p (b c)"), ACT.Copy,
                               scale=gate[:, bass.ds(q, 1)]).then_inc(s["y_free"], 1)

            with act.Fori(0, PAIRS - 1) as q:
                pair(q, 1)
            pair(PAIRS - 1, 0)
            for k in range(KT):
                act.wait_ge(s["res_ok"], k + 1)
                act.activation(xf[:, k, :], res[:, k, :], ACT.Square).then_inc(s["fsq_ready"], 1)
            act.wait_ge(s["fvar_done"], 1)
            act.activation(rstd, psum[:, 5, :], ACT.Sqrt, bias=eps6).then_inc(s["fstd"], 1)
            for r in range(2 * NT):
                act.wait_ge(s["out_tr"], r + 1)
                act.copy(out_tok[:, r // 2, (r % 2) * 512:(r % 2 + 1) * 512], psum[:, 6 + r % 2, :])\
                   .then_inc(s["out_ok"], 1)

        @block.vector
        def _(dve):
            scale2 = mod[:, 32:40, 0:1].rearrange("p k w -> p (k w)")
            dve.scalar_tensor_tensor(out=nscale, in0=scale2, scalar=1.0, in1=params[:, 72:80],
                                     op0=ALU.add, op1=ALU.mult)
            dve.wait_ge(s["std_ready"], 1)
            dve.reciprocal(rstd, rstd)
            dve.drain()
            for k in range(KT):
                dve.scalar_tensor_tensor(out=xf[:, k, :], in0=res[:, k, :], scalar=nscale[:, k:k + 1],
                                         in1=rstd, op0=ALU.mult, op1=ALU.mult).then_inc(s["n_ready"], 1)
            dve.wait_ge(s["logit_done"], 1)
            logits = psum[:, 4, 0:NT * E].rearrange("p (t e) -> p t e", e=E)
            dve.tensor_reduce(amax, logits, AX.X, ALU.max)
            dve.drain()
            dve.tensor_tensor(aff, logits, amax.unsqueeze(2).to_broadcast([128, NT, E]), ALU.subtract)\
               .then_inc(s["aff_sub"], 1)
            dve.wait_ge(s["aff_exp"], 1)
            dve.tensor_reduce(asum, aff, AX.X, ALU.add)
            dve.drain()
            dve.reciprocal(asum, asum)
            dve.drain()
            dve.tensor_tensor(aff, aff, asum.unsqueeze(2).to_broadcast([128, NT, E]), ALU.mult)\
               .then_inc(s["aff_ok"], 1)
            dve.wait_ge(s["affT_done"], 1)
            dve.tensor_copy(aff_rows, psum[0:E, 0, :])
            dve.tensor_copy(left, psum[0:E, 0, :])
            for _ in range(CAP // 8):
                dve.drain()
                dve.max(top8, left)
                dve.drain()
                dve.match_replace(left, top8, left, -1.0)
            dve.drain()
            dve.tensor_scalar(taken, left, 0.0, None, ALU.is_lt)
            dve.drain()
            dve.wait_ge(s["consts"], 1)
            dve.tensor_tensor_scan(pos, ones_row, taken, 0.0, ALU.mult, ALU.add)
            dve.drain()
            dve.tensor_tensor(pos, pos, taken, ALU.mult)
            dve.drain()
            dve.tensor_scalar(slot_rows, pos, -1.0, None, ALU.add).then_inc(s["slot_ok"], 1)
            dve.wait_ge(s["const_in"], 64)
            dve.wait_ge(s["slotT_done"], 1)
            dve.tensor_copy(slot_tok, psum[:, 1, 0:NT * E].rearrange("p (t e) -> p t e", e=E))
            dve.drain()
            for t in range(NT):
                last = dve.tensor_tensor(one_hot[:, t, :].rearrange("p (e c) -> p e c", c=CAP),
                                         slot_iota.unsqueeze(1).to_broadcast([128, E, CAP]),
                                         slot_tok[:, t, :].unsqueeze(2).to_broadcast([128, E, CAP]),
                                         ALU.is_equal)
            last.then_inc(s["hot_ok"], 1)
            for q in range(PAIRS):
                dve.wait_ge(s["rows_done"], q + 1)
                b = 4 if q % 2 == 0 else 2
                dve.tensor_scalar(scatter[:, q, :], psum[:, b, :], slot_of_part, None, ALU.is_equal)
                dve.drain()
                dve.scalar_tensor_tensor(out=junk, in0=psum[:, b + 1, :], scalar=1.0, in1=scatter[:, q, :],
                                         op0=ALU.mult, op1=ALU.mult, accum_out=gate[:, q:q + 1])
                dve.drain()
                dve.sem_inc(s["scat_ok"], 1)

            def halves(v):
                return v.rearrange("p k c -> p (k c)")

            dve.wait_ge(s["gather_done"], 1)
            dve.tensor_copy(halves(xg[:, 4:8, :]), psum[:, 5, :]).then_inc(s["xg_dve"], 1)

            def pair(q, more):
                dve.wait_ge(s["silu_ok"], q + 1)
                dve.tensor_tensor(hid, hid, psum[:, 2:4, :].rearrange("p b c -> p (b c)"), ALU.mult)\
                   .then_inc(s["hid_ok"], 1)
                if more:
                    dve.wait_ge(s["gather_done"], q + 2)
                    dve.tensor_copy(halves(xg[:, 4:8, :]), psum[:, 5, :]).then_inc(s["xg_dve"], 1)
                dve.wait_ge(s["hT_done"], q + 1)
                dve.tensor_copy(halves(hidT[:, 4:8, :]), psum[:, 1, :]).then_inc(s["hT_dve"], 1)

            with dve.Fori(0, PAIRS - 1) as q:
                pair(q, 1)
            pair(PAIRS - 1, 0)
            for m in range(KT):
                dve.wait_ge(s["sc_done"], m + 1)
                dve.scalar_tensor_tensor(out=res[:, m, :], in0=psum[:, m % 2, :], scalar=mod[:, 40 + m, 0:1],
                                         in1=res[:, m, :], op0=ALU.mult, op1=ALU.add)\
                   .then_inc(s["res_ok"], 1)
            dve.wait_ge(s["fstd"], 1)
            dve.reciprocal(rstd, rstd)
            dve.drain()
            for k in range(KT):
                dve.scalar_tensor_tensor(out=res[:, k, :], in0=res[:, k, :], scalar=params[:, 104 + k:105 + k],
                                         in1=rstd, op0=ALU.mult, op1=ALU.mult).then_inc(s["fn_ok"], 1)


_INS = ("x rel_bias ln_g ln_b ffn_w_gate ffn_w_up ffn_w_down w_in conv_dw_w conv_dw_b conv_ln_g conv_ln_b "
        "lru_conv_w lru_conv_b lru_wa lru_ba lru_wx lru_bx lru_lambda attn_sinks w_out c_2 ctx_2 c_ctx_2 "
        "ada_w_2 ada_b_2 norm1_w_2 norm2_w_2 w_in_2 conv_w_2 conv_b_2 dt_bias_2 a_log_2 d_skip_2 "
        "ssd_norm_w_2 sgu_ln_w_2 sgu_ln_b_2 w_s_2 b_s_2 w_pa_2 w_pb_2 w_o_2 router_w_2 w_gate_2 w_up_2 "
        "w_down_2 final_norm_w_2").split()


def shape_constants():
    dist = 127 - np.arange(128)
    far = 16 + (np.log(np.maximum(dist, 1) / 16) / np.log(8) * 16).astype(int)
    bucket = np.where(dist < 16, dist, np.minimum(far, 31))
    onehot = (np.arange(32)[:, None] == bucket[None, :]).astype(np.float32)
    part = np.arange(128)
    selector = (np.arange(16)[:, None, None] == 2 * np.arange(8)[None, :, None] + part // 64)
    return {"bucket_onehot": onehot, "slot_iota": np.arange(64, dtype=np.float32),
            "slot_of_partition": (part % 64).astype(np.float32)[:, None],
            "pair_selector": selector.astype(np.float32)}


def build(nc, d):
    f32 = mybir.dt.float32
    size = 53000
    scratch = nc.dram_tensor("band_scratch", (8, 128, 384), f32, kind="Internal").ap()
    with ExitStack() as ctx:
        mem = {"arena": ctx.enter_context(nc.sbuf_tensor("arena", [128, size], f32)),
               "psum": ctx.enter_context(nc.psum_tensor("psum", [128, 8, 512], f32)),
               "scratch": scratch, "size": size}
        for program in (first_block_program, second_mixer_program, experts_program):
            sems = []

            def sem(name):
                sems.append(nc.alloc_semaphore(name))
                return sems[-1]

            mem["sem"] = sem
            program(nc, d, mem)
            nc.clear_and_free_semaphores(sems)
            nc.all_engine_barrier()


def kernel(**inputs):
    import concourse.bacc as bacc
    from concourse.bass_utils import run_bass_kernel_spmd

    nc = bacc.Bacc("TRN2", target_bir_lowering=False, num_devices=1)
    arrays, d = {}, {}
    for name, a in [(n, inputs[n]) for n in _INS] + list(shape_constants().items()):
        a = np.ascontiguousarray(a)
        arrays[f"in_{name}_dram"] = a
        d[name] = nc.dram_tensor(f"in_{name}_dram", a.shape, mybir.dt.from_np(a.dtype),
                                 kind="ExternalInput").ap()
    d["out"] = nc.dram_tensor("out_0_dram", (1, 512, 1024), mybir.dt.float32, kind="ExternalOutput").ap()
    build(nc, d)
    r = run_bass_kernel_spmd(nc, [arrays], core_ids=[0])
    return r.results[0]["out_0_dram"]
```

```python
import concourse.bass as bass
from concourse import mybir
from contextlib import ExitStack
import numpy as np


def first_block_program(nc, d, mem):
    f32 = mybir.dt.float32
    ALU, ACT, AX = mybir.AluOpType, mybir.ActivationFunctionType, mybir.AxisListType
    ALPHA = (2.0 * 2) ** 0.25
    L, KT, FT, T = 2, 8, 22, 512
    HEADS, WIN = 8, 128

    ctx = ExitStack()
    with ctx:
        arena, psum, scratch = mem["arena"], mem["psum"], mem["scratch"]
        cursor = [0]

        def place(*shape):
            size = int(np.prod(shape))
            v = arena[:, cursor[0]:cursor[0] + size]
            cursor[0] += size
            assert cursor[0] <= mem["size"], cursor[0]
            if len(shape) == 2:
                return v.rearrange("p (a b) -> p a b", b=shape[1])
            if len(shape) == 3:
                return v.rearrange("p (a b c) -> p a b c", b=shape[1], c=shape[2])
            return v

        def sem(name):
            return mem["sem"](name)

        xT = place(KT, T)
        ident = place(128)
        mod = place(49, 2)
        params2 = place(160)
        rT = place(KT, T)
        ring = [place(FT * 128) for _ in range(2)]
        onesD = place(128)
        ones256 = place(128)
        CL = 136
        params = place(L * CL)
        cur = place(CL)
        lam_y, lam_z, lam_q, lam_s = place(L, 2), place(L, 2), place(L, 2), place(L, 2)
        sinks = place(L * HEADS)
        gate_w = place(4, 128)
        band = place(HEADS, 2 * WIN)
        acc = place(T)
        std = place(T)
        sg = place(2, T)
        eps_ln, eps_conv = place(1), place(1)
        silu_c = place(2, KT)
        ada_slot = place(KT, 128)
        ada_prod = place(2, KT, 128)
        ada_acc = place(2, 128)
        ones_col = place(1)
        mx, nmx, esink, esum, rsum = (place(2, HEADS) for _ in range(5))
        hid_at = cursor[0]
        hid = place(FT, T)
        end = cursor[0]
        cursor[0] = hid_at
        cpad = place(2, 30 + T)
        lpad = place(2, 3 + T)
        gelu_b = place(2, T)
        qT = place(4, T)
        kT = place(T)
        v_tok = place(4, 128)
        xc = place(2, T)
        r_gate, i_gate, decay, mult = (place(2, T) for _ in range(4))
        conv = place(2, T)
        conv_sq = place(2, T)
        conv_rstd = place(T)
        yT = place(KT, T)
        prob = [place(HEADS, 2 * WIN) for _ in range(2)]
        probT = place(HEADS, 2, WIN)
        cursor[0] = max(cursor[0], end)
        x_tok = yT.rearrange("p a b -> p (a b)").rearrange("p (t n) -> p t n", n=KT * 128)
        rows = prob[0].rearrange("p a b -> p (a b)")[:, 0:768].rearrange("p (a b) -> p a b", b=128)
        onehot = prob[1].rearrange("p a b -> p (a b)")[:, 0:WIN]
        relb = prob[1].rearrange("p a b -> p (a b)")[:, WIN:WIN + HEADS]
        erow = prob[1].rearrange("p a b -> p (a b)")[:, 256:256 + 3 * WIN]

        def bank(b):
            return psum[:, b, :]

        LNG, LNB, CB, CG, CBB, LW, LB, BA, BX, LAM, CW, C8, NC8 = (
            0, 24, 48, 50, 52, 54, 62, 64, 66, 68, 70, 132, 134)

        def col(c):
            return cur[:, c:c + 1]

        x_in, rows_in, oh_in, sink_in, e_out, band_in = map(sem, (
            "x_in", "rows_in", "oh_in", "sink_in", "e_out", "band_in"))
        consts, x_tr, par_tr, par_ok, e_mm, e_ok, y_exp, y_in, lam_ok = map(sem, (
            "consts", "x_tr", "par_tr", "par_ok", "e_mm", "e_ok", "y_exp", "y_in", "lam_ok"))
        ada_in, ada_prods, ada_ready, ada_sum, silu_ok, par2_ok = map(sem, (
            "ada_in", "ada_prods", "ada_ready", "ada_sum", "silu_ok", "par2_ok"))
        w_ready = [sem("w_ready0"), sem("w_ready1")]
        bank_free = [sem("bank_free0"), sem("bank_free1")]
        unit_done, x_ready, silu_done = sem("unit_done"), sem("x_ready"), sem("silu_done")
        cur_ready, acc_taken = sem("cur_ready"), sem("acc_taken")
        acc_ready, mean_done, diff_ready, sq_ready, var_done, std_ready, norm_ready = map(sem, (
            "acc_ready", "mean_done", "diff_ready", "sq_ready", "var_done", "std_ready",
            "norm_ready"))
        gw_ready, gw_used, xc_ready, gate_mm, gates_ready, decay_ready, m2_ready, mult_ready = map(
            sem, ("gw_ready", "gw_used", "xc_ready", "gate_mm", "gates_ready", "decay_ready",
                  "m2_ready", "mult_ready"))
        conv_ready, cmean_done, cdiff, csq, cvar_done, cstd, cnorm, y_act, y_dve = map(sem, (
            "conv_ready", "cmean_done", "cdiff", "csq", "cvar_done", "cstd", "cnorm", "y_act",
            "y_dve"))
        s_done, s_used, max_ready, exp_ready, prob_ready, tr_done, pt_ready, o_done, o_used = map(
            sem, ("s_done", "s_used", "max_ready", "exp_ready", "prob_ready", "tr_done",
                  "pt_ready", "o_done", "o_used"))

        UP, DOWN, WIN_P, WOUT = FT // 2, KT // 2, 7, KT // 2
        AT_MIX = UP + DOWN
        AT_OUT = AT_MIX + WIN_P
        AT_FF2 = AT_OUT + WOUT
        PL = AT_FF2 + UP + DOWN
        MIX = [("a", 0), ("g", 0), ("a", 1), ("g", 1), ("xb", 0), ("xb", 1), ("gb", 0), ("gb", 1),
               ("k", 0), ("v", 0), ("q", 0), ("q", 1), ("q", 2), ("q", 3)]
        COLS = {"a": 0, "g": 256, "xb": 512, "gb": 768, "k": 1536, "v": 1664}

        block = ctx.enter_context(nc.Block())

        @block.sync
        def _(sp):
            sp.dma_start(x_tok, d["x"][0].rearrange("(t p) n -> p t n", p=128)).then_inc(x_in, 16)
            for l in range(L):
                at = 0
                for name in ("ln_g", "ln_b"):
                    sp.dma_start(rows[at:at + 24, 2 * l, :],
                                 d[name][l].rearrange("s (k p) -> (s k) p", p=128)).then_inc(rows_in, 16)
                    at += 24
                for name in ("conv_dw_b", "conv_ln_g", "conv_ln_b", "lru_conv_w", "lru_conv_b",
                             "lru_ba", "lru_bx", "lru_lambda"):
                    n = 8 if name == "lru_conv_w" else 2
                    src = (d[name][l].rearrange("s (k p) -> (s k) p", p=128) if n == 8
                           else d[name][l].rearrange("(k p) -> k p", p=128))
                    sp.dma_start(rows[at:at + n, 2 * l, :], src).then_inc(rows_in, 16)
                    at += n
                sp.dma_start(rows[0:62, 2 * l + 1, :],
                             d["conv_dw_w"][l].rearrange("s (k p) -> (s k) p", p=128)).then_inc(rows_in, 16)
            at = 0
            for name, n in (("c_2", 8), ("c_ctx_2", 8), ("ada_b_2", 48), ("norm1_w_2", 8), ("norm2_w_2", 8),
                            ("conv_b_2", 16), ("ssd_norm_w_2", 8), ("final_norm_w_2", 8)):
                v = d[name] if len(d[name].shape) == 1 else d[name][0]
                sp.dma_start(rows[at:at + n, 4, :], v.rearrange("(k p) -> k p", p=128)).then_inc(rows_in, 16)
                at += n
            sp.dma_start(rows[0:48, 5, :], d["conv_w_2"][0].rearrange("s (k p) -> (s k) p", p=128))\
              .then_inc(rows_in, 16)
            sp.dma_start(onehot[0:32, :], d["bucket_onehot"]).then_inc(oh_in, 16)
            sp.dma_start(relb[0:32, :], d["rel_bias"]).then_inc(oh_in, 16)
            sp.dma_start(sinks, d["attn_sinks"].rearrange("l h -> (l h)").partition_broadcast(128))\
              .then_inc(sink_in, 16)
            sp.wait_ge(e_ok, 1)
            sp.dma_start(scratch, erow[0:HEADS, :].unsqueeze(1).to_broadcast([HEADS, 128, 3 * WIN]))\
              .then_inc(e_out, 16)
            sp.wait_ge(e_out, 16)
            sp.dma_start(band, bass.AP(scratch.tensor, scratch.offset + WIN - 1,
                                       [[3 * WIN - 1, 128], [128 * 3 * WIN, HEADS], [1, 2 * WIN]]))\
              .then_inc(band_in, 16)

            def slot_free(pair, side):
                sp.wait_ge(unit_done, 2 * pair + side + 1)

            def tiles(w):
                return w.rearrange("(k p) c -> p k c", p=128)

            def ada_load(a):
                sp.wait_ge(ada_prods, a + 1)
                sp.dma_start(ada_slot, tiles(d["ada_w_2"][0, :, bass.ds(a * 128, 128)])).then_inc(ada_in, 16)

            def ffn_loads(l, s, at):
                with sp.Fori(0, UP) as i:
                    ada_load(l * 24 + s * 12 + i)
                    for side in range(2):
                        slot_free(at + i, side)
                        to = ring[side][:, 0:2 * KT * 128].rearrange("p (k c) -> p k c", c=128)
                        cols = bass.ds((i * 2 + side) * 128, 128)
                        sp.dma_start(to[:, 0:KT, :], tiles(d["ffn_w_gate"][l, s, :, cols]))\
                          .then_inc(w_ready[side], 16)
                        sp.dma_start(to[:, KT:, :], tiles(d["ffn_w_up"][l, s, :, cols]))\
                          .then_inc(w_ready[side], 16)
                ada_load(l * 24 + s * 12 + UP)
                with sp.Fori(0, DOWN) as i:
                    for side in range(2):
                        slot_free(at + UP + i, side)
                        to = ring[side].rearrange("p (k c) -> p k c", c=128)
                        cols = bass.ds((i * 2 + side) * 128, 128)
                        half = FT // 2
                        sp.dma_start(to[:, 0:half, :], tiles(d["ffn_w_down"][l, s, 0:half * 128, cols]))\
                          .then_inc(w_ready[side], 16)
                        sp.dma_start(to[:, half:, :], tiles(d["ffn_w_down"][l, s, half * 128:, cols]))\
                          .then_inc(w_ready[side], 16)

            sp.wait_ge(consts, 1)
            with sp.Fori(0, L) as l:
                sp.wait_ge(gw_used, l + 1)
                for a, name in enumerate(("lru_wa", "lru_wx")):
                    for half in range(2):
                        part = slice(64 * half, 64 * half + 64)
                        src = d[name][l].rearrange("(t f) i j -> f i t j", f=2)[half]
                        sp.dma_start(gate_w[part, 2 * a:2 * a + 2, part], src).then_inc(gw_ready, 16)
                ffn_loads(l, 0, l * PL)
                for n, (kind, t) in enumerate(MIX):
                    pair, side = l * PL + AT_MIX + n // 2, n % 2
                    slot_free(pair, side)
                    to = ring[side][:, 0:KT * 128].rearrange("p (k c) -> p k c", c=128)
                    if kind == "q":
                        for g in range(2):
                            c = 1024 + 64 * (t + 4 * g)
                            sp.dma_start(to[:, :, 64 * g:64 * g + 64], tiles(d["w_in"][l, :, c:c + 64]))\
                              .then_inc(w_ready[side], 16)
                    else:
                        c = COLS[kind] + 128 * t
                        for h in range(2):
                            sp.dma_start(to[:, 4 * h:4 * h + 4, :],
                                         tiles(d["w_in"][l, 512 * h:512 * h + 512, c:c + 128]))\
                              .then_inc(w_ready[side], 16)
                with sp.Fori(0, WOUT) as i:
                    for side in range(2):
                        slot_free(l * PL + AT_OUT + i, side)
                        to = ring[side][:, 0:KT * 128].rearrange("p (k c) -> p k c", c=128)
                        cols = bass.ds((i * 2 + side) * 128, 128)
                        sp.dma_start(to[:, 0:4, :], tiles(d["w_out"][l, 0:512, cols]))\
                          .then_inc(w_ready[side], 16)
                        for g in range(2):
                            src = d["w_out"][l, 512 + 256 * g:768 + 256 * g, cols]
                            sp.dma_start(to[64 * g:64 * g + 64, 4:8, :],
                                         src.rearrange("(j p) c -> p j c", p=64)).then_inc(w_ready[side], 16)
                ffn_loads(l, 1, l * PL + AT_FF2)

        @block.gpsimd
        def _(pool):
            pool.memset(gate_w, 0.0)
            pool.memset(onesD, 1.0 / 1024)
            pool.memset(ones256, 1.0 / 256)
            pool.memset(eps_ln, 1e-5 / ALPHA ** 2)
            pool.memset(eps_conv, 1e-5)
            pool.memset(ones_col, 1.0)
            pool.memset(ada_acc, 0.0)
            pool.memset(ident, 0.0)
            pool.drain()
            pool.affine_select(out=ident, in_=ident, compare_op=ALU.not_equal, fill=1.0, base=0,
                               pattern=[[-1, 128]], channel_multiplier=1)
            pool.drain()
            pool.memset(acc, 0.0).then_inc(consts, 1)
            pool.sem_inc(ada_prods, 1)
            pool.wait_ge(silu_ok, 1)

            def ada_products(a):
                pool.wait_ge(ada_in, a * 16 + 16)
                pool.wait_ge(ada_ready, a + 1)
                for w in range(2):
                    last = pool.tensor_tensor(ada_prod[:, w, :, :], ada_slot,
                                              silu_c[:, w, :].unsqueeze(2).to_broadcast([128, KT, 128]),
                                              ALU.mult)
                last.then_inc(ada_prods, 1)

            def ada_all(a0):
                with pool.Fori(0, UP) as i:
                    ada_products(a0 + i)
                ada_products(a0 + UP)

            def sum_tiles(pair0):
                with pool.Fori(0, KT // 2) as i:
                    for side in range(2):
                        pool.wait_ge(bank_free[side], pair0 + i + 2)
                        tile = rT[:, bass.ds(i * 2 + side, 1), :].rearrange("p a b -> p (a b)")
                        pool.tensor_tensor(acc, acc, tile, ALU.add)
                        pool.drain()

            with pool.Fori(0, L) as l:
                for n, at in enumerate((UP, AT_OUT, AT_FF2 + UP)):
                    if n != 1:
                        ada_all(l * 24 + 6 * n)
                    pool.wait_ge(bank_free[0], l * PL + at + 1)
                    pool.sem_inc(acc_taken, 1)
                    pool.memset(acc, 0.0)
                    pool.drain()
                    sum_tiles(l * PL + at)
                    pool.sem_inc(acc_ready, 1)

        @block.tensor
        def _(pe):
            pe.sem_inc(unit_done, 2)
            pe.sem_inc(bank_free[0], 1)
            pe.sem_inc(bank_free[1], 1)
            pe.sem_inc(gw_used, 1)
            pe.wait_ge(consts, 1)
            pe.wait_ge(x_in, 16)
            for k in range(KT):
                if k >= 2:
                    pe.wait_ge(x_ready, k - 1)
                for t in range(4):
                    mm = pe.transpose(bank(6 + k % 2)[:, t * 128:(t + 1) * 128],
                                      x_tok[:, t, k * 128:(k + 1) * 128], ident)
                mm.then_inc(x_tr, 1)
            pe.wait_ge(rows_in, 16 * (11 * L + 9))
            for l in range(L):
                pe.transpose(psum[:, 4, l * 132:l * 132 + 70], rows[0:70, 2 * l, :], ident[0:70, 0:70])
                mm = pe.transpose(psum[:, 4, l * 132 + 70:l * 132 + 132], rows[0:62, 2 * l + 1, :],
                                  ident[0:62, 0:62])
            pe.transpose(psum[:, 4, 264:376], rows[0:112, 4, :], ident[0:112, 0:112])
            mm = pe.transpose(psum[:, 4, 376:424], rows[0:48, 5, :], ident[0:48, 0:48])
            mm.then_inc(par_tr, 1)
            pe.wait_ge(oh_in, 32)
            pe.matmul(psum[0:HEADS, 5, 0:WIN], relb[0:32, :], onehot[0:32, :], start=True, stop=True)\
              .then_inc(e_mm, 1)

            def wait_unit(pair, side, extra):
                pe.wait_ge(w_ready[side], pair * 32 + extra + 32)
                pe.wait_ge(bank_free[side], pair + 1)

            def norm_stats(n):
                pe.wait_ge(acc_ready, n + 1)
                pe.matmul(bank(4), onesD, acc, start=True, stop=True).then_inc(mean_done, 1)
                for k in range(KT):
                    pe.wait_ge(sq_ready, n * KT + k + 1)
                    mm = pe.matmul(bank(5), onesD, xT[:, k, :], start=(k == 0), stop=(k == KT - 1))
                mm.then_inc(var_done, 1)

            def ada_column(a):
                pe.wait_ge(ada_ready, a + 1)
                pe.matmul(psum[:, 6, 0:1], ada_acc[:, 0, :], ones_col, start=True, stop=True)
                pe.matmul(psum[:, 6, 1:2], ada_acc[:, 1, :], ones_col, start=True, stop=True)\
                  .then_inc(ada_sum, 1)

            def ffn(l, s, at, extra):
                with pe.Fori(0, UP) as i:
                    ada_column(l * 24 + s * 12 + i)
                    for side in range(2):
                        wait_unit(at + i, side, extra)
                        for half in range(2):
                            for k in range(KT):
                                if side == 0 and half == 0:
                                    pe.wait_ge(x_ready, l * 24 + s * 16 + k + 1)
                                c = (half * KT + k) * 128
                                mm = pe.matmul(bank(side + 2 * half), ring[side][:, c:c + 128],
                                               xT[:, k, :], start=(k == 0), stop=(k == KT - 1))
                        mm.then_inc(unit_done, 1)
                ada_column(l * 24 + s * 12 + UP)
                with pe.Fori(0, DOWN) as i:
                    for side in range(2):
                        wait_unit(at + UP + i, side, extra)
                        if side == 0:
                            pe.wait_ge(bank_free[1], at + UP + 1)
                        for k in range(FT):
                            mm = pe.matmul(bank(side), ring[side][:, k * 128:(k + 1) * 128],
                                           hid[:, k, :], start=(k == 0), stop=(k == FT - 1))
                        mm.then_inc(unit_done, 1)
                norm_stats(l * 3 + 2 * s)

            def scores(l, n):
                if n == 0:
                    pe.wait_ge(gates_ready, l + 1)
                else:
                    pe.wait_ge(s_used, l * 4 + n)
                first = 0 if n else WIN
                for j in range(4):
                    for g in range(2):
                        part = slice(64 * g, 64 * g + 64)
                        c = 256 * (j % 2)
                        mm = pe.matmul(psum[:, 4 + 2 * g + j // 2, c + first:c + 256],
                                       qT[part, j, n * 128:(n + 1) * 128],
                                       kT[part, (n - 1) * 128 + first:(n + 1) * 128],
                                       start=True, stop=True)
                mm.then_inc(s_done, 1)

            def attend(l, n):
                pe.wait_ge(prob_ready, l * 4 + n + 1)
                halves = (0, 1) if n else (1,)
                for r in range(4):
                    if r >= 2:
                        pe.wait_ge(pt_ready, l * 16 + n * 4 + r - 1)
                    for h in (2 * r, 2 * r + 1):
                        for half in halves:
                            c = ((h % 2) * 2 + half) * 128
                            mm = pe.transpose(psum[:, 2 + r % 2, c:c + 128],
                                              prob[n % 2][:, h, half * 128:half * 128 + 128], ident)
                    mm.then_inc(tr_done, 1)
                pe.wait_ge(pt_ready, l * 16 + n * 4 + 4)
                if n >= 2:
                    pe.wait_ge(o_used, l * 4 + n - 1)
                for j in range(4):
                    for g in range(2):
                        for half in halves:
                            mm = pe.matmul(psum[64 * g:64 * g + 64, n % 2, j * 128:(j + 1) * 128],
                                           v_tok[:, n - 1 + half, 64 * g:64 * g + 64],
                                           probT[:, 4 * g + j, half, :],
                                           start=(half == halves[0]), stop=(half == 1))
                mm.then_inc(o_done, 1)

            def mixer(l, extra):
                for n, (kind, _) in enumerate(MIX):
                    side = n % 2
                    wait_unit(l * PL + AT_MIX + n // 2, side, extra)
                    w = ring[side][:, 0:KT * 128].rearrange("p (k c) -> p k c", c=128)
                    for t in range(4 if kind == "v" else 1):
                        for k in range(KT):
                            if n == 0:
                                pe.wait_ge(x_ready, l * 24 + 8 + k + 1)
                            if kind == "v":
                                mm = pe.matmul(bank(side)[:, t * 128:(t + 1) * 128],
                                               xT[:, k, t * 128:(t + 1) * 128], w[:, k, :],
                                               start=(k == 0), stop=(k == KT - 1))
                            else:
                                mm = pe.matmul(bank(side), w[:, k, :], xT[:, k, :],
                                               start=(k == 0), stop=(k == KT - 1))
                    mm.then_inc(unit_done, 1)
                pe.wait_ge(xc_ready, l + 1)
                pe.wait_ge(gw_ready, l * 64 + 64)
                for a in range(2):
                    for t in range(2):
                        mm = pe.matmul(bank(4 + 2 * a + t), gate_w[:, 2 * a + t, :], xc[:, t, :],
                                       start=True, stop=True)
                mm.then_inc(gate_mm, 1)
                pe.wait_ge(conv_ready, l + 1)
                for t in range(2):
                    mm = pe.matmul(bank(2), ones256, conv[:, t, :], start=(t == 0), stop=(t == 1))
                mm.then_inc(cmean_done, 1)
                for t in range(2):
                    pe.wait_ge(csq, l * 2 + t + 1)
                    mm = pe.matmul(bank(3), ones256, conv_sq[:, t, :], start=(t == 0), stop=(t == 1))
                mm.then_inc(cvar_done, 1)
                pe.wait_ge(bank_free[0], l * PL + AT_OUT + 1)
                pe.wait_ge(bank_free[1], l * PL + AT_OUT + 1)
                pe.wait_ge(cstd, l + 1)
                scores(l, 0)
                for n in range(4):
                    if n < 3:
                        scores(l, n + 1)
                    attend(l, n)
                pe.sem_inc(gw_used, 1)
                with pe.Fori(0, WOUT) as i:
                    for side in range(2):
                        wait_unit(l * PL + AT_OUT + i, side, extra + (i * 16 + 16))
                        if side == 0:
                            pe.wait_ge(o_used, l * 4 + 4)
                            pe.wait_ge(y_act, l * 2 + 2)
                            pe.wait_ge(y_dve, l * 2 + 2)
                        for k in range(KT):
                            mm = pe.matmul(bank(side), ring[side][:, k * 128:(k + 1) * 128],
                                           yT[:, k, :], start=(k == 0), stop=(k == KT - 1))
                        mm.then_inc(unit_done, 1)
                norm_stats(l * 3 + 1)

            pe.wait_ge(par_ok, 1)
            with pe.Fori(0, L) as l:
                ffn(l, 0, l * PL, l * 64)
                mixer(l, l * 64)
                ffn(l, 1, l * PL + AT_FF2, l * 64 + 64)
            ada_column(2 * 24)

        @block.scalar
        def _(act):
            for k in range(KT):
                act.wait_ge(x_tr, k + 1)
                act.copy(xT[:, k, :], bank(6 + k % 2)).then_inc(x_ready, 1)
            act.wait_ge(par2_ok, 1)
            act.activation(silu_c.rearrange("p w k -> p (w k)"), params2[:, 0:16], ACT.Silu)\
               .then_inc(silu_ok, 1)
            act.wait_ge(y_in, 1)
            act.activation(lam_y, lam_y, ACT.Exp).then_inc(y_exp, 1)
            act.wait_ge(consts, 1)

            def norm(n, g):
                for k in range(KT):
                    act.wait_ge(diff_ready, n * KT + k + 1)
                    act.activation(xT[:, k, :], rT[:, k, :], ACT.Square).then_inc(sq_ready, 1)
                act.wait_ge(var_done, n + 1)
                act.activation(std, bank(5), ACT.Sqrt, bias=eps_ln).then_inc(std_ready, 1)
                for k in range(KT):
                    act.wait_ge(norm_ready, n * KT + k + 1)
                    act.activation(xT[:, k, :], rT[:, k, :], ACT.Identity,
                                   bias=col(LNB + g + k)).then_inc(x_ready, 1)

            def ffn(l, s, at):
                with act.Fori(0, UP) as i:
                    for side in range(2):
                        act.wait_ge(unit_done, at * 2 + i * 2 + side + 3)
                        act.activation(sg[:, side, :], bank(side), ACT.Silu).then_inc(silu_done, 1)
                norm(l * 3 + 2 * s, 16 * s)

            def exps(l, n):
                act.wait_ge(max_ready, l * 4 + n + 1)
                first = 0 if n else WIN
                for h in range(HEADS):
                    p = prob[n % 2][:, h, first:]
                    act.activation(p, p, ACT.Exp, bias=nmx[:, n % 2, h:h + 1],
                                   accum_out=esum[:, n % 2, h:h + 1])
                act.activation(esink[:, n % 2, :], esink[:, n % 2, :], ACT.Exp).then_inc(exp_ready, 1)

            def copies(l, n):
                for r in range(4):
                    act.wait_ge(tr_done, l * 16 + n * 4 + r + 1)
                    first = 0 if n else 1
                    src = psum[:, 2 + r % 2, :].rearrange("p (h f q) -> p h f q", f=2, q=128)
                    act.copy(probT[:, 2 * r:2 * r + 2, first:, :], src[:, :, first:, :])\
                       .then_inc(pt_ready, 1)
                act.wait_ge(o_done, l * 4 + n + 1)
                act.copy(yT[:, 4:8, n * 128:(n + 1) * 128],
                         psum[:, n % 2, :].rearrange("p (j q) -> p j q", q=128)).then_inc(o_used, 1)

            def mixer(l):
                for n, (kind, t) in enumerate(MIX):
                    side = n % 2
                    if kind in ("a", "xb"):
                        continue
                    act.wait_ge(unit_done, (l * PL + AT_MIX) * 2 + n + 3)
                    if kind == "g":
                        out, func, scale = sg[:, t, :], ACT.Sigmoid, 1.0
                    elif kind == "gb":
                        out, func, scale = gelu_b[:, t, :], ACT.Gelu_apprx_tanh, 1.0
                    elif kind == "k":
                        out, func, scale = kT, ACT.Copy, 1.0
                    elif kind == "v":
                        out, func, scale = v_tok.rearrange("p a b -> p (a b)"), ACT.Copy, 1.0
                    else:
                        out, func, scale = qT[:, t, :], ACT.Copy, 64 ** -0.5
                    act.activation(out, bank(side), func, scale=scale).then_inc(bank_free[side], 1)
                act.wait_ge(gate_mm, l + 1)
                for t in range(2):
                    act.activation(r_gate[:, t, :], bank(4 + t), ACT.Sigmoid, bias=col(BA + t))
                for t in range(2):
                    last = act.activation(i_gate[:, t, :], bank(6 + t), ACT.Sigmoid, bias=col(BX + t))
                last.then_inc(gates_ready, 1)
                act.drain()
                for t in range(2):
                    act.activation(decay[:, t, :], r_gate[:, t, :], ACT.Exp, scale=col(C8 + t))
                    last = act.activation(mult[:, t, :], r_gate[:, t, :], ACT.Tanh, scale=col(NC8 + t))
                last.then_inc(decay_ready, 1)
                for t in range(2):
                    act.wait_ge(cdiff, l * 2 + t + 1)
                    act.activation(conv_sq[:, t, :], conv[:, t, :], ACT.Square).then_inc(csq, 1)
                act.wait_ge(m2_ready, l + 1)
                act.activation(mult, mult, ACT.Sqrt).then_inc(mult_ready, 1)
                act.wait_ge(cvar_done, l + 1)
                act.activation(conv_rstd, bank(3), ACT.Sqrt, bias=eps_conv).then_inc(cstd, 1)
                for t in range(2):
                    act.wait_ge(cnorm, l * 2 + t + 1)
                    act.activation(yT[:, t, :], conv[:, t, :], ACT.Silu, bias=col(CBB + t))\
                       .then_inc(y_act, 1)
                exps(l, 0)
                for n in range(4):
                    if n < 3:
                        exps(l, n + 1)
                    copies(l, n)
                norm(l * 3 + 1, 8)

            with act.Fori(0, L) as l:
                act.wait_ge(cur_ready, l + 1)
                ffn(l, 0, l * PL)
                mixer(l)
                ffn(l, 1, l * PL + AT_FF2)

        @block.vector
        def _(dve):
            dve.memset(erow[0:HEADS, :], -1e30)
            dve.wait_ge(par_tr, 1)
            dve.tensor_copy(params2, psum[:, 4, 264:424]).then_inc(par2_ok, 1)
            pv = params.rearrange("p (l c) -> p l c", c=CL)
            dve.tensor_copy(pv[:, :, 0:132], psum[:, 4, 0:2 * 132].rearrange("p (l c) -> p l c", c=132))\
               .then_inc(par_ok, 1)
            dve.wait_ge(e_mm, 1)
            dve.drain()
            dve.tensor_copy(erow[0:HEADS, WIN:2 * WIN], psum[0:HEADS, 5, 0:WIN]).then_inc(e_ok, 1)
            lam = pv[:, :, LAM:LAM + 2]
            dve.drain()
            dve.scalar_tensor_tensor(out=lam_y, in0=lam, scalar=-1.0, in1=lam, op0=ALU.mult,
                                     op1=ALU.min).then_inc(y_in, 1)
            dve.wait_ge(y_exp, 1)
            dve.tensor_scalar(lam_z, lam_y, 2.0, None, ALU.add)
            dve.drain()
            dve.reciprocal(lam_z, lam_z)
            dve.drain()
            dve.tensor_tensor(lam_z, lam_z, lam_y, ALU.mult)
            dve.drain()
            dve.tensor_tensor(lam_q, lam_z, lam_z, ALU.mult)
            dve.memset(lam_s, 1.0 / 19)
            for c in range(17, 0, -2):
                dve.drain()
                dve.tensor_tensor(lam_s, lam_s, lam_q, ALU.mult)
                dve.drain()
                dve.tensor_scalar(lam_s, lam_s, 1.0 / c, None, ALU.add)
            dve.drain()
            dve.scalar_tensor_tensor(out=lam_s, in0=lam_s, scalar=2.0, in1=lam_z, op0=ALU.mult, op1=ALU.mult)
            dve.drain()
            dve.scalar_tensor_tensor(out=lam_s, in0=lam, scalar=0.0, in1=lam_s, op0=ALU.min,
                                     op1=ALU.subtract)
            dve.drain()
            dve.tensor_scalar(pv[:, :, C8:C8 + 2], lam_s, 8.0, None, ALU.mult)
            dve.tensor_scalar(pv[:, :, NC8:NC8 + 2], lam_s, -8.0, None, ALU.mult)
            dve.wait_ge(sink_in, 16)
            dve.wait_ge(band_in, 16)
            dve.wait_ge(consts, 1)
            dve.drain()
            dve.sem_inc(ada_ready, 1)

            def norm(n, g):
                dve.wait_ge(mean_done, n + 1)
                for k in range(KT):
                    dve.tensor_tensor(rT[:, k, :], rT[:, k, :], bank(4), ALU.subtract)\
                       .then_inc(diff_ready, 1)
                dve.wait_ge(std_ready, n + 1)
                dve.reciprocal(std, std)
                dve.drain()
                for k in range(KT):
                    dve.scalar_tensor_tensor(out=rT[:, k, :], in0=rT[:, k, :], scalar=col(LNG + g + k),
                                             in1=std, op0=ALU.mult, op1=ALU.mult)\
                       .then_inc(norm_ready, 1)

            def residuals(pair0, scale):
                with dve.Fori(0, KT // 2) as i:
                    for side in range(2):
                        dve.wait_ge(unit_done, (pair0 + i) * 2 + side + 3)
                        tile = bass.ds(i * 2 + side, 1)
                        dve.scalar_tensor_tensor(
                            out=rT[:, tile, :].rearrange("p a b -> p (a b)"), in0=bank(side),
                            scalar=scale, in1=xT[:, tile, :].rearrange("p a b -> p (a b)"),
                            op0=ALU.mult, op1=ALU.add).then_inc(bank_free[side], 1)

            def put_modulation(a):
                dve.wait_ge(ada_sum, a + 1)
                dve.tensor_tensor(mod[:, bass.ds(a, 1), :].rearrange("p a b -> p (a b)"), psum[:, 6, 0:2],
                                  params2[:, bass.ds(a + 15, 1)].to_broadcast([128, 2]), ALU.add)

            def ada_sums(a):
                put_modulation(a)
                dve.wait_ge(ada_prods, a + 2)
                dve.tensor_reduce(ada_acc, ada_prod.rearrange("p w k c -> p w c k"), AX.X, ALU.add)\
                   .then_inc(ada_ready, 1)

            def ffn(l, s, at):
                with dve.Fori(0, UP) as i:
                    ada_sums(l * 24 + s * 12 + i)
                    for side in range(2):
                        dve.wait_ge(silu_done, l * 2 * FT + s * FT + i * 2 + side + 1)
                        tile = hid[:, bass.ds(i * 2 + side, 1), :].rearrange("p a b -> p (a b)")
                        dve.tensor_tensor(tile, sg[:, side, :], bank(2 + side), ALU.mult)\
                           .then_inc(bank_free[side], 1)
                ada_sums(l * 24 + s * 12 + UP)
                residuals(at + UP, 0.5 / ALPHA)
                norm(l * 3 + 2 * s, 16 * s)

            def scores(l, n):
                b, first = n % 2, 0 if n else WIN
                p = prob[b][:, :, first:]
                dve.wait_ge(s_done, l * 4 + n + 1)
                ps = psum[:, 4:8, :].rearrange("p b (h k) -> p (b h) k", k=256)
                dve.tensor_tensor(p, ps[:, :, first:], band[:, :, first:], ALU.add).then_inc(s_used, 1)
                dve.drain()
                dve.tensor_reduce(mx[:, b, :], p, AX.X, ALU.max)
                dve.drain()
                dve.tensor_tensor(mx[:, b, :], mx[:, b, :], sink_of[0], ALU.max)
                dve.drain()
                dve.tensor_tensor(esink[:, b, :], sink_of[0], mx[:, b, :], ALU.subtract)
                dve.tensor_scalar(nmx[:, b, :], mx[:, b, :], -1.0, None, ALU.mult).then_inc(max_ready, 1)

            def normalise(l, n):
                b, first = n % 2, 0 if n else WIN
                p = prob[b][:, :, first:]
                dve.wait_ge(exp_ready, l * 4 + n + 1)
                dve.tensor_tensor(rsum[:, b, :], esum[:, b, :], esink[:, b, :], ALU.add)
                dve.drain()
                dve.reciprocal(rsum[:, b, :], rsum[:, b, :])
                dve.drain()
                dve.tensor_tensor(p, p, rsum[:, b, :].unsqueeze(2).to_broadcast([128, HEADS, 256 - first]),
                                  ALU.mult).then_inc(prob_ready, 1)

            def taps(out, pad, n, w, bias):
                for c in range(n):
                    for t in range(2):
                        src = pad[:, t, c:c + T]
                        if c == 0:
                            last = dve.tensor_scalar(out[:, t, :], src, col(w + t), col(bias + t),
                                                     ALU.mult, ALU.add)
                        else:
                            last = dve.scalar_tensor_tensor(out=out[:, t, :], in0=src,
                                                            scalar=col(w + 2 * c + t), in1=out[:, t, :],
                                                            op0=ALU.mult, op1=ALU.add)
                    if c < n - 1:
                        dve.drain()
                return last

            sink_of = [None]

            def mixer(l):
                sink_of[0] = sinks[:, bass.ds(l * HEADS, HEADS)]
                dve.memset(cpad[:, :, 0:30], 0.0)
                dve.memset(lpad[:, :, 0:3], 0.0)
                for n, (kind, t) in enumerate(MIX[:6]):
                    pair, side = l * PL + AT_MIX + n // 2, n % 2
                    if kind == "a":
                        dve.wait_ge(bank_free[1], pair + 2)
                        dve.tensor_tensor(cpad[:, t, 30:], sg[:, t, :], bank(0), ALU.mult)\
                           .then_inc(bank_free[0], 1)
                    elif kind == "xb":
                        dve.wait_ge(unit_done, pair * 2 + side + 3)
                        dve.tensor_copy(lpad[:, t, 3:], bank(side)).then_inc(bank_free[side], 1)
                dve.drain()
                taps(xc, lpad, 4, LW, LB).then_inc(xc_ready, 1)
                taps(conv, cpad, 31, CW, CB).then_inc(conv_ready, 1)
                dve.wait_ge(decay_ready, l + 1)
                dve.tensor_tensor(i_gate, i_gate, xc, ALU.mult)
                dve.tensor_tensor(r_gate, decay, decay, ALU.mult)
                dve.drain()
                dve.scalar_tensor_tensor(out=mult, in0=r_gate, scalar=1.0, in1=mult, op0=ALU.add,
                                         op1=ALU.mult).then_inc(m2_ready, 1)
                dve.wait_ge(cmean_done, l + 1)
                for t in range(2):
                    dve.tensor_tensor(conv[:, t, :], conv[:, t, :], bank(2), ALU.subtract)\
                       .then_inc(cdiff, 1)
                dve.wait_ge(mult_ready, l + 1)
                dve.tensor_tensor(i_gate, i_gate, mult, ALU.mult)
                dve.drain()
                for t in range(2):
                    dve.tensor_tensor_scan(r_gate[:, t, :], decay[:, t, :], i_gate[:, t, :], 0.0,
                                           ALU.mult, ALU.add)
                dve.wait_ge(cstd, l + 1)
                dve.reciprocal(conv_rstd, conv_rstd)
                dve.drain()
                for t in range(2):
                    dve.scalar_tensor_tensor(out=conv[:, t, :], in0=conv[:, t, :], scalar=col(CG + t),
                                             in1=conv_rstd, op0=ALU.mult, op1=ALU.mult)\
                       .then_inc(cnorm, 1)
                for t in range(2):
                    dve.wait_ge(bank_free[t], l * PL + AT_MIX + 5)
                    dve.tensor_tensor(yT[:, 2 + t, :], r_gate[:, t, :], gelu_b[:, t, :], ALU.mult)\
                       .then_inc(y_dve, 1)
                scores(l, 0)
                for n in range(4):
                    if n < 3:
                        scores(l, n + 1)
                    normalise(l, n)
                residuals(l * PL + AT_OUT, 1.0 / ALPHA)
                norm(l * 3 + 1, 8)

            with dve.Fori(0, L) as l:
                dve.wait_ge(x_ready, l * 24 + 8)
                dve.tensor_copy(cur, params[:, bass.ds(l * CL, CL)]).then_inc(cur_ready, 1)
                ffn(l, 0, l * PL)
                mixer(l)
                ffn(l, 1, l * PL + AT_FF2)
            put_modulation(2 * 24)


def second_mixer_program(nc, d, mem):
    f32 = mybir.dt.float32
    ALU, ACT, AX = mybir.AluOpType, mybir.ActivationFunctionType, mybir.AxisListType
    KT, T, C = 8, 512, 256
    NT, NC, CH = 4, 2, 128
    H, G = 16, 4
    XS, BM, CM = 0, 8, 12
    ZC, UC, VC, GA, GB = 2080, 3104, 4128, 5152, 6176

    ctx = ExitStack()
    with ctx:
        arena, psum = mem["arena"], mem["psum"]
        cursor = [0]

        def place(*shape):
            size = int(np.prod(shape))
            v = arena[:, cursor[0]:cursor[0] + size]
            cursor[0] += size
            assert cursor[0] <= mem["size"], cursor[0]
            if len(shape) == 2:
                return v.rearrange("p (a b) -> p a b", b=shape[1])
            if len(shape) == 3:
                return v.rearrange("p (a b c) -> p a b c", b=shape[1], c=shape[2])
            return v

        def sem(name):
            return mem["sem"]("m_" + name)

        res = place(KT, T)
        ident = place(128)
        mod = place(49, 2)[:, 1:, :]
        params = place(160)
        ring = [place(2048) for _ in range(2)]
        onesD, ones1, ones256 = place(128), place(128), place(128)
        tri_f, tri_b, mask_f, mask_b = place(128), place(128), place(128), place(128)
        eps6 = place(1)
        nscale = place(KT, 2)
        d_all, d_skip = place(H), place(KT)
        dt_bias, a_neg = place(32), place(32)
        w_dt = place(KT, 32)
        dt, dta, dt_y, dt_z, dt_q, dt_s = (place(6, 32) for _ in range(6))
        nacum, w_end, c_dec = place(6, 32), place(6, 32), place(6, 32)
        rstd = place(T)
        pad_l = place(2, T + 2)
        pad_c = place(2, C + 2)
        cv = place(2, T)
        xm = place(KT, T)
        y = place(KT, T)
        c_in = y[:, 0:4, :].rearrange("p a b -> p (a b)").rearrange("p (a b) -> p a b", b=C)
        xm_c = y[:, 4:8, :].rearrange("p a b -> p (a b)").rearrange("p (a b) -> p a b", b=C)
        xbc = place(16, T)
        xbc_flat = xbc.rearrange("p a b -> p (a b)")
        xbc_c = xbc_flat[:, 0:12 * C].rearrange("p (a b) -> p a b", b=C)
        sq_c = xbc_flat[:, 4096:4096 + KT * C].rearrange("p (a b) -> p a b", b=C)
        c_tok = xbc_flat[:, 0:2048].rearrange("p (a b) -> p a b", b=1024)
        x_tok = place(NT, 1024)
        b_tok_at = cursor[0]
        b_tok = place(NT, 512)
        xw = place(2, 1024)
        state = [place(NT, 1024) for _ in range(2)]
        df, db, cf, cb = (place(2, 4, CH) for _ in range(4))
        v_tok = arena[:, b_tok_at:b_tok_at + NT * 1024].rearrange("p (a b) -> p a b", b=1024)
        uT = res
        sgu = state[1].rearrange("p a b -> p (a b)").rearrange("p (a b) -> p a b", b=T)
        sq_y = xbc[:, 0:8, :]
        x_flat = x_tok.rearrange("p a b -> p (a b)")
        merged = x_flat.rearrange("p (a b) -> p a b", b=T)
        tail = xbc[:, 8:16, :].rearrange("p a b -> p (a b)")
        ln_w, ln_b, bs_bc = tail[:, 0:1024], tail[:, 1024:2048], tail[:, 2048:3072]
        ws_T = tail[:, 3072:4096].rearrange("p (g i) -> p g i", g=8)
        ws_in = x_flat[:, 0:1024].rearrange("p (g j) -> p g j", g=8)
        sq_v = x_flat[:, 1024:2048]
        mixed = x_flat[:, 2048:3072].rearrange("p (s t) -> p s t", s=2)
        z_s = df.rearrange("p s h i -> p s (h i)")
        gates = [[v.rearrange("p s h i -> p s (h i)")[:, i, :] for i in range(2)] for v in (cf, df)]
        rs_y = db.rearrange("p s h i -> p s (h i)")
        rs_y2 = cb.rearrange("p s h i -> p s (h i)")
        v_sum, v_var = place(NT), place(NT)

        PN1, PCB, PSN, PCW = 64, 80, 96, 112

        def bank(b):
            return psum[:, b, :]

        def par(c):
            return params[:, c:c + 1]

        names = ("ctx_in small_in wdt_in consts ctx_tr ctx_t a_exp "
                 "unit_done sqc_ready varc_done stdc_ready nc_ready xmc_ready sql_ready varl_done "
                 "stdl_ready nl_ready xml_ready dt_mm dt_abs dt_exp dt_ok cum_done ac_ready w_ready2 tr_done "
                 "tr_used xw_ready st_done st_used  conv_done xbc_ready bc_done tm_ready "
                 "ea_ready fb_ready ff_ready cc_ready pb_ready m_ready y_done y_used ln_in ws_in_s "
                 "vh_done vh_free res_out res_back v_gelu v_mean v_sq v_std v_ok ws_tr ws_ok u_ok mix_done mix_used y_sq gvar_done gstd y_ok "
                 "z_ok ga_ready sgu_ok").split()
        s = {n: sem(n) for n in names}
        w_ready = [sem("w_ready0"), sem("w_ready1")]
        bank_free = [sem("bank_free0"), sem("bank_free1")]
        unit_done = s["unit_done"]

        CTX, SCAN, VP, UP, ZP, MERGE, WO = 0, 6, 14, 16, 20, 24, 32

        block = ctx.enter_context(nc.Block())

        @block.sync
        def _(sp):
            sp.dma_start(c_tok, d["ctx_2"][0].rearrange("(t p) n -> p t n", p=128)).then_inc(s["ctx_in"], 16)

            def slot_free(pair, side):
                sp.wait_ge(unit_done, 2 * pair + side + 1)

            def tiles(w):
                return w.rearrange("(k p) c -> p k c", p=128)

            def load(side, cols, sources):
                if len(sources) == 1:
                    to = ring[side][:, 0:KT * cols].rearrange("p (k c) -> p k c", c=cols)
                    for h in range(2):
                        sp.dma_start(to[:, 4 * h:4 * h + 4, :], tiles(sources[0](512 * h, 512)))\
                          .then_inc(w_ready[side], 16)
                else:
                    to = ring[side].rearrange("p (k c) -> p k c", c=cols)
                    for h in range(2):
                        sp.dma_start(to[:, KT * h:KT * h + KT, :], tiles(sources[h](0, 1024)))\
                          .then_inc(w_ready[side], 16)

            def of(name, c0, i, step, width):
                return lambda r, n: d[name][0, r:r + n, bass.ds(i * step + c0, width)]

            sp.dma_start(d_all, d["d_skip_2"][0].partition_broadcast(128)).then_inc(s["small_in"], 16)
            sp.dma_start(dt_bias, d["dt_bias_2"][0].rearrange("a h -> (a h)").partition_broadcast(128))\
              .then_inc(s["small_in"], 16)
            sp.dma_start(a_neg, d["a_log_2"][0].rearrange("a h -> (a h)").partition_broadcast(128))\
              .then_inc(s["small_in"], 16)
            sp.dma_start(w_dt, tiles(d["w_in_2"][0, :, 2048:2080])).then_inc(s["wdt_in"], 16)

            def single(pair0, n, c0, name="w_in_2"):
                with sp.Fori(0, n) as i:
                    for side in range(2):
                        slot_free(i + pair0, side)
                        load(side, 128, [of(name, c0 + side * 128, i, 256, 128)])

            single(CTX, 6, 0)
            single(SCAN, 8, 0)
            sp.wait_ge(s["xml_ready"], KT)
            sp.dma_start(d["res_scratch"], res).then_inc(s["res_out"], 16)
            for n in range(4):
                slot_free(VP + n // 2, n % 2)
                load(n % 2, 256, [of("w_in_2", VC + 256 * n, 0, 0, 256)])
            single(UP, 4, UC)
            sp.wait_ge(s["y_used"], 16)
            for to, name in ((ln_w, "sgu_ln_w_2"), (ln_b, "sgu_ln_b_2")):
                sp.dma_start(to, d[name][0].partition_broadcast(128)).then_inc(s["ln_in"], 16)
            sp.dma_start(bs_bc, d["b_s_2"][0].rearrange("g i -> (g i)").partition_broadcast(128))\
              .then_inc(s["ln_in"], 16)
            sp.dma_start(ws_in, d["w_s_2"][0].rearrange("g i j -> i g j")).then_inc(s["ws_in_s"], 16)
            single(ZP, 4, ZC)
            with sp.Fori(1, 9) as i:
                slot_free(i + (MERGE - 1), 0)
                load(0, 128, [of("w_in_2", GA - 128, i, 128, 128), of("w_in_2", GB - 128, i, 128, 128)])
                slot_free(i + (MERGE - 1), 1)
                load(1, 128, [of("w_pa_2", -128, i, 128, 128), of("w_pb_2", -128, i, 128, 128)])
            sp.wait_ge(s["mix_used"], 8)
            sp.wait_ge(s["res_out"], 16)
            sp.dma_start(res, d["res_scratch"]).then_inc(s["res_back"], 16)
            single(WO, 4, 0, "w_o_2")

        @block.gpsimd
        def _(pool):
            pool.memset(onesD, 1.0 / 1024)
            pool.memset(ones1, 1.0)
            pool.memset(ones256, 1.0 / 256)
            pool.memset(eps6, 1e-6)
            pool.memset(tri_f, 1.0)
            pool.memset(tri_b, 1.0)
            pool.memset(mask_f, 0.0)
            pool.memset(mask_b, 0.0)
            pool.memset(pad_l, 0.0)
            pool.memset(pad_c, 0.0)
            pool.memset(state[0], 0.0)
            pool.memset(state[1], 0.0)
            pool.drain()
            for m, fill, sign in ((tri_f, 0.0, 1), (tri_b, 0.0, -1), (mask_f, -1e30, 1), (mask_b, -1e30, -1)):
                pool.affine_select(out=m, in_=m, compare_op=ALU.is_ge, fill=fill, base=0,
                                   pattern=[[sign, 128]], channel_multiplier=-sign)
            pool.drain()
            pool.sem_inc(s["consts"], 1)
            for n in range(NT * G):
                c, g, b = n // G, n % G, n % 2
                ct = xbc[:, CM + g, c * CH:(c + 1) * CH].unsqueeze(1).to_broadcast([128, 4, CH])
                pool.wait_ge(s["ea_ready"], n + 1)
                pool.tensor_tensor(cf[:, b, :, :], cf[:, b, :, :], ct, ALU.mult)
                pool.tensor_tensor(cb[:, b, :, :], cb[:, b, :, :], ct, ALU.mult).then_inc(s["cc_ready"], 1)
                pool.wait_ge(s["fb_ready"], n + 1)
                dtb = dt[:, c, H + 4 * g:H + 4 * g + 4].unsqueeze(2).to_broadcast([128, 4, CH])
                pool.tensor_tensor(db[:, b, :, :], db[:, b, :, :], dtb, ALU.mult).then_inc(s["pb_ready"], 1)

        steps = ([(0, NT + c, 0, 0) for c in range(NC)] + [(1, NT + c, 3, 3) for c in reversed(range(NC))])
        steps_l = [(0, c, c, c + 1) for c in range(3)] + [(1, c, c, c - 1) for c in (3, 2, 1)]

        def st_banks(k):
            return (2, 3) if k % 2 == 0 else (6, 7)

        @block.tensor
        def _(pe):
            pe.sem_inc(unit_done, 2)
            pe.sem_inc(bank_free[0], 1)
            pe.sem_inc(bank_free[1], 1)
            pe.wait_ge(s["ctx_in"], 16)
            for k in range(KT):
                if k >= 2:
                    pe.wait_ge(s["ctx_t"], k - 1)
                for t in range(NC):
                    mm = pe.transpose(psum[:, 6 + k % 2, t * 128:(t + 1) * 128],
                                      c_tok[:, t, k * 128:(k + 1) * 128], ident)
                mm.then_inc(s["ctx_tr"], 1)

            def wait_unit(pair, side):
                pe.wait_ge(w_ready[side], pair * 32 + 32)
                pe.wait_ge(bank_free[side], pair + 1)

            pe.wait_ge(s["consts"], 1)
            def rms(sq, ready, done, width):
                for k in range(KT):
                    pe.wait_ge(ready, k + 1)
                    mm = pe.matmul(psum[:, 5, 0:width], onesD, sq[:, k, :], start=(k == 0), stop=(k == KT - 1))
                mm.then_inc(done, 1)

            def raw_dt(x, ready, t0, n, base):
                pe.wait_ge(ready, KT)
                pe.wait_ge(s["wdt_in"], 16)
                for t in range(n):
                    for k in range(KT):
                        mm = pe.matmul(psum[:, 4, (t0 + t) * 32:(t0 + t + 1) * 32], x[:, k, t * 128:(t + 1) * 128],
                                       w_dt[:, k, :], start=(k == 0), stop=(k == KT - 1))
                mm.then_inc(s["dt_mm"], 1)

            def units(pair0, n, x, width):
                with pe.Fori(0, n) as i:
                    for side in range(2):
                        wait_unit(i + pair0, side)
                        for k in range(KT):
                            mm = pe.matmul(psum[:, side, 0:width], ring[side][:, k * 128:(k + 1) * 128],
                                           x[:, k, :], start=(k == 0), stop=(k == KT - 1))
                        mm.then_inc(unit_done, 1)

            def cumulate(t0, n, call):
                pe.wait_ge(s["dt_ok"], call)
                for t in range(t0, t0 + n):
                    pe.matmul(psum[:, 5, t * 64:t * 64 + 16], tri_f, dta[:, t, 0:16], start=True, stop=True)
                    pe.matmul(psum[:, 5, t * 64 + 16:t * 64 + 32], tri_b, dta[:, t, 16:32], start=True, stop=True)
                    mm = pe.matmul(psum[:, 5, t * 64 + 32:t * 64 + 64], ones1, dta[:, t, :], start=True, stop=True)
                mm.then_inc(s["cum_done"], 1)

            def to_tokens(x, n, round0, x_count):
                pe.wait_ge(s["xbc_ready"], x_count)
                for r in range(3 * n):
                    if round0 + r >= 2:
                        pe.wait_ge(s["tr_used"], round0 + r - 1)
                    c, part = r // 3, r % 3
                    for q in range(4):
                        mm = pe.transpose(psum[:, 6 + r % 2, q * 128:(q + 1) * 128],
                                          x[:, 4 * part + q, c * CH:(c + 1) * CH], ident)
                    mm.then_inc(s["tr_done"], 1)
                pe.wait_ge(s["tr_used"], round0 + 3 * n)

            def states(k0, some):
                for k, (way, t, _, _) in enumerate(some, k0):
                    pe.wait_ge(s["xw_ready"], k + 1)
                    if k >= 2:
                        pe.wait_ge(s["st_used"], k - 1)
                    for g in range(G):
                        mm = pe.matmul(psum[:, st_banks(k)[g // 2], (g % 2) * 256:(g % 2) * 256 + 256],
                                       b_tok[:, t % NT, g * 128:(g + 1) * 128],
                                       xw[:, k % 2, g * 256:(g + 1) * 256], start=True, stop=True)
                    mm.then_inc(s["st_done"], 1)

            rms(sq_c, s["sqc_ready"], s["varc_done"], C)
            raw_dt(xm_c, s["xmc_ready"], NT, NC, 0)
            units(CTX, 6, xm_c, C)
            cumulate(NT, NC, 1)
            to_tokens(xbc_c, NC, 0, 12)
            states(0, steps)
            rms(y, s["sql_ready"], s["varl_done"], T)
            raw_dt(xm, s["xml_ready"], 0, NT, 0)
            units(SCAN, 8, xm, T)
            cumulate(0, NT, 2)
            to_tokens(xbc, NT, 3 * NC, 12 + 16)
            states(4, steps_l)
            pe.wait_ge(s["st_used"], 10)
            pe.wait_ge(bank_free[0], VP + 1)
            pe.wait_ge(bank_free[1], VP + 1)

            def bcasts(n):
                c, g, b = n // G, n % G, n % 2
                if n >= 2:
                    pe.wait_ge(s["ff_ready"], n - 1)
                    pe.wait_ge(s["m_ready"], n - 1)
                    pe.wait_ge(s["y_used"], n - 1)
                chunk = slice(c * CH, (c + 1) * CH)
                pe.matmul(psum[:, 4 + 3 * b, 0:CH], xbc[:, BM + g, chunk], xbc[:, CM + g, chunk],
                          start=True, stop=True)
                for way, tri in ((0, tri_f), (1, tri_b)):
                    for h in range(4):
                        col = dta[:, c, H * way + 4 * g + h:H * way + 4 * g + h + 1]
                        mm = pe.matmul(psum[:, 2 + 3 * b + way, h * CH:(h + 1) * CH],
                                       col.to_broadcast([128, 128]), tri, start=True, stop=True)
                mm.then_inc(s["bc_done"], 1)

            def outputs(n):
                c, g, b = n // G, n % G, n % 2
                pe.wait_ge(s["cc_ready"], n + 1)
                pe.wait_ge(s["m_ready"], n + 1)
                for h in range(4):
                    cols = slice((4 * g + h) * 64, (4 * g + h + 1) * 64)
                    out = psum[64 * (h % 2):64 * (h % 2) + 64, 4 + 3 * b, 256 + (h // 2) * CH:256 + (h // 2 + 1) * CH]
                    pe.matmul(out, x_tok[:, c, cols], df[:, b, h, :], start=True, stop=False)
                    pe.matmul(out, state[0][:, c, cols], cf[:, b, h, :], start=False, stop=False)
                    mm = pe.matmul(out, state[1][:, c, cols], cb[:, b, h, :], start=False, stop=True)
                mm.then_inc(s["y_done"], 1)

            def v_half(j):
                n, half = j // 2, j % 2
                pair, side = VP + n // 2, n % 2
                wait_unit(pair, side)
                if n and half == 0:
                    pe.wait_ge(s["vh_free"], n)
                if n and half:
                    before = VP * 2 + n - 1
                    pe.wait_ge(bank_free[before % 2], before // 2 + 2)
                w = ring[side].rearrange("p (k c) -> p k c", c=256)
                for t in range(2):
                    tile = 2 * half + t
                    for k in range(KT):
                        mm = pe.matmul(psum[:, half, t * 256:(t + 1) * 256],
                                       xm[:, k, tile * 128:(tile + 1) * 128], w[:, k, :],
                                       start=(k == 0), stop=(k == KT - 1))
                mm.then_inc(unit_done if half else s["vh_done"], 1)

            def unit(m, x):
                side = m % 2
                wait_unit(m // 2, side)
                for k in range(KT):
                    mm = pe.matmul(bank(side), ring[side][:, k * 128:(k + 1) * 128], x[:, k, :],
                                   start=(k == 0), stop=(k == KT - 1))
                mm.then_inc(unit_done, 1)

            bcasts(0)
            for n in range(NT * G):
                if n + 1 < NT * G:
                    bcasts(n + 1)
                if n < 8:
                    v_half(n)
                else:
                    if n == 8:
                        pe.wait_ge(s["vh_free"], 4)
                        pe.wait_ge(bank_free[1], UP + 1)
                    unit(UP * 2 + n - 8, xm)
                outputs(n)
            pe.wait_ge(s["ws_in_s"], 16)
            for r in range(2):
                for q in range(4):
                    mm = pe.transpose(psum[:, 6 + r, q * 128:(q + 1) * 128], ws_in[:, 4 * r + q, :], ident)
            mm.then_inc(s["ws_tr"], 1)

            def mix(g):
                if g == 0:
                    pe.wait_ge(s["v_ok"], 1)
                    pe.wait_ge(s["ws_ok"], 1)
                if g >= 2:
                    pe.wait_ge(s["mix_used"], g - 1)
                for c in range(NT):
                    mm = pe.matmul(psum[:, 4 + g % 2, c * CH:(c + 1) * CH], v_tok[:, c, g * 128:(g + 1) * 128],
                                   ws_T[:, g, :], start=True, stop=True)
                mm.then_inc(s["mix_done"], 1)

            def group_var(q):
                if q >= 2:
                    pe.wait_ge(s["gstd"], q - 1)
                for t in range(2):
                    pe.wait_ge(s["y_sq"], 2 * q + t + 1)
                    mm = pe.matmul(bank(6 + q % 2), ones256, sq_y[:, 2 * q + t, :], start=(t == 0), stop=(t == 1))
                mm.then_inc(s["gvar_done"], 1)

            for n in range(8):
                unit(ZP * 2 + n, xm)
                if n >= 5:
                    group_var(n - 5)
                if n >= 4:
                    mix(2 * (n - 4))
                    mix(2 * (n - 4) + 1)
            group_var(3)
            pe.wait_ge(bank_free[0], MERGE + 1)
            pe.wait_ge(bank_free[1], MERGE + 1)
            with pe.Fori(0, 4) as i:
                for turn in range(2):
                    for side in range(2):
                        pe.wait_ge(w_ready[side], (i * 2 + turn + MERGE) * 32 + 32)
                        pe.wait_ge(bank_free[side], i * 2 + turn + MERGE)
                        if side == 0 and turn:
                            pe.wait_ge(s["mix_used"], 8)
                            pe.wait_ge(s["gstd"], 4)
                        if side:
                            pe.wait_ge(s["y_ok"], 8)
                            pe.wait_ge(s["mix_used"], 8)
                        for half in range(2):
                            x = (y, sgu)[half] if side else xm
                            for k in range(KT):
                                c = (half * KT + k) * 128
                                mm = pe.matmul(bank(4 * turn + side + 2 * half), ring[side][:, c:c + 128],
                                               x[:, k, :], start=(k == 0), stop=(k == KT - 1))
                        mm.then_inc(unit_done, 1)
            pe.wait_ge(bank_free[1], WO + 1)
            units(WO, 4, merged, T)

        @block.scalar
        def _(act):
            for k in range(KT):
                act.wait_ge(s["ctx_tr"], k + 1)
                act.copy(c_in[:, k, :], psum[:, 6 + k % 2, 0:C]).then_inc(s["ctx_t"], 1)
            act.drain()
            for k in range(KT):
                act.activation(sq_c[:, k, :], c_in[:, k, :], ACT.Square).then_inc(s["sqc_ready"], 1)
            act.wait_ge(s["small_in"], 48)
            act.activation(a_neg, a_neg, ACT.Exp).then_inc(s["a_exp"], 1)

            def rms(width, dst, which, done, std_ready, n_ready, out_ready):
                act.wait_ge(done, 1)
                act.activation(rstd[:, 0:width], psum[:, 5, 0:width], ACT.Sqrt, bias=eps6).then_inc(std_ready, 1)
                for k in range(KT):
                    act.wait_ge(n_ready, k + 1)
                    act.activation(dst[:, k, :], dst[:, k, :], ACT.Identity, bias=mod[:, k, which:which + 1])\
                       .then_inc(out_ready, 1)

            def scan_units(pair0, n, pad, width, dst):
                with act.Fori(0, n) as i:
                    for side in range(2):
                        act.wait_ge(unit_done, (i + pair0) * 2 + side + 3)
                        act.copy(pad[:, side, 1:1 + width], psum[:, side, 0:width]).then_inc(bank_free[side], 1)
                        act.wait_ge(s["conv_done"], (i + (pair0 - CTX)) * 2 + side + 1)
                        act.activation(dst[:, bass.ds(i * 2 + side, 1), :].rearrange("p a b -> p (a b)"),
                                       cv[:, side, 0:width], ACT.Silu,
                                       bias=params[:, bass.ds(i * 2 + (PCB + side), 1)])\
                           .then_inc(s["xbc_ready"], 1)

            def softplus_exp(call, t0, n):
                act.wait_ge(s["dt_abs"], call)
                act.activation(dt_y[:, t0:t0 + n, :], dt_y[:, t0:t0 + n, :], ACT.Exp).then_inc(s["dt_exp"], 1)

            def decays(call, t0, n):
                act.wait_ge(s["ac_ready"], call)
                act.activation(w_end[:, t0:t0 + n, :], w_end[:, t0:t0 + n, :], ACT.Exp)
                act.activation(c_dec[:, t0:t0 + n, :], c_dec[:, t0:t0 + n, :], ACT.Exp).then_inc(s["w_ready2"], 1)

            def token_copies(n, round0):
                for r in range(3 * n):
                    act.wait_ge(s["tr_done"], round0 + r + 1)
                    c, part = r // 3, r % 3
                    to = x_tok[:, c, part * 512:(part + 1) * 512] if part < 2 else b_tok[:, c, :]
                    act.copy(to, bank(6 + r % 2)).then_inc(s["tr_used"], 1)

            rms(C, xm_c, 1, s["varc_done"], s["stdc_ready"], s["nc_ready"], s["xmc_ready"])
            softplus_exp(1, NT, NC)
            scan_units(CTX, 6, pad_c, C, xbc_c)
            decays(1, NT, NC)
            token_copies(NC, 0)
            act.wait_ge(unit_done, SCAN * 2 + 2)
            for k in range(KT):
                act.activation(y[:, k, :], res[:, k, :], ACT.Square).then_inc(s["sql_ready"], 1)
            rms(T, xm, 0, s["varl_done"], s["stdl_ready"], s["nl_ready"], s["xml_ready"])
            softplus_exp(2, 0, NT)
            scan_units(SCAN, 8, pad_l, T, xbc)
            decays(2, 0, NT)
            token_copies(NT, 3 * NC)
            def decay_matrices(n):
                c, g, b = n // G, n % G, n % 2
                act.wait_ge(s["tm_ready"], n + 1)
                if n >= 2:
                    act.wait_ge(s["y_done"], n - 1)
                act.activation(cf[:, b, :, :].rearrange("p h i -> p (h i)"), bank(2 + 3 * b), ACT.Exp)
                act.activation(cb[:, b, :, :].rearrange("p h i -> p (h i)"), bank(3 + 3 * b), ACT.Exp)\
                   .then_inc(s["ea_ready"], 1)
                for way, m, ready in ((1, db, "fb_ready"), (0, df, "ff_ready")):
                    for h in range(4):
                        at = H * way + 4 * g + h
                        last = act.activation(m[:, b, h, :], m[:, b, h, :], ACT.Exp,
                                              bias=nacum[:, c, at:at + 1])
                    last.then_inc(s[ready], 1)

            decay_matrices(0)
            for n in range(NT * G):
                if n + 1 < NT * G:
                    decay_matrices(n + 1)
                if n < 8:
                    at, half = n // 2, n % 2
                    if half:
                        act.wait_ge(unit_done, VP * 2 + at + 3)
                    else:
                        act.wait_ge(s["vh_done"], at + 1)
                    act.activation(v_tok[:, 2 * half:2 * half + 2, at * 256:(at + 1) * 256],
                                   bank(half).rearrange("p (t c) -> p t c", c=256), ACT.Gelu_apprx_tanh)\
                       .then_inc(bank_free[at % 2] if half else s["vh_free"], 1)
                else:
                    if n == 8:
                        act.wait_ge(s["res_out"], 16)
                    act.wait_ge(unit_done, UP * 2 + n - 8 + 3)
                    act.activation(uT[:, n - 8, :], bank(n % 2), ACT.Gelu_apprx_tanh)\
                       .then_inc(bank_free[n % 2], 1)
                if n == 8:
                    act.drain()
                    act.sem_inc(s["v_gelu"], 1)
            act.wait_ge(s["ws_tr"], 1)
            for r in range(2):
                last = act.copy(ws_T[:, 4 * r:4 * r + 4, :].rearrange("p a b -> p (a b)"), bank(6 + r))
            last.then_inc(s["ws_ok"], 1)
            act.wait_ge(s["v_mean"], 1)
            for t in range(NT):
                if t:
                    act.drain()
                last = act.activation(sq_v, v_tok[:, t, :], ACT.Square, accum_out=v_var[:, t:t + 1])
            act.drain()
            act.activation(v_var, v_var, ACT.Sqrt, scale=1.0 / 1024, bias=eps6).then_inc(s["v_std"], 1)
            def group_std(q):
                act.wait_ge(s["gvar_done"], q + 1)
                act.activation((rs_y if q < 2 else rs_y2)[:, q % 2, :], bank(6 + q % 2), ACT.Sqrt, bias=eps6)\
                   .then_inc(s["gstd"], 1)

            for n in range(8):
                act.wait_ge(unit_done, ZP * 2 + n + 3)
                if n >= 2:
                    act.wait_ge(s["z_ok"], n - 1)
                act.activation(z_s[:, n % 2, :], bank(n % 2), ACT.Silu).then_inc(bank_free[n % 2], 1)
                act.wait_ge(s["z_ok"], n + 1)
                act.activation(sq_y[:, n, :], y[:, n, :], ACT.Square).then_inc(s["y_sq"], 1)
                if n >= 5:
                    group_std(n - 5)
            group_std(3)
            with act.Fori(0, 4) as i:
                for turn in range(2):
                    act.wait_ge(unit_done, (i * 2 + turn + MERGE) * 2 + 3)
                    act.wait_ge(bank_free[1], i * 2 + turn + MERGE)
                    act.activation(gates[turn][0], bank(4 * turn), ACT.Sigmoid)
                    act.activation(gates[turn][1], bank(4 * turn + 2), ACT.Sigmoid).then_inc(bank_free[0], 1)

        @block.vector
        def _(dve):
            n1 = params[:, PN1:PN1 + KT].unsqueeze(2).to_broadcast([128, KT, 2])
            dve.tensor_tensor(nscale, mod[:, 8:16, :], n1, ALU.mult)
            dve.drain()
            dve.tensor_tensor(nscale, nscale, n1, ALU.add)
            dve.wait_ge(s["a_exp"], 1)
            dve.tensor_scalar(a_neg, a_neg, -1.0, None, ALU.mult)
            for half in range(2):
                part = slice(64 * half, 64 * half + 64)
                dve.tensor_copy(d_skip[part, :], d_all[part, :].rearrange("p (k f) -> p k f", f=2)[:, :, half])
            dve.drain()

            def rms(src, dst, width, which, std_ready, n_ready):
                dve.wait_ge(std_ready, 1)
                dve.reciprocal(rstd[:, 0:width], rstd[:, 0:width])
                dve.drain()
                for k in range(KT):
                    dve.scalar_tensor_tensor(out=dst[:, k, :], in0=src[:, k, :],
                                             scalar=nscale[:, k, which:which + 1], in1=rstd[:, 0:width],
                                             op0=ALU.mult, op1=ALU.mult).then_inc(n_ready, 1)

            def time_steps(call, t0, n):
                x, e, z, q, p = (v[:, t0:t0 + n, :] for v in (dt, dt_y, dt_z, dt_q, dt_s))
                bias = dt_bias.unsqueeze(1).to_broadcast([128, n, 32])
                dve.wait_ge(s["dt_mm"], call)
                dve.tensor_tensor(x, psum[:, 4, t0 * 32:(t0 + n) * 32].rearrange("p (t h) -> p t h", h=32),
                                  bias, ALU.add)
                dve.drain()
                dve.scalar_tensor_tensor(out=e, in0=x, scalar=-1.0, in1=x, op0=ALU.mult, op1=ALU.min)\
                   .then_inc(s["dt_abs"], 1)
                dve.wait_ge(s["dt_exp"], call)
                dve.tensor_scalar(z, e, 2.0, None, ALU.add)
                dve.drain()
                dve.reciprocal(z, z)
                dve.drain()
                dve.tensor_tensor(z, z, e, ALU.mult)
                dve.drain()
                dve.tensor_tensor(q, z, z, ALU.mult)
                dve.memset(p, 1.0 / 19)
                for c in range(17, 0, -2):
                    dve.drain()
                    dve.tensor_tensor(p, p, q, ALU.mult)
                    dve.drain()
                    dve.tensor_scalar(p, p, 1.0 / c, None, ALU.add)
                dve.drain()
                dve.scalar_tensor_tensor(out=p, in0=p, scalar=2.0, in1=z, op0=ALU.mult, op1=ALU.mult)
                dve.drain()
                dve.scalar_tensor_tensor(out=x, in0=x, scalar=0.0, in1=p, op0=ALU.max, op1=ALU.add)
                dve.drain()
                dve.tensor_tensor(dta[:, t0:t0 + n, :], x, a_neg.unsqueeze(1).to_broadcast([128, n, 32]),
                                  ALU.mult).then_inc(s["dt_ok"], 1)

            def scan_units(pair0, n, pad, width):
                with dve.Fori(0, n) as i:
                    for side in range(2):
                        dve.wait_ge(bank_free[side], i + pair0 + 2)
                        o = cv[:, side, 0:width]
                        w = [params[:, bass.ds(i * 2 + (PCW + 16 * c + side), 1)] for c in range(3)]
                        dve.tensor_scalar(o, pad[:, side, 0:width], w[0], None, ALU.mult)
                        for c in (1, 2):
                            dve.drain()
                            last = dve.scalar_tensor_tensor(out=o, in0=pad[:, side, c:c + width], scalar=w[c],
                                                            in1=o, op0=ALU.mult, op1=ALU.add)
                        last.then_inc(s["conv_done"], 1)

            def decays(call, t0, n):
                cum = psum[:, 5, t0 * 64:(t0 + n) * 64].rearrange("p (t h) -> p t h", h=64)
                dve.wait_ge(s["cum_done"], call)
                dve.tensor_scalar(nacum[:, t0:t0 + n, :], cum[:, :, 0:32], -1.0, None, ALU.mult)
                dve.tensor_copy(c_dec[:, t0:t0 + n, :], cum[:, :, 32:64])
                dve.drain()
                dve.tensor_tensor(w_end[:, t0:t0 + n, :], nacum[:, t0:t0 + n, :], c_dec[:, t0:t0 + n, :],
                                  ALU.add).then_inc(s["ac_ready"], 1)
                dve.wait_ge(s["w_ready2"], call)
                dve.tensor_tensor(w_end[:, t0:t0 + n, :], w_end[:, t0:t0 + n, :], dt[:, t0:t0 + n, :], ALU.mult)
                dve.drain()

            def heads(v):
                return v.rearrange("p (h d) -> p h d", d=64)

            def states(k0, some, tr):
                dve.wait_ge(s["tr_used"], tr)
                def weigh(k):
                    way, t, _, _ = some[k - k0]
                    if k >= 2:
                        dve.wait_ge(s["st_done"], k - 1)
                    w = w_end[:, t, H * way:H * way + H].unsqueeze(2).to_broadcast([128, H, 64])
                    dve.tensor_tensor(heads(xw[:, k % 2, :]), heads(x_tok[:, t % NT, :]), w, ALU.mult)\
                       .then_inc(s["xw_ready"], 1)

                weigh(k0)
                for k, (way, t, a, b) in enumerate(some, k0):
                    if k + 1 < k0 + len(some):
                        weigh(k + 1)
                    old, new = state[way][:, a, :], state[way][:, b, :]
                    dec = c_dec[:, t, H * way:H * way + H].unsqueeze(2).to_broadcast([128, H, 64])
                    dve.tensor_tensor(heads(new), heads(old), dec, ALU.mult)
                    dve.wait_ge(s["st_done"], k + 1)
                    dve.drain()
                    b0 = st_banks(k)[0]
                    dve.tensor_tensor(new, new, psum[:, b0:b0 + 2, :].rearrange("p a b -> p (a b)"), ALU.add)\
                       .then_inc(s["st_used"], 1)
                    dve.drain()

            rms(c_in, xm_c, C, 1, s["stdc_ready"], s["nc_ready"])
            time_steps(1, NT, NC)
            scan_units(CTX, 6, pad_c, C)
            decays(1, NT, NC)
            dve.wait_ge(s["consts"], 1)
            states(0, steps, 3 * NC)
            rms(res, xm, T, 0, s["stdl_ready"], s["nl_ready"])
            time_steps(2, 0, NT)
            scan_units(SCAN, 8, pad_l, T)
            decays(2, 0, NT)
            states(4, steps_l, 3 * NC + 3 * NT)

            def masked(n):
                b = n % 2
                dve.wait_ge(s["bc_done"], n + 1)
                if n >= 2:
                    dve.wait_ge(s["y_done"], n - 1)
                for m, at, mask in ((df, 2 + 3 * b, mask_f), (db, 3 + 3 * b, mask_b)):
                    last = dve.tensor_tensor(m[:, b, :, :], psum[:, at, :].rearrange("p (h i) -> p h i", i=CH),
                                             mask.unsqueeze(1).to_broadcast([128, 4, CH]), ALU.add)
                last.then_inc(s["tm_ready"], 1)

            def combine(n):
                c, g, b = n // G, n % G, n % 2
                m = df[:, b, :, :]
                dve.wait_ge(s["ff_ready"], n + 1)
                dve.tensor_tensor(m, m, dt[:, c, 4 * g:4 * g + 4].unsqueeze(2).to_broadcast([128, 4, CH]),
                                  ALU.mult)
                dve.wait_ge(s["pb_ready"], n + 1)
                dve.drain()
                dve.tensor_tensor(m, m, db[:, b, :, :], ALU.add)
                dve.drain()
                dve.tensor_tensor(m, m, psum[:, 4 + 3 * b, 0:CH].unsqueeze(1).to_broadcast([128, 4, CH]),
                                  ALU.mult).then_inc(s["m_ready"], 1)

            def skip(n):
                c, g, b = n // G, n % G, n % 2
                chunk = slice(c * CH, (c + 1) * CH)
                dve.wait_ge(s["y_done"], n + 1)
                for t in range(2):
                    k = 2 * g + t
                    last = dve.scalar_tensor_tensor(out=y[:, k, chunk], in0=xbc[:, k, chunk],
                                                    scalar=d_skip[:, k:k + 1],
                                                    in1=psum[:, 4 + 3 * b, 256 + t * CH:256 + (t + 1) * CH],
                                                    op0=ALU.mult, op1=ALU.add)
                last.then_inc(s["y_used"], 1)

            masked(0)
            for n in range(NT * G):
                if n:
                    skip(n - 1)
                if n + 1 < NT * G:
                    masked(n + 1)
                combine(n)
            skip(NT * G - 1)
            dve.wait_ge(s["v_gelu"], 1)
            dve.tensor_reduce(v_sum, v_tok, AX.X, ALU.add)
            dve.drain()
            dve.tensor_scalar(v_sum, v_sum, 1.0 / 1024, None, ALU.mult)
            dve.drain()
            for t in range(NT):
                last = dve.tensor_scalar(v_tok[:, t, :], v_tok[:, t, :], v_sum[:, t:t + 1], None, ALU.subtract)
            last.then_inc(s["v_mean"], 1)

            def gate_y(n):
                dve.wait_ge(bank_free[n % 2], ZP + n // 2 + 2)
                dve.tensor_tensor(y[:, n, :], y[:, n, :], z_s[:, n % 2, :], ALU.mult).then_inc(s["z_ok"], 1)

            def gate_u(g):
                dve.wait_ge(s["mix_done"], g + 1)
                bias = bs_bc[:, g * CH:(g + 1) * CH].unsqueeze(1).to_broadcast([128, NT, CH])
                dve.tensor_tensor(mixed[:, g % 2, :].rearrange("p (c i) -> p c i", i=CH),
                                  psum[:, 4 + g % 2, :].rearrange("p (c i) -> p c i", i=CH), bias, ALU.add)
                dve.drain()
                dve.tensor_tensor(sgu[:, g, :], mixed[:, g % 2, :], uT[:, g, :], ALU.mult).then_inc(s["mix_used"], 1)

            def norm_y(q):
                dve.wait_ge(s["gstd"], q + 1)
                r = (rs_y if q < 2 else rs_y2)[:, q % 2, :]
                dve.reciprocal(r, r)
                dve.drain()
                for t in range(2):
                    k = 2 * q + t
                    dve.scalar_tensor_tensor(out=y[:, k, :], in0=y[:, k, :], scalar=par(PSN + k), in1=r,
                                             op0=ALU.mult, op1=ALU.mult).then_inc(s["y_ok"], 1)

            gate_y(0)
            gate_y(1)
            dve.wait_ge(s["v_std"], 1)
            dve.reciprocal(v_var, v_var)
            dve.wait_ge(s["ln_in"], 48)
            dve.drain()
            for t in range(NT):
                dve.scalar_tensor_tensor(out=v_tok[:, t, :], in0=v_tok[:, t, :], scalar=v_var[:, t:t + 1],
                                         in1=ln_w, op0=ALU.mult, op1=ALU.mult)
            gate_y(2)
            gate_y(3)
            dve.drain()
            dve.tensor_tensor(v_tok, v_tok, ln_b.unsqueeze(1).to_broadcast([128, NT, 1024]), ALU.add)\
               .then_inc(s["v_ok"], 1)
            for n in range(4, 8):
                gate_y(n)
                gate_u(2 * (n - 4))
                gate_u(2 * (n - 4) + 1)
                if n >= 5:
                    norm_y(n - 5)
            norm_y(3)
            dve.drain()
            with dve.Fori(0, 4) as i:
                for turn in range(2):
                    ga, gb = gates[turn]
                    dve.wait_ge(bank_free[0], i * 2 + turn + (MERGE + 2))
                    dve.wait_ge(unit_done, (i * 2 + turn + MERGE) * 2 + 4)
                    dve.tensor_tensor(ga, ga, bank(4 * turn + 1), ALU.mult)
                    dve.tensor_tensor(gb, gb, bank(4 * turn + 3), ALU.mult)
                    dve.drain()
                    dve.tensor_tensor(merged[:, bass.ds(i * 2 + turn, 1), :].rearrange("p a b -> p (a b)"), ga, gb,
                                      ALU.add).then_inc(bank_free[1], 1)
            dve.wait_ge(s["res_back"], 16)
            with dve.Fori(0, 4) as i:
                for side in range(2):
                    dve.wait_ge(unit_done, (i + WO) * 2 + side + 3)
                    tile = res[:, bass.ds(i * 2 + side, 1), :].rearrange("p a b -> p (a b)")
                    dve.scalar_tensor_tensor(out=tile, in0=bank(side),
                                             scalar=mod[:, bass.ds(i * 2 + (16 + side), 1), 0:1]
                                             .rearrange("p a b -> p (a b)"), in1=tile,
                                             op0=ALU.mult, op1=ALU.add).then_inc(bank_free[side], 1)


def experts_program(nc, d, mem):
    f32 = mybir.dt.float32
    ALU, ACT, AX = mybir.AluOpType, mybir.ActivationFunctionType, mybir.AxisListType
    KT, T, NT, E, CAP, D = 8, 512, 4, 16, 64, 1024
    PAIRS, SLOTS = E // 2, 12

    ctx = ExitStack()
    with ctx:
        arena, psum = mem["arena"], mem["psum"]
        cursor = [0]

        def place(*shape):
            size = int(np.prod(shape))
            v = arena[:, cursor[0]:cursor[0] + size]
            cursor[0] += size
            assert cursor[0] <= mem["size"], cursor[0]
            if len(shape) == 2:
                return v.rearrange("p (a b) -> p a b", b=shape[1])
            if len(shape) == 3:
                return v.rearrange("p (a b c) -> p a b c", b=shape[1], c=shape[2])
            return v

        OUT_BANKS = (5, 6, 7, 0, 1, 2, 3, 5)

        res = place(KT, T)
        ident = place(128)
        mod = place(49, 2)[:, 1:, :]
        params = place(160)
        onesD, eps6 = place(128), place(1)
        nscale = place(KT)
        rstd = place(T)
        xf = place(KT, T)
        xf_tok = place(NT, D)
        one_hot = place(NT, E * CAP)
        squares = one_hot.rearrange("p a b -> p (a b)").rearrange("p (a b) -> p a b", b=T)
        scatter = place(T)
        y = place(D)
        ring = [place(2, D) for _ in range(SLOTS)]
        xg_hid = place(3 * D)
        xg, hidT = (xg_hid[:, i * D:(i + 1) * D].rearrange("p (a b) -> p a b", b=128) for i in (0, 2))
        hid = xg_hid[:, D:2 * D]
        w_router = place(KT, E)
        w_scaled = place(KT, E)
        shift_part = place(1)
        std_row = place(T)[0:1]
        aff = place(NT, E)
        amax, asum = place(NT), place(NT)
        slot_tok = place(NT, E)
        slot_iota = place(CAP)
        slot_of_part = place(1)
        gate = place(1)
        final_w = place(D)
        f_rstd = place(NT)
        junk = hid[:, 0:T]
        wide = xg_hid[0:E, :]
        aff_row, left, taken, pos, ones_row = (wide[:, i * T:(i + 1) * T] for i in range(5))
        top8 = wide[:, 5 * T:5 * T + 8]
        logits_row = left
        rows_at = place(2, T)
        aff_rows, slot_rows = rows_at[0:E, 0, :], rows_at[0:E, 1, :]
        pair_rows = place(PAIRS, 128)[0:E]
        selector = place(128)[0:E]
        out_tok = one_hot

        s = {n: mem["sem"]("e_" + n) for n in (
            "consts const_in ws_ready sq_act sq_dve router_in lt_done lg_ok rstd_ok fstd_tr var_done std_ready n_ready xf_ready logit_done aff_sub aff_exp "
            "aff_ok affT_done slot_ok slotT_done hot_ok tok_tr tok_ok "
            "unit_used gather_done xg_act xg_dve silu_ok hid_ok hT_done hT_act hT_dve rows_done scat_ok "
            "sel_ok y_free sc_done res_ok fsq_ready fvar_done fstd out_tr out_ok out_done").split()}
        w_ready = [mem["sem"](f"e_w_ready{i}") for i in range(SLOTS)]

        block = ctx.enter_context(nc.Block())

        @block.sync
        def _(sp):
            sp.dma_start(w_router, d["router_w_2"][0].rearrange("(k p) e -> p k e", p=128))\
              .then_inc(s["router_in"], 16)
            sp.dma_start(slot_iota, d["slot_iota"].partition_broadcast(128)).then_inc(s["const_in"], 16)
            sp.dma_start(slot_of_part, d["slot_of_partition"]).then_inc(s["const_in"], 16)
            sp.dma_start(pair_rows, d["pair_selector"]).then_inc(s["const_in"], 16)
            sp.dma_start(final_w, d["final_norm_w_2"].partition_broadcast(128)).then_inc(s["const_in"], 16)
            with sp.Fori(0, PAIRS) as q:
                for u in range(3 * KT):
                    name, k = ("w_gate_2", "w_up_2", "w_down_2")[u // KT], u % KT
                    sp.wait_ge(s["unit_used"], q * (3 * KT) + (u + 1))
                    src = d[name][0, bass.ds(q * 2, 2), k * 128:(k + 1) * 128, :]
                    sp.dma_start(ring[u % SLOTS], src.rearrange("e p c -> p e c"))\
                      .then_inc(w_ready[u % SLOTS], 16)
            for t in range(NT):
                sp.wait_ge(s["out_ok"], 2 * t + 2)
                sp.dma_start(d["out"][0, t * 128:(t + 1) * 128, :], out_tok[:, t, :]).then_inc(s["out_done"], 16)
            sp.wait_ge(s["out_done"], 16 * NT)

        @block.gpsimd
        def _(pool):
            pool.memset(onesD, 1.0 / 1024)
            pool.memset(ones_row, 1.0)
            pool.memset(eps6, 1e-6)
            pool.drain()
            pool.sem_inc(s["consts"], 1)
            pool.wait_ge(s["rstd_ok"], 1)
            for k in range(KT):
                pool.tensor_tensor(xf[:, k, :], res[:, k, :], rstd, ALU.mult).then_inc(s["n_ready"], 1)

        @block.tensor
        def _(pe):
            pe.sem_inc(s["unit_used"], SLOTS)
            pe.sem_inc(s["y_free"], 1)
            pe.wait_ge(s["consts"], 1)
            for k in range(KT):
                pe.wait_ge(s["sq_dve" if k % 2 else "sq_act"], k // 2 + 1)
                mm = pe.matmul(psum[:, 5, :], onesD, squares[:, k, :], start=(k == 0), stop=(k == KT - 1))
            mm.then_inc(s["var_done"], 1)
            pe.wait_ge(s["ws_ready"], 1)
            for k in range(KT):
                pe.matmul(psum[0:E, 3, 0:1], w_router[:, k, :], mod[:, 24 + k, 0:1],
                          start=(k == 0), stop=(k == KT - 1))
            for k in range(KT):
                mm = pe.matmul(psum[0:E, 2, :], w_scaled[:, k, :], res[:, k, :],
                               start=(k == 0), stop=(k == KT - 1))
            mm.then_inc(s["lt_done"], 1)
            pe.wait_ge(s["lg_ok"], 1)
            for t in range(NT):
                mm = pe.transpose(psum[:, 4, t * E:(t + 1) * E], logits_row[:, t * 128:(t + 1) * 128],
                                  ident[0:E, 0:E])
            mm.then_inc(s["logit_done"], 1)
            pe.wait_ge(s["aff_ok"], 1)
            for t in range(NT):
                mm = pe.transpose(psum[0:E, 0, t * 128:(t + 1) * 128], aff[:, t, :], ident)
            mm.then_inc(s["affT_done"], 1)
            for r in range(2 * NT):
                pe.wait_ge(s["xf_ready"], 4 * (r % 2) + 4)
                if r >= 2:
                    pe.wait_ge(s["tok_ok"], r - 1)
                for k in range(4):
                    mm = pe.transpose(psum[:, 6 + r % 2, k * 128:(k + 1) * 128],
                                      xf[:, 4 * (r % 2) + k, (r // 2) * 128:(r // 2 + 1) * 128], ident)
                mm.then_inc(s["tok_tr"], 1)
            pe.wait_ge(s["slot_ok"], 1)
            for t in range(NT):
                mm = pe.transpose(psum[:, 1, t * E:(t + 1) * E], slot_rows[:, t * 128:(t + 1) * 128],
                                  ident[0:E, 0:E])
            mm.then_inc(s["slotT_done"], 1)

            def gather(q):
                for k in range(KT):
                    for t in range(NT):
                        mm = pe.matmul(psum[:, 4 + k // 4, (k % 4) * 128:(k % 4 + 1) * 128],
                                       xf_tok[:, t, k * 128:(k + 1) * 128],
                                       one_hot[:, t, bass.ds(q * 128, 128)],
                                       start=(t == 0), stop=(t == NT - 1))
                mm.then_inc(s["gather_done"], 1)

            def both_experts(bank0, x, u, k, start, stop):
                for half in range(2):
                    for e in range(2):
                        mm = pe.matmul(psum[64 * e:64 * e + 64, bank0 + half, :], x[:, k, 64 * e:64 * e + 64],
                                       ring[u % SLOTS][:, e, half * 512:(half + 1) * 512],
                                       start=start, stop=stop)
                mm.then_inc(s["unit_used"], 1)

            def put_back(q, m, bank):
                if m == 0:
                    pe.wait_ge(s["y_free"], q + 2)
                    pe.wait_ge(s["scat_ok"], q + 1)
                pe.matmul(psum[:, bank, :], y[:, m * 128:(m + 1) * 128], scatter, start=True, stop=True)\
                  .then_inc(s["sc_done"], 1)

            def pair(q, first, more):
                pe.wait_ge(s["xg_act"], q + 1)
                pe.wait_ge(s["xg_dve"], q + 1)
                for u in range(2 * KT):
                    pe.wait_ge(w_ready[u % SLOTS], q * 32 + (u // SLOTS) * 16 + 16)
                    k = u % KT
                    both_experts(2 * (u // KT), xg, u, k, k == 0, k == KT - 1)
                    if not first and u % 2 == 1:
                        m = u // 2
                        if m >= 2:
                            pe.wait_ge(s["res_ok"], q * 8 + (m - 9))
                        put_back(q - 1, m, 4 + m % 2)
                if more:
                    if not first:
                        pe.wait_ge(s["res_ok"], q * 8)
                    else:
                        pe.wait_ge(s["hot_ok"], 2)
                    gather(q + 1)
                pe.wait_ge(s["hid_ok"], q + 1)
                for k in range(KT):
                    mm = pe.transpose(psum[:, k // 4, (k % 4) * 128:(k % 4 + 1) * 128],
                                      hid[:, k * 128:(k + 1) * 128], ident)
                mm.then_inc(s["hT_done"], 1)
                pe.wait_ge(s["sel_ok"], q + 1)
                pe.matmul(psum[:, 2, :], selector, slot_rows, start=True, stop=True)
                pe.matmul(psum[:, 3, :], selector, aff_rows, start=True, stop=True)\
                  .then_inc(s["rows_done"], 1)
                pe.wait_ge(s["hT_act"], q + 1)
                pe.wait_ge(s["hT_dve"], q + 1)
                for u in range(2 * KT, 3 * KT):
                    pe.wait_ge(w_ready[u % SLOTS], q * 32 + 32)
                    k = u % KT
                    both_experts(6, hidT, u, k, k == 0, k == KT - 1)

            pe.wait_ge(s["hot_ok"], 1)
            pe.wait_ge(s["tok_ok"], 2 * NT)
            gather(0)
            pair(0, 1, 1)
            with pe.Fori(0, PAIRS - 2) as i:
                pair(i + 1, 0, 1)
            pair(PAIRS - 1, 0, 0)
            def last_squares(k):
                pe.wait_ge(s["fsq_ready"], k + 1)
                pe.matmul(psum[0:1, 4, :], onesD[:, 0:1], xf[:, k, :], start=(k == 0), stop=(k == KT - 1))\
                  .then_inc(s["fvar_done"], 1)

            for m in range(KT):
                if m >= 4:
                    pe.wait_ge(s["res_ok"], KT * (PAIRS - 1) + m - 3)
                put_back(PAIRS - 1, m, m % 4)
                if m >= 3:
                    last_squares(m - 3)
            for k in range(KT - 3, KT):
                last_squares(k)

            def to_tokens(r, b):
                for k in range(4):
                    mm = pe.transpose(psum[:, b, k * 128:(k + 1) * 128],
                                      res[:, 4 * (r % 2) + k, (r // 2) * 128:(r // 2 + 1) * 128], ident)
                mm.then_inc(s["out_tr"], 1)

            for r, b in enumerate(OUT_BANKS):
                if r == 7:
                    pe.wait_ge(s["out_ok"], 1)
                to_tokens(r, b)
                if r == 1:
                    pe.wait_ge(s["fstd"], 1)
                    for t in range(NT):
                        mm = pe.transpose(psum[:, 4, t:t + 1], std_row[:, t * 128:(t + 1) * 128], ident[0:1, 0:1])
                    mm.then_inc(s["fstd_tr"], 1)

        @block.scalar
        def _(act):
            for k in range(0, KT, 2):
                act.activation(squares[:, k, :], res[:, k, :], ACT.Square).then_inc(s["sq_act"], 1)
            act.wait_ge(s["consts"], 1)
            act.wait_ge(s["var_done"], 1)
            act.activation(rstd, psum[:, 5, :], ACT.Sqrt, bias=eps6).then_inc(s["std_ready"], 1)
            act.wait_ge(s["aff_sub"], 1)
            act.activation(aff, aff, ACT.Exp).then_inc(s["aff_exp"], 1)
            for k in range(KT):
                act.wait_ge(s["n_ready"], k + 1)
                act.activation(xf[:, k, :], xf[:, k, :], ACT.Identity, bias=mod[:, 24 + k, 0:1],
                               scale=nscale[:, k:k + 1]).then_inc(s["xf_ready"], 1)
            for r in range(2 * NT):
                act.wait_ge(s["tok_tr"], r + 1)
                act.copy(xf_tok[:, r // 2, (r % 2) * 512:(r % 2 + 1) * 512], psum[:, 6 + r % 2, :])\
                   .then_inc(s["tok_ok"], 1)

            def halves(v):
                return v.rearrange("p k c -> p (k c)")

            act.wait_ge(s["gather_done"], 1)
            act.copy(halves(xg[:, 0:4, :]), psum[:, 4, :]).then_inc(s["xg_act"], 1)

            def pair(q, first, more):
                if not first:
                    act.wait_ge(s["rows_done"], q)
                act.copy(selector, pair_rows[:, bass.ds(q, 1), :].rearrange("p a b -> p (a b)"))\
                   .then_inc(s["sel_ok"], 1)
                act.wait_ge(s["unit_used"], q * 24 + (SLOTS + 2 * KT))
                act.activation(hid, psum[:, 0:2, :].rearrange("p b c -> p (b c)"), ACT.Silu)\
                   .then_inc(s["silu_ok"], 1)
                if more:
                    act.wait_ge(s["gather_done"], q + 2)
                    act.copy(halves(xg[:, 0:4, :]), psum[:, 4, :]).then_inc(s["xg_act"], 1)
                act.wait_ge(s["hT_done"], q + 1)
                act.copy(halves(hidT[:, 0:4, :]), psum[:, 0, :]).then_inc(s["hT_act"], 1)
                act.wait_ge(s["unit_used"], q * 24 + (SLOTS + 3 * KT))
                act.wait_ge(s["scat_ok"], q + 1)
                act.activation(y, psum[:, 6:8, :].rearrange("p b c -> p (b c)"), ACT.Copy,
                               scale=gate).then_inc(s["y_free"], 1)

            act.wait_ge(s["const_in"], 64)
            pair(0, 1, 1)
            with act.Fori(0, PAIRS - 2) as i:
                pair(i + 1, 0, 1)
            pair(PAIRS - 1, 0, 0)
            for k in range(KT):
                act.wait_ge(s["res_ok"], KT * (PAIRS - 1) + k + 1)
                act.activation(xf[:, k, :], res[:, k, :], ACT.Square).then_inc(s["fsq_ready"], 1)
            act.wait_ge(s["fvar_done"], KT)
            act.activation(std_row, psum[0:1, 4, :], ACT.Sqrt, bias=eps6[0:1]).then_inc(s["fstd"], 1)

        @block.vector
        def _(dve):
            scale2 = mod[:, 32:40, 0:1].rearrange("p k w -> p (k w)")
            dve.scalar_tensor_tensor(out=nscale, in0=scale2, scalar=1.0, in1=params[:, 72:80],
                                     op0=ALU.add, op1=ALU.mult)
            dve.wait_ge(s["router_in"], 16)
            dve.drain()
            dve.tensor_tensor(w_scaled, w_router, nscale.unsqueeze(2).to_broadcast([128, KT, E]), ALU.mult)\
               .then_inc(s["ws_ready"], 1)
            for k in range(1, KT, 2):
                dve.tensor_tensor(squares[:, k, :], res[:, k, :], res[:, k, :], ALU.mult)\
                   .then_inc(s["sq_dve"], 1)
            dve.wait_ge(s["std_ready"], 1)
            dve.reciprocal(rstd, rstd)
            dve.drain()
            dve.sem_inc(s["rstd_ok"], 1)
            dve.wait_ge(s["lt_done"], 1)
            dve.tensor_copy(shift_part[0:E], psum[0:E, 3, 0:1])
            dve.tensor_tensor(logits_row, psum[0:E, 2, :], rstd[0:E, :], ALU.mult)
            dve.drain()
            dve.tensor_scalar(logits_row, logits_row, shift_part[0:E], None, ALU.add).then_inc(s["lg_ok"], 1)
            dve.wait_ge(s["logit_done"], 1)
            logits = psum[:, 4, 0:NT * E].rearrange("p (t e) -> p t e", e=E)
            dve.tensor_reduce(amax, logits, AX.X, ALU.max)
            dve.drain()
            dve.tensor_tensor(aff, logits, amax.unsqueeze(2).to_broadcast([128, NT, E]), ALU.subtract)\
               .then_inc(s["aff_sub"], 1)
            dve.wait_ge(s["aff_exp"], 1)
            dve.tensor_reduce(asum, aff, AX.X, ALU.add)
            dve.drain()
            dve.reciprocal(asum, asum)
            dve.drain()
            dve.tensor_tensor(aff, aff, asum.unsqueeze(2).to_broadcast([128, NT, E]), ALU.mult)\
               .then_inc(s["aff_ok"], 1)
            dve.wait_ge(s["affT_done"], 1)
            dve.tensor_copy(aff_rows, psum[0:E, 0, :])
            dve.tensor_copy(left, psum[0:E, 0, :])
            for _ in range(CAP // 8):
                dve.drain()
                dve.max(top8, left)
                dve.drain()
                dve.match_replace(left, top8, left, -1.0)
            dve.drain()
            dve.tensor_scalar(taken, left, 0.0, None, ALU.is_lt)
            dve.drain()
            dve.wait_ge(s["consts"], 1)
            dve.tensor_tensor_scan(pos, ones_row, taken, 0.0, ALU.mult, ALU.add)
            dve.drain()
            dve.tensor_tensor(pos, pos, taken, ALU.mult)
            dve.drain()
            dve.tensor_scalar(slot_rows, pos, -1.0, None, ALU.add).then_inc(s["slot_ok"], 1)
            dve.wait_ge(s["const_in"], 64)
            dve.wait_ge(s["slotT_done"], 1)
            dve.tensor_copy(slot_tok, psum[:, 1, 0:NT * E].rearrange("p (t e) -> p t e", e=E))
            dve.drain()
            for e0, e1 in ((0, 2), (2, E)):
                for t in range(NT):
                    last = dve.tensor_tensor(one_hot[:, t, e0 * CAP:e1 * CAP].rearrange("p (e c) -> p e c", c=CAP),
                                             slot_iota.unsqueeze(1).to_broadcast([128, e1 - e0, CAP]),
                                             slot_tok[:, t, e0:e1].unsqueeze(2).to_broadcast([128, e1 - e0, CAP]),
                                             ALU.is_equal)
                last.then_inc(s["hot_ok"], 1)

            def halves(v):
                return v.rearrange("p k c -> p (k c)")

            dve.wait_ge(s["gather_done"], 1)
            dve.tensor_copy(halves(xg[:, 4:8, :]), psum[:, 5, :]).then_inc(s["xg_dve"], 1)

            def add_back(q, m, bank):
                dve.wait_ge(s["sc_done"], q * 8 + (m + 1))
                dve.scalar_tensor_tensor(out=res[:, m, :], in0=psum[:, bank, :], scalar=mod[:, 40 + m, 0:1],
                                         in1=res[:, m, :], op0=ALU.mult, op1=ALU.add)\
                   .then_inc(s["res_ok"], 1)

            def pair(q, first, more):
                if not first:
                    for m in range(KT):
                        add_back(q - 1, m, 4 + m % 2)
                dve.wait_ge(s["silu_ok"], q + 1)
                dve.tensor_tensor(hid, hid, psum[:, 2:4, :].rearrange("p b c -> p (b c)"), ALU.mult)\
                   .then_inc(s["hid_ok"], 1)
                if more:
                    dve.wait_ge(s["gather_done"], q + 2)
                    dve.tensor_copy(halves(xg[:, 4:8, :]), psum[:, 5, :]).then_inc(s["xg_dve"], 1)
                dve.wait_ge(s["hT_done"], q + 1)
                dve.tensor_copy(halves(hidT[:, 4:8, :]), psum[:, 1, :]).then_inc(s["hT_dve"], 1)
                dve.wait_ge(s["rows_done"], q + 1)
                dve.tensor_scalar(scatter, psum[:, 2, :], slot_of_part, None, ALU.is_equal)
                dve.drain()
                dve.scalar_tensor_tensor(out=junk, in0=psum[:, 3, :], scalar=1.0, in1=scatter,
                                         op0=ALU.mult, op1=ALU.mult, accum_out=gate)
                dve.drain()
                dve.sem_inc(s["scat_ok"], 1)

            pair(0, 1, 1)
            with dve.Fori(0, PAIRS - 2) as i:
                pair(i + 1, 0, 1)
            pair(PAIRS - 1, 0, 0)
            for m in range(KT):
                add_back(PAIRS - 1, m, m % 4)
            dve.wait_ge(s["fstd_tr"], 1)
            dve.reciprocal(f_rstd, psum[:, 4, 0:NT])
            dve.drain()
            for r, b in enumerate(OUT_BANKS):
                dve.wait_ge(s["out_tr"], r + 1)
                half = slice((r % 2) * 512, (r % 2 + 1) * 512)
                dve.scalar_tensor_tensor(out=out_tok[:, r // 2, half], in0=psum[:, b, :],
                                         scalar=f_rstd[:, r // 2:r // 2 + 1], in1=final_w[:, half],
                                         op0=ALU.mult, op1=ALU.mult).then_inc(s["out_ok"], 1)


_INS = ("x rel_bias ln_g ln_b ffn_w_gate ffn_w_up ffn_w_down w_in conv_dw_w conv_dw_b conv_ln_g conv_ln_b "
        "lru_conv_w lru_conv_b lru_wa lru_ba lru_wx lru_bx lru_lambda attn_sinks w_out c_2 ctx_2 c_ctx_2 "
        "ada_w_2 ada_b_2 norm1_w_2 norm2_w_2 w_in_2 conv_w_2 conv_b_2 dt_bias_2 a_log_2 d_skip_2 "
        "ssd_norm_w_2 sgu_ln_w_2 sgu_ln_b_2 w_s_2 b_s_2 w_pa_2 w_pb_2 w_o_2 router_w_2 w_gate_2 w_up_2 "
        "w_down_2 final_norm_w_2").split()


def shape_constants():
    dist = 127 - np.arange(128)
    far = 16 + (np.log(np.maximum(dist, 1) / 16) / np.log(8) * 16).astype(int)
    bucket = np.where(dist < 16, dist, np.minimum(far, 31))
    onehot = (np.arange(32)[:, None] == bucket[None, :]).astype(np.float32)
    part = np.arange(128)
    selector = (np.arange(16)[:, None, None] == 2 * np.arange(8)[None, :, None] + part // 64)
    return {"bucket_onehot": onehot, "slot_iota": np.arange(64, dtype=np.float32),
            "slot_of_partition": (part % 64).astype(np.float32)[:, None],
            "pair_selector": selector.astype(np.float32)}


def build(nc, d):
    f32 = mybir.dt.float32
    size = 53000
    scratch = nc.dram_tensor("band_scratch", (8, 128, 384), f32, kind="Internal").ap()
    d["res_scratch"] = nc.dram_tensor("residual_scratch", (128, 8, 512), f32, kind="Internal").ap()
    with ExitStack() as ctx:
        mem = {"arena": ctx.enter_context(nc.sbuf_tensor("arena", [128, size], f32)),
               "psum": ctx.enter_context(nc.psum_tensor("psum", [128, 8, 512], f32)),
               "scratch": scratch, "size": size}
        for program in (first_block_program, second_mixer_program, experts_program):
            sems = []

            def sem(name):
                sems.append(nc.alloc_semaphore(name))
                return sems[-1]

            mem["sem"] = sem
            program(nc, d, mem)
            nc.clear_and_free_semaphores(sems)
            nc.all_engine_barrier()


def kernel(**inputs):
    import concourse.bacc as bacc
    from concourse.bass_utils import run_bass_kernel_spmd

    nc = bacc.Bacc("TRN2", target_bir_lowering=False, num_devices=1)
    arrays, d = {}, {}
    for name, a in [(n, inputs[n]) for n in _INS] + list(shape_constants().items()):
        a = np.ascontiguousarray(a)
        arrays[f"in_{name}_dram"] = a
        d[name] = nc.dram_tensor(f"in_{name}_dram", a.shape, mybir.dt.from_np(a.dtype),
                                 kind="ExternalInput").ap()
    d["out"] = nc.dram_tensor("out_0_dram", (1, 512, 1024), mybir.dt.float32, kind="ExternalOutput").ap()
    build(nc, d)
    r = run_bass_kernel_spmd(nc, [arrays], core_ids=[0])
    return r.results[0]["out_0_dram"]
```
